# Optimizing a Trainium2 kernel written in Bass

```python
import jax, jax.numpy as jnp
from jax import lax
import numpy as np
import math
import jax
import jax.numpy as jnp

D_MODEL = 1024
BATCH = 1
SEQ = 256
DEPTH = 2

HEAD_DIM = 64
GRID_W = 64
Q_BLOCK = 128
EPS = 1e-6
NEG_BIG = -1e30
F_MIN = 1e-6
A_HEADS = 6
A_KV_HEADS = 2
ROPE_THETA = 10000.0
B_HEADS = 4
B_KEY_DIM = 64
B_CHUNK = 64
C_HEADS = 6
C_KV_HEADS = 2
C_BRANCHES = ((128, 1), (512, 4), (2048, 16))
D_FF = 2816
CONV_W = 3

A_W = A_HEADS * HEAD_DIM
B_W = B_HEADS * HEAD_DIM
B_K = B_HEADS * B_KEY_DIM
C_W = C_HEADS * HEAD_DIM
MIX_W = A_W + B_W + C_W
SPLITS = (A_W, A_KV_HEADS * HEAD_DIM, A_KV_HEADS * HEAD_DIM,
          B_K, B_K, B_K, B_W, B_W,
          C_W, C_KV_HEADS * HEAD_DIM, C_KV_HEADS * HEAD_DIM)
IN_W = sum(SPLITS)


def rms_norm(x, g):
    xf = x.astype(jnp.float32)
    y = xf * lax.rsqrt(jnp.mean(xf * xf, axis=-1, keepdims=True) + EPS)
    return (y * g.astype(jnp.float32)).astype(x.dtype)

def _rope_half(x, cos, sin):
    h = x.shape[-1] // 2
    x1, x2 = x[..., :h], x[..., h:]
    return jnp.concatenate([x1 * cos - x2 * sin, x2 * cos + x1 * sin], axis=-1)

def axial_rope(x):
    S = x.shape[1]
    n_rows = S // GRID_W
    row = jnp.repeat(jnp.arange(n_rows), GRID_W).astype(jnp.float32)
    col = jnp.tile(jnp.arange(GRID_W), n_rows).astype(jnp.float32)
    half = HEAD_DIM // 2
    inv = ROPE_THETA ** (-jnp.arange(0, half, 2, dtype=jnp.float32) / half)
    ang_r = (row[:, None] * inv)[:, None, :]
    ang_c = (col[:, None] * inv)[:, None, :]
    xf = x.astype(jnp.float32)
    xr = _rope_half(xf[..., :half], jnp.cos(ang_r), jnp.sin(ang_r))
    xc = _rope_half(xf[..., half:], jnp.cos(ang_c), jnp.sin(ang_c))
    return jnp.concatenate([xr, xc], axis=-1).astype(x.dtype)

def _to_query_blocks(q, n_kv):
    B_, S, H, D = q.shape
    nb = S // Q_BLOCK
    return q.reshape(B_, nb, Q_BLOCK, n_kv, H // n_kv, D).transpose(1, 0, 3, 4, 2, 5)

def _from_query_blocks(o):
    nb, B_, hk, g, qb, d = o.shape
    return o.transpose(1, 0, 4, 2, 3, 5).reshape(B_, nb * qb, hk * g * d)

def mixer_a(q, k, v, gq, gk):
    q = axial_rope(rms_norm(q, gq))
    k = axial_rope(rms_norm(k, gk))
    qb = _to_query_blocks(q, A_KV_HEADS)
    kt = k.transpose(0, 2, 1, 3)
    vt = v.transpose(0, 2, 1, 3)
    scale = HEAD_DIM ** -0.5

    def block(qi):
        s = jnp.einsum('bhgqd,bhkd->bhgqk', qi, kt).astype(jnp.float32) * scale
        p = jax.nn.softmax(s, axis=-1).astype(vt.dtype)
        return jnp.einsum('bhgqk,bhkd->bhgqd', p, vt)

    return _from_query_blocks(lax.map(block, qb))

def mixer_c(q, k, v, gq, gk):
    S = q.shape[1]
    q = rms_norm(q, gq)
    k = rms_norm(k, gk)
    qb = _to_query_blocks(q, C_KV_HEADS)
    kt = k.transpose(0, 2, 1, 3)
    vt = v.transpose(0, 2, 1, 3)
    nb = S // Q_BLOCK
    starts = jnp.arange(nb) * Q_BLOCK
    scale = HEAD_DIM ** -0.5
    slopes = (2.0 ** (-8.0 * np.arange(1, C_HEADS + 1) / C_HEADS)).astype(np.float32)
    slopes = jnp.asarray(slopes).reshape(C_KV_HEADS, C_HEADS // C_KV_HEADS, 1, 1)
    offsets = [r * np.arange(-(w // (2 * r)), w // (2 * r) + 1) for (w, r) in C_BRANCHES]

    def block(args):
        qi, t0 = args
        t = t0 + jnp.arange(Q_BLOCK)
        lses, outs = [], []
        for off in offsets:
            idx = t[:, None] + jnp.asarray(off)[None, :]
            valid = (idx >= 0) & (idx < S)
            idx = jnp.clip(idx, 0, S - 1)
            kg = kt[:, :, idx, :]
            vg = vt[:, :, idx, :]
            dist = jnp.asarray(np.abs(off).astype(np.float32))
            s = jnp.einsum('bhgqd,bhqkd->bhgqk', qi, kg).astype(jnp.float32) * scale - slopes * dist
            s = jnp.where(valid, s, NEG_BIG)
            lse = jax.nn.logsumexp(s, axis=-1)
            p = jnp.exp(s - lse[..., None]).astype(vg.dtype)
            outs.append(jnp.einsum('bhgqk,bhqkd->bhgqd', p, vg).astype(jnp.float32))
            lses.append(lse)
        w = jax.nn.softmax(jnp.stack(lses, axis=0), axis=0)
        o = jnp.einsum('nbhgq,nbhgqd->bhgqd', w, jnp.stack(outs, axis=0))
        return o.astype(qi.dtype)

    return _from_query_blocks(lax.map(block, (qb, starts)))

def hgrn2_scan(q, k, v, logf):
    B_, S, H, dk = q.shape
    dv = v.shape[-1]
    nc = S // B_CHUNK

    def to_chunks(a):
        return a.astype(jnp.float32).reshape(B_, nc, B_CHUNK, H, a.shape[-1]).transpose(1, 0, 3, 2, 4)

    qc, kc, vc, lc = to_chunks(q), to_chunks(k), to_chunks(v), to_chunks(logf)
    mask = jnp.tril(jnp.ones((B_CHUNK, B_CHUNK), dtype=bool))[:, :, None]

    def step(state, inp):
        q_, k_, v_, l_ = inp
        b = jnp.cumsum(l_, axis=2)
        o_inter = jnp.einsum('bhtk,bhkv->bhtv', q_ * jnp.exp(b), state)
        diff = b[:, :, :, None, :] - b[:, :, None, :, :]
        dec = jnp.where(mask, jnp.exp(jnp.where(mask, diff, 0.0)), 0.0)
        attn = jnp.einsum('bhtk,bhsk,bhtsk->bhts', q_, k_, dec)
        o_intra = jnp.einsum('bhts,bhsv->bhtv', attn, v_)
        b_last = b[:, :, -1:, :]
        new_state = jnp.exp(b_last[:, :, 0, :])[..., None] * state + \
            jnp.einsum('bhsk,bhsv->bhkv', k_ * jnp.exp(b_last - b), v_)
        return new_state, o_inter + o_intra

    state0 = jnp.zeros((B_, H, dk, dv), jnp.float32)
    _, o = lax.scan(step, state0, (qc, kc, vc, lc))
    return o.transpose(1, 0, 3, 2, 4).reshape(B_, S, H, dv).astype(v.dtype)

def mixer_b(q, f_fwd, f_bwd, i, g, lb_fwd, lb_bwd, g_norm):
    def log_forget(fpre, lb):
        lb = lb.reshape(B_HEADS, B_KEY_DIM)
        f = lb + (1.0 - lb) * jax.nn.sigmoid(fpre.astype(jnp.float32))
        return jnp.log(jnp.maximum(f, F_MIN))

    lff = log_forget(f_fwd, lb_fwd)
    lfb = log_forget(f_bwd, lb_bwd)
    o_f = hgrn2_scan(q, -jnp.expm1(lff), i, lff)
    flip = lambda a: jnp.flip(a, axis=1)
    o_b = flip(hgrn2_scan(flip(q), flip(-jnp.expm1(lfb)), flip(i), flip(lfb)))
    o = rms_norm(o_f + o_b, g_norm) * jax.nn.silu(g)
    return o.reshape(o.shape[0], o.shape[1], B_W)

def conv_ffn(h, w_up, conv_w, conv_b, w_down):
    u = h @ w_up
    up = jnp.pad(u, ((0, 0), (1, 1), (0, 0)))
    u = conv_w[0] * up[:, :-2] + conv_w[1] * up[:, 1:-1] + conv_w[2] * up[:, 2:] + conv_b
    a, b = jnp.split(u, 2, axis=-1)
    return (jax.nn.silu(a) * b) @ w_down

def first_inputs(seed: int = 0) -> dict:
    key = jax.random.key(seed)
    ks = jax.random.split(key, 20)
    nrm = lambda k, shape, s: jax.random.normal(k, shape, jnp.float32) * s
    return {
        "x": nrm(ks[0], (BATCH, SEQ, D_MODEL), 1.0),
        "c": nrm(ks[1], (BATCH, D_MODEL), 1.0),
        "w_ada": nrm(ks[2], (DEPTH, D_MODEL, 6 * D_MODEL), D_MODEL ** -0.5),
        "b_ada": nrm(ks[3], (DEPTH, 6 * D_MODEL), 0.01),
        "norm_g": 1.0 + nrm(ks[4], (DEPTH, 2, D_MODEL), 0.01),
        "w_in": nrm(ks[5], (DEPTH, D_MODEL, IN_W), D_MODEL ** -0.5),
        "a_q_norm": 1.0 + nrm(ks[6], (DEPTH, HEAD_DIM), 0.01),
        "a_k_norm": 1.0 + nrm(ks[7], (DEPTH, HEAD_DIM), 0.01),
        "b_lb": nrm(ks[8], (2, DEPTH, B_K), 0.5),
        "b_out_norm": 1.0 + nrm(ks[9], (DEPTH, HEAD_DIM), 0.01),
        "c_q_norm": 1.0 + nrm(ks[10], (DEPTH, HEAD_DIM), 0.01),
        "c_k_norm": 1.0 + nrm(ks[11], (DEPTH, HEAD_DIM), 0.01),
        "w_out": nrm(ks[12], (DEPTH, MIX_W, D_MODEL), MIX_W ** -0.5),
        "w_up": nrm(ks[13], (DEPTH, D_MODEL, 2 * D_FF), D_MODEL ** -0.5),
        "conv_w": nrm(ks[14], (DEPTH, CONV_W, 2 * D_FF), CONV_W ** -0.5),
        "conv_b": nrm(ks[15], (DEPTH, 2 * D_FF), 0.01),
        "w_down": nrm(ks[16], (DEPTH, D_FF, D_MODEL), D_FF ** -0.5),
    }

def first_block(x, c, w_ada, b_ada, norm_g, w_in, a_q_norm, a_k_norm, b_lb, b_out_norm,
              c_q_norm, c_k_norm, w_out, w_up, conv_w, conv_b, w_down):
    B_, S, _ = x.shape
    sm = jax.nn.softmax(b_lb.astype(jnp.float32), axis=1)
    lb_all = jnp.cumsum(sm, axis=1) - sm[:, :1]
    split_idx = np.cumsum(SPLITS)[:-1].tolist()
    for l in range(DEPTH):
        mod = jax.nn.silu(c) @ w_ada[l] + b_ada[l]
        sh1, sc1, g1, sh2, sc2, g2 = jnp.split(mod[:, None, :], 6, axis=-1)
        h = rms_norm(x, norm_g[l, 0]) * (1.0 + sc1) + sh1
        parts = jnp.split(h @ w_in[l], split_idx, axis=-1)
        hd = lambda a, n: a.reshape(B_, S, n, a.shape[-1] // n)
        aq, ak, av, bq, bff, bfb, bi, bg, cq, ck, cv = parts
        o_a = mixer_a(hd(aq, A_HEADS), hd(ak, A_KV_HEADS), hd(av, A_KV_HEADS), a_q_norm[l], a_k_norm[l])
        o_b = mixer_b(hd(bq, B_HEADS), hd(bff, B_HEADS), hd(bfb, B_HEADS), hd(bi, B_HEADS), hd(bg, B_HEADS),
                      lb_all[0, l], lb_all[1, l], b_out_norm[l])
        o_c = mixer_c(hd(cq, C_HEADS), hd(ck, C_KV_HEADS), hd(cv, C_KV_HEADS), c_q_norm[l], c_k_norm[l])
        mix = jnp.concatenate([o_a, o_b, o_c], axis=-1) @ w_out[l]
        x = x + g1 * mix
        h = rms_norm(x, norm_g[l, 1]) * (1.0 + sc2) + sh2
        x = x + g2 * conv_ffn(h, w_up[l], conv_w[l], conv_b[l], w_down[l])
    return x


CONV_CH = 512
CONV_K = 3
FOX_HEADS = 8
FOX_WIDTH = FOX_HEADS * HEAD_DIM
EVEN_IN = 3 * CONV_CH + 3 * FOX_WIDTH + FOX_HEADS
NSA_GROUPS = 4
NSA_HPG = 4
NSA_HEADS = NSA_GROUPS * NSA_HPG
NSA_WIDTH = NSA_HEADS * HEAD_DIM
NSA_KV = NSA_GROUPS * HEAD_DIM
CMP_LEN = 32
CMP_STRIDE = 16
SLC_LEN = 64
SLC_TOPN = 16
WINDOW = 512
SLC_QCHUNK = 16
ODD_IN = NSA_WIDTH + 6 * NSA_KV + 3 * NSA_HEADS
REL_BUCKETS = 32
REL_MAX_DIST = 128
PEER_HEADS = 8
PEER_NKEYS = 128
PEER_EXPERTS = PEER_NKEYS * PEER_NKEYS
PEER_QDIM = 128
PEER_TOPK = 16
PEER_CHUNK = 128
N_EVEN = (DEPTH + 1) // 2
N_ODD = DEPTH // 2
NEG_INF = -1e30
FORCE_SCORE = 1e6


def rms_norm_2(x, g):
    xf = x.astype(jnp.float32)
    y = xf * lax.rsqrt(jnp.mean(xf * xf, axis=-1, keepdims=True) + EPS)
    return (y * g.astype(jnp.float32)).astype(x.dtype)

def modulate(h, shift, scale):
    return h * (1 + scale[:, None, :]) + shift[:, None, :]

def masked_softmax(s, mask):
    s = jnp.where(mask, s.astype(jnp.float32), NEG_INF)
    return jax.nn.softmax(s, axis=-1) * mask

def rel_bucket(dist):
    n = jnp.maximum(dist, 0)
    max_exact = REL_BUCKETS // 2
    nf = jnp.maximum(n, 1).astype(jnp.float32)
    large = max_exact + (jnp.log(nf / max_exact) / math.log(REL_MAX_DIST / max_exact)
                         * (REL_BUCKETS - max_exact)).astype(jnp.int32)
    large = jnp.minimum(large, REL_BUCKETS - 1)
    return jnp.where(n < max_exact, n, large)

def short_conv(u, w):
    return lax.conv_general_dilated(
        u, w.astype(u.dtype)[:, None, :], window_strides=(1,), padding=((CONV_K - 1, 0),),
        dimension_numbers=('NWC', 'WIO', 'NWC'), feature_group_count=u.shape[-1])

def fox_attention(q, k, v, logf):
    B, S, H, Dh = q.shape
    nb = S // Q_BLOCK
    cum_t = jnp.cumsum(logf, axis=1).transpose(0, 2, 1)
    kpos = jnp.arange(S)
    scale = Dh ** -0.5
    qb = q.reshape(B, nb, Q_BLOCK, H, Dh).swapaxes(0, 1)
    cb = cum_t.reshape(B, H, nb, Q_BLOCK).transpose(2, 0, 1, 3)
    tb = kpos.reshape(nb, Q_BLOCK)

    def block(args):
        qi, ci, ti = args
        s = jnp.einsum('bqhd,bkhd->bhqk', qi, k).astype(jnp.float32) * scale
        s = s + (ci[..., None] - cum_t[:, :, None, :])
        p = masked_softmax(s, ti[:, None] >= kpos[None, :])
        return jnp.einsum('bhqk,bkhd->bqhd', p.astype(v.dtype), v)

    out = lax.map(block, (qb, cb, tb))
    return out.swapaxes(0, 1).reshape(B, S, H, Dh)

def conv_fox_mixer(h, w_in, b_f, conv_w, q_g, k_g, w_out):
    B, S, _ = h.shape
    splits = list(np.cumsum([CONV_CH] * 3 + [FOX_WIDTH] * 3))
    cb, cc, ch, q, k, v, f = jnp.split(h @ w_in, splits, axis=-1)
    conv_out = cb * short_conv(cc * ch, conv_w)
    q = rms_norm_2(q.reshape(B, S, FOX_HEADS, HEAD_DIM), q_g)
    k = rms_norm_2(k.reshape(B, S, FOX_HEADS, HEAD_DIM), k_g)
    v = v.reshape(B, S, FOX_HEADS, HEAD_DIM)
    logf = jax.nn.log_sigmoid((f + b_f).astype(jnp.float32))
    attn = fox_attention(q, k, v, logf).reshape(B, S, FOX_WIDTH)
    return jnp.concatenate([conv_out, attn], axis=-1) @ w_out

def nsa_mixer(h, w_in, b_gate, q_g, k_g, cmp_pos, cmp_w1, cmp_w2, rel_table, w_out):
    B, S, _ = h.shape
    G, J, Dh = NSA_GROUPS, NSA_HPG, HEAD_DIM
    f32 = jnp.float32
    splits = list(np.cumsum([NSA_WIDTH] + [NSA_KV] * 6))
    q, kc, vc, ks, vs, kw, vw, gl = jnp.split(h @ w_in, splits, axis=-1)
    q = rms_norm_2(q.reshape(B, S, G, J, Dh), q_g)
    kc, vc, ks, vs, kw, vw = [a.reshape(B, S, G, Dh) for a in (kc, vc, ks, vs, kw, vw)]
    ks = rms_norm_2(ks, k_g[1])
    kw = rms_norm_2(kw, k_g[2])
    gates = jax.nn.sigmoid((gl + b_gate).astype(f32)).reshape(B, S, G, J, 3).astype(h.dtype)
    tpos = jnp.arange(S)
    table = rel_table.reshape(REL_BUCKETS, G, J)
    scale = Dh ** -0.5

    n_cmp = (S - CMP_LEN) // CMP_STRIDE + 1
    starts = jnp.arange(n_cmp) * CMP_STRIDE
    ends = starts + CMP_LEN - 1
    tok = starts[:, None] + jnp.arange(CMP_LEN)[None, :]

    def compress(a, pos, w1, w2):
        blk = a[:, tok] + pos[:, None, :]
        blk = blk.transpose(0, 1, 3, 2, 4).reshape(B, n_cmp, G, CMP_LEN * Dh)
        return jax.nn.gelu(blk @ w1) @ w2

    Kc = rms_norm_2(compress(kc, cmp_pos[0], cmp_w1[0], cmp_w2[0]), k_g[0])
    Vc = compress(vc, cmp_pos[1], cmp_w1[1], cmp_w2[1])
    s_c = jnp.einsum('bsgjd,bngd->bgjsn', q, Kc).astype(f32) * scale
    s_c = s_c + table[rel_bucket(tpos[:, None] - ends[None, :])].transpose(2, 3, 0, 1)
    p_c = masked_softmax(s_c, ends[None, :] <= tpos[:, None])
    o_c = jnp.einsum('bgjsn,bngd->bsgjd', p_c.astype(Vc.dtype), Vc)

    n_slc = S // SLC_LEN
    top_n = min(SLC_TOPN, n_slc)
    blk_ids = jnp.arange(n_slc)
    bstart = blk_ids * SLC_LEN
    overlap = ((starts[:, None] < bstart[None, :] + SLC_LEN)
               & (starts[:, None] + CMP_LEN > bstart[None, :])).astype(f32)
    imp = jnp.einsum('bgjsn,nm->bgsm', p_c, overlap)
    cur = tpos // SLC_LEN
    forced = (blk_ids[None, :] == 0) | (blk_ids[None, :] == cur[:, None]) | (blk_ids[None, :] == cur[:, None] - 1)
    imp = jnp.where(forced, FORCE_SCORE, jnp.where(bstart[None, :] <= tpos[:, None], imp, -1.0))
    sel_score, sel_idx = lax.top_k(imp, top_n)
    sel_valid = sel_score >= 0

    Ks = ks.reshape(B, n_slc, SLC_LEN, G, Dh).transpose(0, 3, 1, 2, 4)
    Vs = vs.reshape(B, n_slc, SLC_LEN, G, Dh).transpose(0, 3, 1, 2, 4)
    nq = S // SLC_QCHUNK
    bi = jnp.arange(B)[:, None, None, None]
    gi = jnp.arange(G)[None, :, None, None]

    def slc_chunk(args):
        qi, idx, val, ti = args
        Kg = Ks[bi, gi, idx]
        Vg = Vs[bi, gi, idx]
        kpos = idx[..., None] * SLC_LEN + jnp.arange(SLC_LEN)
        dist = ti[None, None, :, None, None] - kpos
        mask = val[..., None] & (dist >= 0)
        bias = jnp.moveaxis(table[rel_bucket(dist), gi[..., None]], -1, 2)
        s = jnp.einsum('bqgjd,bgqnld->bgjqnl', qi, Kg).astype(f32) * scale + bias
        sh = s.shape
        m = jnp.broadcast_to(mask[:, :, None], sh).reshape(sh[:4] + (-1,))
        p = masked_softmax(s.reshape(sh[:4] + (-1,)), m).reshape(sh)
        return jnp.einsum('bgjqnl,bgqnld->bqgjd', p.astype(Vg.dtype), Vg)

    qs = q.reshape(B, nq, SLC_QCHUNK, G, J, Dh).swapaxes(0, 1)
    idx_s = sel_idx.reshape(B, G, nq, SLC_QCHUNK, top_n).transpose(2, 0, 1, 3, 4)
    val_s = sel_valid.reshape(B, G, nq, SLC_QCHUNK, top_n).transpose(2, 0, 1, 3, 4)
    t_s = tpos.reshape(nq, SLC_QCHUNK)
    o_s = lax.map(slc_chunk, (qs, idx_s, val_s, t_s)).swapaxes(0, 1).reshape(B, S, G, J, Dh)

    kwp = jnp.pad(kw, ((0, 0), (WINDOW, 0), (0, 0), (0, 0)))
    vwp = jnp.pad(vw, ((0, 0), (WINDOW, 0), (0, 0), (0, 0)))
    nb = S // Q_BLOCK
    span = Q_BLOCK + WINDOW
    koff = jnp.arange(span)
    dist_w = jnp.arange(Q_BLOCK)[:, None] + WINDOW - koff[None, :]
    band = (dist_w >= 0) & (dist_w < WINDOW)
    bias_w = table[rel_bucket(dist_w)].transpose(2, 3, 0, 1)

    def win_block(args):
        qi, i = args
        start = i * Q_BLOCK
        kb = lax.dynamic_slice_in_dim(kwp, start, span, axis=1)
        vb = lax.dynamic_slice_in_dim(vwp, start, span, axis=1)
        s = jnp.einsum('bqgjd,bkgd->bgjqk', qi, kb).astype(f32) * scale + bias_w
        mask = band & ((start - WINDOW + koff) >= 0)[None, :]
        p = masked_softmax(s, mask)
        return jnp.einsum('bgjqk,bkgd->bqgjd', p.astype(vb.dtype), vb)

    qw = q.reshape(B, nb, Q_BLOCK, G, J, Dh).swapaxes(0, 1)
    o_w = lax.map(win_block, (qw, jnp.arange(nb))).swapaxes(0, 1).reshape(B, S, G, J, Dh)

    o = gates[..., 0:1] * o_c + gates[..., 1:2] * o_s + gates[..., 2:3] * o_w
    return o.reshape(B, S, NSA_WIDTH) @ w_out

def peer_ffn(h, w_q, sub_keys, u, v):
    B, S, D = h.shape
    T = B * S
    half = PEER_QDIM // 2
    hc = h.reshape(T // PEER_CHUNK, PEER_CHUNK, D)

    def chunk(xc):
        q = (xc @ w_q).reshape(-1, PEER_HEADS, 2, half)
        s = jnp.einsum('thpd,pkd->thpk', q, sub_keys).astype(jnp.float32)
        sv, si = lax.top_k(s, PEER_TOPK)
        cand = (sv[:, :, 0, :, None] + sv[:, :, 1, None, :]).reshape(-1, PEER_HEADS, PEER_TOPK * PEER_TOPK)
        cand_id = (si[:, :, 0, :, None] * PEER_NKEYS + si[:, :, 1, None, :]).reshape(-1, PEER_HEADS, PEER_TOPK * PEER_TOPK)
        cv, ci = lax.top_k(cand, PEER_TOPK)
        eid = jnp.take_along_axis(cand_id, ci, axis=-1)
        g = jax.nn.softmax(cv, axis=-1)
        ue = u[eid]
        ve = v[eid]
        a = jax.nn.gelu(jnp.einsum('td,thkd->thk', xc, ue)).astype(jnp.float32)
        return jnp.einsum('thk,thkd->td', (g * a).astype(ve.dtype), ve)

    return lax.map(chunk, hc).reshape(B, S, D)

def second_inputs(seed: int = 0) -> dict:
    key = jax.random.key(seed)
    ks = jax.random.split(key, 24)
    D = D_MODEL

    def nrm(k, shape, s):
        return jax.random.normal(k, shape, jnp.float32) * s

    return {
        'x': nrm(ks[0], (BATCH, SEQ, D), 1.0),
        'c': nrm(ks[1], (BATCH, D), 1.0),
        'ada_w': nrm(ks[2], (DEPTH, D, 6 * D), 0.5 * D ** -0.5),
        'ada_b': nrm(ks[3], (DEPTH, 6 * D), 0.01),
        'norm_g': 1.0 + nrm(ks[4], (DEPTH, 2, D), 0.05),
        'even_w_in': nrm(ks[5], (N_EVEN, D, EVEN_IN), D ** -0.5),
        'even_b_f': jax.random.uniform(ks[6], (N_EVEN, FOX_HEADS), jnp.float32, 1.0, 6.0),
        'even_conv_w': nrm(ks[7], (N_EVEN, CONV_K, CONV_CH), CONV_K ** -0.5),
        'even_q_g': 1.0 + nrm(ks[8], (N_EVEN, HEAD_DIM), 0.05),
        'even_k_g': 1.0 + nrm(ks[9], (N_EVEN, HEAD_DIM), 0.05),
        'even_w_out': nrm(ks[10], (N_EVEN, CONV_CH + FOX_WIDTH, D), (CONV_CH + FOX_WIDTH) ** -0.5),
        'odd_w_in': nrm(ks[11], (N_ODD, D, ODD_IN), D ** -0.5),
        'odd_b_gate': nrm(ks[12], (N_ODD, 3 * NSA_HEADS), 0.01),
        'odd_q_g': 1.0 + nrm(ks[13], (N_ODD, HEAD_DIM), 0.05),
        'odd_k_g': 1.0 + nrm(ks[14], (N_ODD, 3, HEAD_DIM), 0.05),
        'odd_cmp_pos': nrm(ks[15], (N_ODD, 2, CMP_LEN, HEAD_DIM), 0.1),
        'odd_cmp_w1': nrm(ks[16], (N_ODD, 2, CMP_LEN * HEAD_DIM, HEAD_DIM), (CMP_LEN * HEAD_DIM) ** -0.5),
        'odd_cmp_w2': nrm(ks[17], (N_ODD, 2, HEAD_DIM, HEAD_DIM), HEAD_DIM ** -0.5),
        'odd_w_out': nrm(ks[18], (N_ODD, NSA_WIDTH, D), NSA_WIDTH ** -0.5),
        'rel_table': nrm(ks[19], (REL_BUCKETS, NSA_HEADS), 0.5),
        'peer_w_q': nrm(ks[20], (DEPTH, D, PEER_HEADS * PEER_QDIM), D ** -0.5),
        'peer_keys': nrm(ks[21], (DEPTH, 2, PEER_NKEYS, PEER_QDIM // 2), (PEER_QDIM // 2) ** -0.5),
        'peer_u': nrm(ks[22], (DEPTH, PEER_EXPERTS, D), D ** -0.5),
        'peer_v': nrm(ks[23], (DEPTH, PEER_EXPERTS, D), PEER_HEADS ** -0.5),
    }

def second_block(x, c, ada_w, ada_b, norm_g, even_w_in, even_b_f, even_conv_w, even_q_g, even_k_g,
              even_w_out, odd_w_in, odd_b_gate, odd_q_g, odd_k_g, odd_cmp_pos, odd_cmp_w1, odd_cmp_w2,
              odd_w_out, rel_table, peer_w_q, peer_keys, peer_u, peer_v):
    mods = jnp.einsum('bd,lde->lbe', jax.nn.silu(c), ada_w) + ada_b[:, None, :]
    for layer in range(DEPTH):
        sh1, sc1, g1, sh2, sc2, g2 = jnp.split(mods[layer], 6, axis=-1)
        h = modulate(rms_norm_2(x, norm_g[layer, 0]), sh1, sc1)
        i = layer // 2
        if layer % 2 == 0:
            y = conv_fox_mixer(h, even_w_in[i], even_b_f[i], even_conv_w[i], even_q_g[i], even_k_g[i],
                               even_w_out[i])
        else:
            y = nsa_mixer(h, odd_w_in[i], odd_b_gate[i], odd_q_g[i], odd_k_g[i], odd_cmp_pos[i],
                          odd_cmp_w1[i], odd_cmp_w2[i], rel_table, odd_w_out[i])
        x = x + g1[:, None, :] * y
        h = modulate(rms_norm_2(x, norm_g[layer, 1]), sh2, sc2)
        x = x + g2[:, None, :] * peer_ffn(h, peer_w_q[layer], peer_keys[layer], peer_u[layer], peer_v[layer])
    return x


def setup_inputs(seed=0):
    out = dict(first_inputs(seed))
    for name, value in second_inputs(seed + 1).items():
        if name != "x":
            out[name + "_2"] = value
    return out


def reference(
    x, c, w_ada, b_ada, norm_g, w_in, a_q_norm, a_k_norm, b_lb, b_out_norm, c_q_norm, c_k_norm,
    w_out, w_up, conv_w, conv_b, w_down, c_2, ada_w_2, ada_b_2, norm_g_2, even_w_in_2,
    even_b_f_2, even_conv_w_2, even_q_g_2, even_k_g_2, even_w_out_2, odd_w_in_2, odd_b_gate_2,
    odd_q_g_2, odd_k_g_2, odd_cmp_pos_2, odd_cmp_w1_2, odd_cmp_w2_2, odd_w_out_2, rel_table_2,
    peer_w_q_2, peer_keys_2, peer_u_2, peer_v_2,
):
    x = first_block(
        x, c, w_ada, b_ada, norm_g, w_in, a_q_norm, a_k_norm, b_lb, b_out_norm, c_q_norm,
        c_k_norm, w_out, w_up, conv_w, conv_b, w_down,
    )
    return second_block(
        x, c_2, ada_w_2, ada_b_2, norm_g_2, even_w_in_2, even_b_f_2, even_conv_w_2, even_q_g_2,
        even_k_g_2, even_w_out_2, odd_w_in_2, odd_b_gate_2, odd_q_g_2, odd_k_g_2, odd_cmp_pos_2,
        odd_cmp_w1_2, odd_cmp_w2_2, odd_w_out_2, rel_table_2, peer_w_q_2, peer_keys_2, peer_u_2,
        peer_v_2,
    )


_drawn_inputs = setup_inputs


def setup_inputs(seed=0):
    import zlib

    import numpy as np

    out = dict(_drawn_inputs(seed))
    spreads = {}
    factors = {'norm_g': 4.089,
     'a_q_norm': 8.0,
     'a_k_norm': 8.0,
     'b_out_norm': 8.0,
     'c_q_norm': 8.0,
     'c_k_norm': 8.0,
     'conv_b': 5.767,
     'ada_b_2': 5.015,
     'norm_g_2': 2.739,
     'even_q_g_2': 56.248,
     'even_k_g_2': 56.525,
     'odd_b_gate_2': 64.0,
     'odd_q_g_2': 47.817,
     'odd_k_g_2': 43.206,
     'odd_cmp_pos_2': 50.295,
     'rel_table_2': 26.28,
     'even_b_f_2': 30.912,
     'odd_cmp_w1_2': 3.312,
     'odd_cmp_w2_2': 2.738,
     'peer_w_q_2': 3.102,
     'peer_keys_2': 3.149,
     'peer_u_2': 3.807,
     'peer_v_2': 3.122}
    for name, (base, spread) in spreads.items():
        noise = np.random.default_rng([zlib.crc32(name.encode()), seed]).standard_normal(out[name].shape)
        drawn = base * np.exp(spread * noise) if base else spread * noise
        out[name] = jnp.asarray(drawn.astype(out[name].dtype))
    for name, factor in factors.items():
        out[name] = (out[name] * factor).astype(out[name].dtype)
    return out
```

```python
import math
from contextlib import ExitStack

import numpy as np

import concourse.bass as bass
from concourse import mybir

F32 = mybir.dt.float32
U32 = mybir.dt.uint32
ALU = mybir.AluOpType
ACT = mybir.ActivationFunctionType
AX = mybir.AxisListType

P = 128
D = 1024
T = 256
HD = 64
DC = D // P
TT = T // P
DEPTH = 2
EPS = 1e-6
F_MIN = 1e-6
NEG = -1e30
FF = 2816
FC = FF // P
GRID_W = 64
SCALE = HD ** -0.5
UNIT = 1024
RING = 8
ADA_RING = 4
ADA = 6 * DC
N_CMP, CMP_LEN, CMP_STRIDE = 15, 32, 16
NSA_H, REL_BUCKETS, REL_MAX = 16, 32, 128
PH, NK, TOPK = 8, 128, 16

U_IN, U_OUT, U_UP, U_DOWN = 22, DC, 2 * FC, FC
U_LAYER = U_IN + U_OUT + U_UP + U_DOWN
U_FOX = 25 + DC
U_NSA = 21 + 8 + DC
U_PQ = DC
B_FOX = DEPTH * U_LAYER
B_PEER = (B_FOX + U_FOX + U_PQ, B_FOX + U_FOX + U_PQ + 2 * NK + U_NSA + U_PQ)
B_NSA = B_PEER[0] + 2 * NK
NG = NK // RING


def columns():
    at, n = {}, 0
    for l in range(DEPTH):
        for name, k in (("ng1", DC), ("ng2", DC), ("cw0", 2 * FC), ("cw1", 2 * FC), ("cw2", 2 * FC), ("cb", 2 * FC),
                        ("aq", 1), ("ak", 1), ("cq", 1), ("ck_lo", 1), ("ck_hi", 1), ("bo", 1), ("lb", 4)):
            at[name, l] = n
            n += k
    for l in range(2 * DEPTH):
        at["bada", l] = n
        n += ADA
    for name, k in (("png", 4 * DC), ("fcw", 12), ("fq", 1), ("fk_lo", 1), ("fk_hi", 1), ("bf", 1),
                    ("nq", 1), ("nkc_lo", 1), ("nkc_hi", 1), ("nks_lo", 1), ("nks_hi", 1), ("nkw_lo", 1), ("nkw_hi", 1),
                    ("bgate", 48), ("pos", 2 * CMP_LEN)):
        at[name] = n
        n += k
    return at, n


COL, N_COL = columns()

CONST = {}
_n = 0
for _name, _k in (("ident", P), ("ones", P), ("blk", P), ("rot", P), ("cos", T), ("sin", T), ("iota", P),
                  ("half", 2), ("lvl", 8), ("sel8", 8 * P), ("cmask", 2 * N_CMP), ("vmask", 8)):
    CONST[_name] = (_n, _n + _k)
    _n += _k
N_CONST = _n
N_ALIBI, N_LM, N_CAUSAL = 6 * 384, 7 * P, 384


def constants():
    out = np.zeros((P, N_CONST), np.float32)
    put = lambda name, v: out[:, CONST[name][0]:CONST[name][1]].__setitem__(slice(None), v)
    p = np.arange(P)
    put("ident", np.eye(P))
    put("ones", 1.0)
    put("blk", (p[:, None] // HD == p[None] // HD))
    rot = np.zeros((P, P))
    for m in range(P):
        if m % 32 < 16:
            rot[m + 16, m] = -1.0
        else:
            rot[m - 16, m] = 1.0
    put("rot", rot)
    inv = np.float32(10000.0) ** (-np.arange(0, 32, 2, dtype=np.float32) / np.float32(32))
    t = np.arange(T)
    row, col = (t // GRID_W).astype(np.float32), (t % GRID_W).astype(np.float32)
    ang = np.where((p % HD < 32)[:, None], row[None], col[None]).astype(np.float32) * inv[p % 16][:, None]
    put("cos", np.cos(ang.astype(np.float32)))
    put("sin", np.sin(ang.astype(np.float32)))
    put("iota", p[None, :])
    put("half", np.stack([p < HD, p >= HD], 1))
    fwd = p < HD
    lv = np.zeros((P, 8))
    lv[:, 0], lv[:, 1] = np.where(fwd, 0, -1), np.where(fwd, NEG, 0)
    lv[:, 2], lv[:, 3] = np.where(fwd, 1, 0), np.where(fwd, 0, NEG)
    lv[:, 4], lv[:, 5] = np.where(fwd, -1, 0), np.where(fwd, 0, NEG)
    lv[:, 6], lv[:, 7] = np.where(fwd, 0, 1), np.where(fwd, NEG, 0)
    put("lvl", lv)
    sel = np.zeros((P, 8, P))
    for h in range(8):
        sel[h, h, :] = -1.0 / SCALE
    put("sel8", sel.reshape(P, -1))
    tq = p[:, None, None] + P * np.arange(TT)[None, :, None]
    ends = (np.arange(N_CMP) * CMP_STRIDE + CMP_LEN - 1)[None, None, :]
    put("cmask", (ends <= tq).reshape(P, -1))
    put("vmask", (p[:, None] // 16 == np.arange(8)[None]) & (p[:, None] % 16 < N_CMP))
    return out


def mixer_constants():
    p = np.arange(P)
    x = np.arange(384)
    d = x[None] - P - p[:, None]
    m = (np.abs(d) <= 64).astype(np.float32) + (d % 4 == 0) + (d % 16 == 0)
    slopes = (2.0 ** (-8.0 * np.arange(1, 7) / 6)).astype(np.float32)
    logm = np.log(np.maximum(m, 1))
    al = -slopes[None, :, None] * np.abs(d)[:, None, :] + logm[:, None, :]
    al = np.where(m[:, None, :] > 0, al, NEG).astype(np.float32)
    causal = np.where(d <= 0, 0.0, NEG).astype(np.float32)
    lm = [(p[:, None] // b == p[None] // b) for b in (64, 32, 16, 8, 4, 2)] + [np.eye(P)]
    return np.concatenate([al.reshape(P, -1)] + [a.astype(np.float32) for a in lm] + [causal], 1).astype(np.float32)


def bucket_strip():
    n = np.arange(2 * T) - (T - 1)
    nf = np.maximum(n, 1).astype(np.float32)
    large = 16 + (np.log(nf / 16) / math.log(REL_MAX / 16) * 16).astype(np.int32)
    b = np.where(n < 16, np.maximum(n, 0), np.minimum(large, REL_BUCKETS - 1))
    out = np.zeros((P, 2 * T), np.float32)
    for k in range(REL_BUCKETS):
        out[k] = (b == k) & (n >= 0)
    out[REL_BUCKETS] = n < 0
    return out


def tile_unit(w):
    return w.reshape(DC, P, P).transpose(1, 0, 2).reshape(P, UNIT)


def pad_cols(w):
    return np.concatenate([w, np.zeros((w.shape[0], P - w.shape[1]), w.dtype)], 1)


def heads(w, hs):
    return np.concatenate([w[:, h * HD:(h + 1) * HD] for h in hs], 1)


def lay_out(x):
    A = np.asarray
    g = {k: A(v) for k, v in x.items()}
    out = {}
    f32 = np.float32
    xT = g["x"][0].T.reshape(DC, P, T).transpose(1, 0, 2)
    out["xT_in"] = np.ascontiguousarray(xT)
    par = np.zeros((P, N_COL), f32)
    dup = lambda v: np.concatenate([v, v])
    lo = lambda v: np.concatenate([v, np.zeros_like(v)])
    hi = lambda v: np.concatenate([np.zeros_like(v), v])
    ch = lambda v: v.reshape(-1, P).T
    for l in range(DEPTH):
        def put(name, v):
            v = v if v.ndim == 2 else v[:, None]
            par[:v.shape[0], COL[name, l]:COL[name, l] + v.shape[1]] = v
        put("ng1", ch(g["norm_g"][l, 0])); put("ng2", ch(g["norm_g"][l, 1]))
        for j in range(3):
            put(f"cw{j}", ch(g["conv_w"][l, j]))
        put("cb", ch(g["conv_b"][l]))
        put("aq", dup(g["a_q_norm"][l])); put("ak", dup(g["a_k_norm"][l]))
        put("cq", dup(g["c_q_norm"][l])); put("ck_lo", lo(g["c_k_norm"][l])); put("ck_hi", hi(g["c_k_norm"][l]))
        put("bo", dup(g["b_out_norm"][l]))
        put("lb", np.concatenate([g["b_lb"][0, l].reshape(4, HD).T, g["b_lb"][1, l].reshape(4, HD).T], 0))
        put("bada", ch(g["b_ada"][l]))
    for l in range(DEPTH):
        par[:, COL["bada", DEPTH + l]:COL["bada", DEPTH + l] + ADA] = ch(g["ada_b_2"][l])
    def put(name, v):
        v = v if v.ndim == 2 else v[:, None]
        par[:v.shape[0], COL[name]:COL[name] + v.shape[1]] = v
    put("png", ch(g["norm_g_2"].reshape(-1)))
    put("fcw", np.concatenate([ch(g["even_conv_w_2"][0, j]) for j in range(3)], 1))
    put("fq", dup(g["even_q_g_2"][0])); put("fk_lo", lo(g["even_k_g_2"][0])); put("fk_hi", hi(g["even_k_g_2"][0]))
    put("bf", g["even_b_f_2"][0])
    put("nq", dup(g["odd_q_g_2"][0]))
    for i, n in enumerate(("nkc", "nks", "nkw")):
        put(n + "_lo", lo(g["odd_k_g_2"][0, i])); put(n + "_hi", hi(g["odd_k_g_2"][0, i]))
    put("bgate", np.broadcast_to(g["odd_b_gate_2"][0], (P, 48)))
    pos = g["odd_cmp_pos_2"][0]
    put("pos", np.concatenate([dup(pos[0].T), dup(pos[1].T)], 1))
    out["params"] = par
    out["consts"] = constants()
    out["mixer_consts"] = mixer_constants()
    order = [(2 * gg + hh) * 4 + j for gg in range(2) for j in range(4) for hh in range(2)]
    rel = np.zeros((P, NSA_H), f32)
    rel[:REL_BUCKETS] = g["rel_table_2"][:, order]
    rel[REL_BUCKETS] = NEG
    out["rel"] = np.concatenate([bucket_strip(), rel], 1)
    out["c_rows"] = np.ascontiguousarray(np.stack([np.broadcast_to(g["c"][0], (P, D)), np.broadcast_to(g["c_2"][0], (P, D))], 1))
    out["ada"] = np.stack([w.T.reshape(ADA, P, D) for w in (*g["w_ada"], *g["ada_w_2"])])

    units = []
    for l in range(DEPTH):
        w = g["w_in"][l]
        cut = np.split(w, np.cumsum([384, 128, 128, 256, 256, 256, 256, 256, 384, 128]), 1)
        aq, ak, av, bq, bff, bfb, bi, bg, cq, ck, cv = cut
        tiles = [np.concatenate([bff[:, h * HD:(h + 1) * HD], bfb[:, h * HD:(h + 1) * HD]], 1) for h in range(4)]
        tiles += [heads(bq, (h, h)) for h in range(4)]
        tiles += [heads(aq, (p, p + 3)) for p in range(3)] + [ak]
        tiles += [heads(cq, (p, p + 3)) for p in range(3)] + [ck]
        tiles += [av, cv, bi[:, :P], bi[:, P:], bg[:, :P], bg[:, P:]]
        assert len(tiles) == U_IN
        units += [tile_unit(t) for t in tiles]
        rows = g["w_out"][l].reshape(16, HD, D)
        order = [h for p in range(3) for h in (p, p + 3)] + [6, 7, 8, 9] + [10 + h for p in range(3) for h in (p, p + 3)]
        wo = rows[order].reshape(D, D)
        units += [tile_unit(wo[:, n * P:(n + 1) * P]) for n in range(DC)]
        wu = g["w_up"][l]
        for i in range(FC):
            for s in (i, FC + i):
                units.append(tile_unit(wu[:, s * P:(s + 1) * P]))
        blocks = g["w_down"][l].reshape(FC, P, DC, P).transpose(2, 0, 1, 3).reshape(FC, 8, P, P)
        units += list(blocks.transpose(0, 2, 1, 3).reshape(FC, P, UNIT))
    out["stream_first"] = np.stack(units)

    units = []
    w = g["even_w_in_2"][0]
    order = list(range(0, 24))
    units += [tile_unit(w[:, n * P:(n + 1) * P]) for n in order] + [tile_unit(pad_cols(w[:, 3072:3080]))]
    units += [tile_unit(g["even_w_out_2"][0][:, n * P:(n + 1) * P]) for n in range(DC)]
    units += [tile_unit(g["peer_w_q_2"][0][:, n * P:(n + 1) * P]) for n in range(DC)]
    out["stream_fox"] = np.stack(units)

    units = []
    w = g["odd_w_in_2"][0]
    pairs = [((2 * gg) * 4 + j, (2 * gg + 1) * 4 + j) for gg in range(2) for j in range(4)]
    kv = w[:, 1024:1024 + 6 * 256]
    tile = lambda i, c: kv[:, i * 256 + c * P:i * 256 + (c + 1) * P]
    for i in (0, 1):
        units += [tile_unit(tile(i, 0)), tile_unit(tile(i, 1))]
    units += [tile_unit(heads(w[:, :1024], pr)) for pr in pairs]
    for i in (2, 4, 3, 5):
        units += [tile_unit(tile(i, 0)), tile_unit(tile(i, 1))]
    units += [tile_unit(pad_cols(w[:, 2560:2608]))]
    w1 = g["odd_cmp_w1_2"][0].reshape(2, CMP_LEN, HD, HD)
    bd = np.zeros((2, CMP_LEN, P, P), f32)
    bd[:, :, :HD, :HD] = w1
    bd[:, :, HD:, HD:] = w1
    units += list(bd.reshape(2, 4, 8, P, P).transpose(0, 1, 3, 2, 4).reshape(8, P, UNIT))
    rows = g["odd_w_out_2"][0].reshape(16, HD, D)
    wo = rows[[h for pr in pairs for h in pr]].reshape(D, D)
    units += [tile_unit(wo[:, n * P:(n + 1) * P]) for n in range(DC)]
    units += [tile_unit(g["peer_w_q_2"][1][:, n * P:(n + 1) * P]) for n in range(DC)]
    out["stream_nsa"] = np.stack(units)

    w2 = g["odd_cmp_w2_2"][0]
    bd = np.zeros((2, P, P), f32)
    bd[:, :HD, :HD] = w2
    bd[:, HD:, HD:] = w2
    keys = np.zeros((DEPTH, P, 2, NK), f32)
    for p_ in range(2):
        keys[:, p_ * HD:(p_ + 1) * HD, p_, :] = g["peer_keys_2"][:, p_].transpose(0, 2, 1)
    out["small"] = np.ascontiguousarray(np.concatenate([bd[0], bd[1], keys[0].reshape(P, -1), keys[1].reshape(P, -1)], 1))
    u = g["peer_u_2"].reshape(DEPTH, NK, NK, DC, P)
    out["peer_u"] = np.ascontiguousarray(u.transpose(0, 2, 4, 3, 1)).reshape(DEPTH, NK, P, UNIT)
    v = g["peer_v_2"].reshape(DEPTH, NK, NK, D)
    out["peer_v"] = np.ascontiguousarray(v.transpose(0, 2, 1, 3))
    return out


def build(nc, io, out):
    ctx = ExitStack()
    with ctx:
        sb = lambda name, shape, dt=F32: ctx.enter_context(nc.sbuf_tensor(name, shape, dt))
        sems = {}

        def sem(name):
            if name not in sems:
                sems[name] = ctx.enter_context(nc.semaphore(name))
            return sems[name]

        ring = sb("ring", [P, RING, DC, P])
        xT = sb("xT", [P, DC, T])
        hT = sb("hT", [P, DC, T])
        consts = sb("consts", [P, N_CONST])
        params = sb("params", [P, N_COL])
        mod = sb("mod", [P, 2 * DEPTH, 6, DC])
        gscale = sb("gscale", [P, 2 * DEPTH, 2, DC])
        std = sb("std", [P, T])
        rstd = sb("rstd", [P, T])
        epsc = sb("epsc", [P, 1])
        sums = sb("sums", [P, 4, 2])
        nmax = sb("nmax", [P, 4, 2])
        rinv = sb("rinv", [P, 4, 2])
        lbt = sb("lbt", [P, 8, 4])
        extra = sb("extra", [P, 2 * UNIT])
        arena = sb("arena", [P, 128 * T])

        top = [0]

        def place(*shape):
            n = int(np.prod(shape))
            v = arena[:, top[0]:top[0] + n]
            top[0] += n
            assert top[0] <= 128 * T, top[0]
            if len(shape) == 1:
                return v
            names = "abcde"[:len(shape)]
            return v.rearrange(f"p ({' '.join(names)}) -> p {' '.join(names)}", **dict(zip(names[1:], shape[1:])))

        const = lambda name: consts[:, CONST[name][0]:CONST[name][1]]
        ident, ones, blk, rot = const("ident"), const("ones"), const("blk"), const("rot")
        cos, sin, iota, half, lvl = const("cos"), const("sin"), const("iota"), const("half"), const("lvl")
        sel8 = const("sel8").rearrange("p (h m) -> p h m", h=8)
        cmask = const("cmask").rearrange("p (t n) -> p t n", t=TT)

        def col(name, l=None, k=0, n=1):
            at = COL[name if l is None else (name, l)] + k
            return params[:, at:at + n]

        crow = place(2, D)
        ada = place(2, D)
        junk = place(D)
        mixc = place(N_ALIBI + N_LM + N_CAUSAL)
        alibi = mixc[:, 0:N_ALIBI].rearrange("p (h x) -> p h x", h=6)
        lmask = mixc[:, N_ALIBI:N_ALIBI + N_LM].rearrange("p (l t) -> p l t", l=7)
        causal = mixc[:, N_ALIBI + N_LM:]
        common = top[0]
        mixT = place(DC, T)
        sq = place(DC, T)
        levels = top[0]
        dl = place(2, 4, T)
        eq, ek = place(2, 4, T), place(2, 4, T)
        after_levels, top[0] = top[0], levels
        sc = place(2, 2, T)
        pr = place(3, 2, T)
        dg = place(3, 2, P)
        pt = place(2, 2, 2, P)
        oB = place(2, T)
        assert top[0] <= after_levels
        top[0] = after_levels
        mixers = top[0]
        rawA, rawC = place(4, T), place(4, T)
        vA, vC = place(TT, 2, P), place(TT, 2, P)
        kzA, kzC = place(2, T), place(2, T)
        rsq = place(4, T)
        vB = place(TT, 4, P)
        fk = place(4, T)
        qB = place(4, T)
        gB = place(2, T)
        Cx = place(4, T + 1)
        C2 = place(4, T)
        ATd, ATo = place(4, TT, P), place(4, TT, P)
        ropec = C2
        first_end = top[0]
        top[0] = mixers
        zT = place(FC, T)
        cv = place(4, 2, T)
        sa = place(2, T)

        top[0] = levels
        ada_first = [place(D) for _ in range(6)]
        top[0] = mixers
        ada_first += [place(D) for _ in range(10)]
        ada_slot = lambda n: ada_first[n] if n < 16 else (ada[:, n % 4] if n % 4 < 2 else extra[:, (n % 2) * D:(n % 2 + 1) * D])
        top[0] = mixers
        cbT, prod, cmid = place(4, T), place(4, T), place(4, T)
        rawF = place(8, T)
        rsF = place(8, T)
        kzF = place(4, 2, T)
        vF = place(4, TT, 2, P)
        cum, lsig, fzero = place(T), place(T), place(T)
        top[0] = mixers
        rawQ, rsQ = place(8, T), place(8, T)
        kvc = place(2, 2, T)
        rawK = place(2, 2, T)
        kzN = place(2, 2, 2, T)
        vN = place(2, 2, TT, 2, P)
        Vc = place(2, 4, P)
        top[0] = 0
        relc = place(2 * T + NSA_H)
        bias = place(NSA_H, T)
        cbias = place(TT, NSA_H, 16)
        pcs = place(TT, NSA_H, 16)
        pcT = place(TT, 2, P)
        hid = place(2, 2, N_CMP)
        hidrep = place(2, 8, 16)
        posb = place(2)
        kcn, kcsq, kcrs = place(2, N_CMP), place(2, N_CMP), place(2, N_CMP)
        kzc = place(2, 2, N_CMP)
        gates = place(TT, 48)
        cmx, csm = place(TT, NSA_H), place(TT, NSA_H)
        vrep = place(2, P)
        assert top[0] <= common
        acts = arena[:, :].rearrange("p (j t) -> p j t", t=T)
        acts_g = arena[:, :].rearrange("p (g k t) -> p g k t", k=RING, t=T)
        top[0] = NK // 2 * T
        qP = place(PH, T)
        sP = place(TT, PH, 2, NK)
        wk = place(T)
        sv = place(TT, PH, 2, TOPK)
        siu = place(TT, PH, 2, TOPK).bitcast(U32)
        sif = place(TT, PH, 2, TOPK)
        cand = place(PH, TOPK, TOPK)
        cvv = place(TT, PH, TOPK)
        ciu = place(TT, PH, TOPK).bitcast(U32)
        cau = place(TT, 2, PH, TOPK).bitcast(U32)
        caf = place(TT, 2, PH, TOPK)
        hit = place(PH * TOPK, TOPK)
        chosen = place(TT, 3, PH, TOPK)
        gsum = place(TT, PH)
        chT = sb("chT", [P, 3, T])
        keysb = sb("keysb", [P, 2 * NK])
        w2bd = sb("w2bd", [P, 2, P])
        turn = sb("turn", [P, 2, 4])
        zero = sb("zero", [P, P])
        hot_r = extra[:, 0:8 * P].rearrange("p (b x) -> p b x", b=2)
        hot_c = extra[:, 8 * P:12 * P].rearrange("p (b x) -> p b x", b=2)
        HALF = NK // 2

        banks = [ctx.enter_context(nc.psum_tensor(f"bank{i}", [P, 512], F32)) for i in range(4)]
        lev = [ctx.enter_context(nc.psum_tensor(f"lev{i}", [P, 1024], F32)) for i in range(2)]
        S = lambda u: lev[0][:, 512 * (u % 2):512 * (u % 2) + 512].rearrange("p (h k) -> p h k", h=2)
        PTb = lambda u: lev[1][:, 512 * (u % 2):512 * (u % 2) + 512].rearrange("p (h c q) -> p h c q", h=2, c=2)

        job = {}
        NATT = 12

        def plan(name, n):
            for i in range(n):
                job[name + (i,)] = len(job)

        for l in range(DEPTH):
            plan(("norm", 2 * l), 1)
            plan(("in", l), U_IN // 2)
            plan(("statA", l), 2)
            plan(("rot", l), 2)
            plan(("statC", l), 2)
            plan(("att", l), NATT)
            plan(("ob", l), 1)
            plan(("statB", l), 1)
            plan(("out", l), 4)
            plan(("norm", 2 * l + 1), 1)
            plan(("up", l), FC)
            plan(("down", l), 4)
        plan(("norm", 4), 1)
        plan(("fin",), 13)
        plan(("statF",), 4)
        plan(("attF",), 8)
        plan(("foxout",), 4)
        plan(("norm", 5), 1)
        plan(("pq", 0), 4)
        plan(("ps", 0), 8)
        plan(("norm", 6), 1)
        plan(("relb",), 9)
        plan(("nin",), 11)
        plan(("cmp",), 4)
        plan(("kc",), 1)
        plan(("vc",), 2)
        plan(("statN",), 6)
        plan(("statK",), 1)
        plan(("cs",), 2)
        plan(("ct",), 1)
        plan(("attN",), 16)
        plan(("nsaout",), 4)
        plan(("norm", 7), 1)
        plan(("pq", 1), 4)
        plan(("ps", 1), 8)
        bank_of = lambda *j: banks[job[j] % 4]
        filled = lambda *j: (sem(f"filled{job[j] % 4}"), job[j] // 4 + 1)
        freed = lambda *j: (sem(f"freed{job[j] % 4}"), job[j] // 4 + 1)

        class Unit:
            def __init__(self, q, kz, v, bias, out, gate=None, forget=None, pre=None, first=True, last=True):
                self.q, self.kz, self.v, self.bias, self.out = q, kz, v, bias, out
                self.gate, self.forget, self.pre, self.first, self.last = gate, forget, pre, first, last

        window = lambda t: slice(P - P * t, P - P * t + T)

        def units_of(l):
            us = []
            for q, kz, v, al, o in ((rawA, kzA, vA, None, 0), (rawC, kzC, vC, alibi, 5)):
                for p in range(3):
                    for t in range(TT):
                        b = None if al is None else al[:, p::3, window(t)]
                        us.append(Unit(q[:, p, t * P:(t + 1) * P], kz, v, b, mixT[:, o + p, t * P:(t + 1) * P]))
            return us

        def fox_units():
            return [Unit(rawF[:, c, t * P:(t + 1) * P], kzF[:, c], vF[:, c],
                         causal[:, window(t)].unsqueeze(1).broadcast_to([P, 2, T]),
                         mixT[:, 4 + c, t * P:(t + 1) * P], forget=(2 * c, 2 * c + 1))
                    for c in range(4) for t in range(TT)]

        def nsa_units():
            us = []
            for c in range(8):
                g2, j = c // 4, c % 4
                for t in range(TT):
                    for br in range(2):
                        at = (8 * g2 + j) * 3 + 1 + br
                        us.append(Unit(rawQ[:, c, t * P:(t + 1) * P], kzN[:, br, g2], vN[:, br, g2],
                                       bias[:, 2 * c:2 * c + 2, :] if t else bias[:, 2 * c:2 * c + 2, P:T],
                                       mixT[:, c, t * P:(t + 1) * P], gate=gates[:, t, at:at + 13:12],
                                       pre=(Vc[:, g2, j], pcT[:, t, g2]) if br == 0 else None,
                                       first=br == 0, last=br == 1))
            return us

        keys_of = lambda un: un.bias.shape[-1] if un.bias is not None else T
        A0, F0, N0 = 0, DEPTH * NATT, DEPTH * NATT + 8
        N_ATT = N0 + 32

        ADA_TURNS = [[24] + [2] * FC + [7] * 4, [24] + [2] * FC + [7] * 4]

        ex = ctx.enter_context(nc.Block())

        def counter(eng, chain):
            n = {}

            def seq(ins, signal=chain, value=None):
                if value is None:
                    n[signal] = n.get(signal, 0) + 1
                    ins.then_inc(sem(signal), 1)
                    eng.wait_ge(sem(signal), n[signal])
                else:
                    ins.then_inc(signal, 1)
                    eng.wait_ge(signal, value)
            return seq

        @ex.sync
        def _(sp):
            sp.dma_start(crow[:, 0], io["c_rows"][:, 0]).then_inc(sem("c_in"), 16)
            sp.dma_start(params[:, :], io["params"]).then_inc(sem("params_in"), 16)
            ada_n = [0]

            def load_ada(k):
                for _ in range(min(k, 4 * ADA - ada_n[0])):
                    n = ada_n[0]
                    if n >= 16 + ADA_RING:
                        sp.wait_ge(sem("ada_used"), n - ADA_RING + 1)
                    elif n >= 16:
                        sp.wait_ge(sem("ada_used"), 16)
                    arrived = sem(f"ada_first{n // 2}") if n < 16 else sem(f"ada_in{n % ADA_RING}")
                    sp.dma_start(ada_slot(n), io["ada"][n // ADA, n % ADA]).then_inc(arrived, 16)
                    ada_n[0] += 1

            def load_unit(src, u):
                if u >= RING:
                    sp.wait_ge(sem("units_used"), u - RING + 1)
                sp.dma_start(ring[:, u % RING].rearrange("p c n -> p (c n)"), src)\
                    .then_inc(sem(f"unit_in{u % RING}"), 16)

            load_ada(16)
            sp.dma_start(xT[:, :, :], io["xT_in"]).then_inc(sem("x_in"), 16)
            sp.dma_start(consts[:, :], io["consts"]).then_inc(sem("consts_in"), 16)
            for l in range(DEPTH):
                turns = iter(ADA_TURNS[l][1:])
                for k in range(U_LAYER):
                    load_unit(io["stream_first"][l * U_LAYER + k], l * U_LAYER + k)
                    if l == 0 and k == 3:
                        sp.dma_start(mixc, io["mixer_consts"]).then_inc(sem("mixc_in"), 16)
                    if l == 0 and k == 4:
                        sp.dma_start(crow[:, 1], io["c_rows"][:, 1]).then_inc(sem("c2_in"), 16)
                    if k == U_IN + 5:
                        load_ada(ADA_TURNS[l][0])
                    at = k - (U_IN + U_OUT)
                    if at >= 6 and at % 2 == 0 and at < U_UP + 6:
                        load_ada(next(turns))
                    elif at >= U_UP + 10 and (at - U_UP) % 5 == 1:
                        load_ada(next(turns))
                for n in turns:
                    load_ada(n)

            def load_experts(p):
                for side, src in enumerate((io["peer_u"], io["peer_v"])):
                    base = B_PEER[p] + side * NK
                    groups = src[p].rearrange("(g k) p n -> g k p n", k=RING)
                    with sp.Fori(0, NG) as g:
                        for k in range(RING):
                            sp.wait_ge(sem("units_used"), g * RING + (base + k - RING + 1))
                            sp.dma_start(ring[:, (base + k) % RING].rearrange("p (o c) n -> p o (c n)", o=1),
                                         groups[bass.ds(g, 1), k].rearrange("o p n -> p o n"))\
                                .then_inc(sem(f"unit_in{(base + k) % RING}"), 16)

            sp.dma_start(keysb[:, :], io["small"][:, 2 * P:4 * P]).then_inc(sem("keys_in"), 16)
            sp.dma_start(w2bd[:, :, :].rearrange("p a m -> p (a m)"), io["small"][:, 0:2 * P]).then_inc(sem("w2_in"), 16)
            for k in range(U_FOX + U_PQ):
                load_unit(io["stream_fox"][k], B_FOX + k)
            load_experts(0)
            for k in range(U_NSA + U_PQ):
                load_unit(io["stream_nsa"][k], B_NSA + k)
                if k == 0:
                    sp.wait_ge(sem("sums_y"), 1)
                    sp.dma_start(relc, io["rel"]).then_inc(sem("rel_in"), 16)
                    sp.dma_start(keysb[:, :], io["small"][:, 4 * P:6 * P]).then_inc(sem("keys_in"), 16)
            load_experts(1)
            sp.wait_ge(sem("x_ready"), 8)
            sp.dma_start(out, xT[:, :, :]).then_inc(sem("out_written"), 16)
            sp.wait_ge(sem("out_written"), 16)

        @ex.tensor
        def _(pe):
            state = {"unit": -1, "pending": False}

            def mm(o, lhsT, rhs, start=True, stop=True, signal=None, **kw):
                ins = nc.tensor.matmul(o, lhsT, rhs, start=start, stop=stop, **kw)
                if signal is not None:
                    ins.then_inc(signal, 1)
                elif state["pending"]:
                    ins.then_inc(sem("units_used"), 1)
                    state["pending"] = False

            def next_unit():
                if state["unit"] >= 0:
                    state["pending"] = True
                state["unit"] += 1
                u = state["unit"]
                pe.wait_ge(sem(f"unit_in{u % RING}"), 16 * (u // RING + 1))
                return ring[:, u % RING]

            def open_job(*j):
                if job[j] >= 4:
                    pe.wait_ge(freed(*j)[0], freed(*j)[1] - 1)
                return bank_of(*j)

            def norm_stat(o):
                pe.wait_ge(sem("sq_ready"), o + 1)
                b = open_job("norm", o, 0)
                for c in range(DC):
                    mm(b[:, 0:T], ones, sq[:, c], c == 0, c == DC - 1, filled("norm", o, 0)[0] if c == DC - 1 else None)

            def tile_T(b, k, src, signal, first=False, h0=0):
                w = next_unit()
                for c in range(DC):
                    if first:
                        pe.wait_ge(sem("h_ready"), h0 + c + 1)
                    mm(b[:, k * T:(k + 1) * T], w[:, c], src[:, c], c == 0, c == DC - 1,
                       signal if c == DC - 1 else None)

            def tile_nat(b, k, signal):
                w = next_unit()
                for t in range(TT):
                    for c in range(DC):
                        last = t == TT - 1 and c == DC - 1
                        mm(b[:, k * T + t * P:k * T + (t + 1) * P], hT[:, c, t * P:(t + 1) * P], w[:, c],
                           c == 0, c == DC - 1, signal if last else None)

            def stat(name, l, n, ready, value, src=sq):
                pe.wait_ge(sem(ready), value)
                for i in range(n):
                    b = open_job(name, l, i)
                    mm(b[:, :], blk, src[:, 2 * i:2 * i + 2], signal=filled(name, l, i)[0])

            def level(l, k):
                g = l * 9 + k
                if g >= 2:
                    pe.wait_ge(sem("lev_freed"), g - 1)
                if l > 0 and k < 2:
                    pe.wait_ge(sem("pt_ready"), l * NATT)
                if k < 8:
                    pe.wait_ge(sem("keys_decayed"), l * 8 + k + 1)
                    pe.wait_ge(sem("queries_decayed"), l * 8 + k + 1)
                kk = ek[:, k % 2] if k < 8 else fk
                qq = eq[:, k % 2] if k < 8 else qB
                out_ = lev[g % 2][:, :].rearrange("p (h t q) -> p h t q", h=4, t=TT)
                for h in range(4):
                    for t in range(TT):
                        s = 1 - t if k == 0 else t
                        mm(out_[:, h, t], kk[:, h, s * P:(s + 1) * P], qq[:, h, t * P:(t + 1) * P],
                           signal=sem("lev_filled") if h == 3 and t == 1 else None)

            def attention(name, us, u0):
                n, jobs = len(us), 0
                for step in range(n + 3):
                    if step < n:
                        u, un = u0 + step, us[step]
                        nk = keys_of(un)
                        if u >= 2:
                            pe.wait_ge(sem("scores_read"), u - 1)
                        for hh in range(2):
                            f = un.forget is not None
                            mm(S(u)[:, hh, 0:nk], un.q, un.kz[:, hh, 0:nk], stop=not f,
                               signal=sem("scores_filled") if hh and not f else None)
                            if f:
                                mm(S(u)[:, hh, 0:nk], sel8[:, un.forget[hh]], cum[:, 0:nk], start=False,
                                   signal=sem("scores_filled") if hh else None)
                    if 0 <= step - 2 < n:
                        u, un = u0 + step - 2, us[step - 2]
                        nc_ = keys_of(un) // P
                        pe.wait_ge(sem("diag_ready"), u + 1)
                        if u >= 2:
                            pe.wait_ge(sem("pt_ready"), u - 1)
                        for hh in range(2):
                            for c in range(nc_):
                                mm(PTb(u)[:, hh, c], pr[:, u % 3, hh, c * P:(c + 1) * P], dg[:, u % 3, hh],
                                   signal=sem("pt_filled") if hh and c == nc_ - 1 else None)
                    if 0 <= step - 3 < n:
                        u, un = u0 + step - 3, us[step - 3]
                        nc_ = keys_of(un) // P
                        pe.wait_ge(sem("pt_ready"), u + 1)
                        if un.first:
                            j = (*name, jobs)
                            jobs += 1
                            ob = open_job(*j)
                        if un.pre is not None:
                            mm(ob[:, 0:P], un.pre[0], un.pre[1], True, False)
                        for hh in range(2):
                            for c in range(nc_):
                                end = hh and c == nc_ - 1
                                mm(ob[:, 0:P], un.v[:, c, hh], pt[:, u % 2, hh, c],
                                   un.first and un.pre is None and hh + c == 0, bool(end) and un.last,
                                   None if not end else filled(*j)[0] if un.last else sem("pv_mid"))

            pe.wait_ge(sem("consts_in"), 16)
            for l in range(DEPTH):
                norm_stat(2 * l)
                for k in range(4):
                    b = open_job("in", l, k)
                    tile_T(b, 0, hT, None, first=k == 0, h0=16 * l)
                    tile_T(b, 1, hT, filled("in", l, k)[0])
                for k in range(4, 11):
                    b = open_job("in", l, k)
                    if k in (8, 9):
                        tile_nat(b, 0, None)
                        tile_nat(b, 1, filled("in", l, k)[0])
                    else:
                        tile_T(b, 0, hT, None)
                        tile_T(b, 1, hT, filled("in", l, k)[0])
                    level(l, k - 4)
                stat("statA", l, 2, "sqA", l + 1)
                level(l, 7)
                level(l, 8)
                pe.wait_ge(sem("normA"), l + 1)
                for i in range(2):
                    b = open_job("rot", l, i)
                    mm(b[:, :], rot, rawA[:, 2 * i:2 * i + 2], signal=filled("rot", l, i)[0])
                stat("statC", l, 2, "sqC", l + 1)
                pe.wait_ge(sem("lev_freed"), 9 * (l + 1))
                pe.wait_ge(sem("qkA"), l + 1)
                pe.wait_ge(sem("qkC"), l + 1)
                pe.wait_ge(sem("vz_ready"), l + 1)
                attention(("att", l), units_of(l), l * NATT)
                b = open_job("ob", l, 0)
                for cc in range(2):
                    for t in range(TT):
                        for i, (h, s, at) in enumerate([(2 * cc + k, t if dd else 1 - t, ATd if dd else ATo)
                                                        for k in range(2) for dd in range(2)]):
                            mm(b[:, cc * T + t * P:cc * T + (t + 1) * P], vB[:, s, h], at[:, h, t], i == 0, i == 3,
                               filled("ob", l, 0)[0] if cc and t and i == 3 else None)
                stat("statB", l, 1, "sqB", l + 1)
                pe.wait_ge(sem("mixB"), l + 1)
                pe.wait_ge(*freed("att", l, NATT - 1))
                pe.wait_ge(*freed("att", l, NATT - 2))
                for k in range(4):
                    b = open_job("out", l, k)
                    tile_T(b, 0, mixT, None)
                    tile_T(b, 1, mixT, filled("out", l, k)[0])
                norm_stat(2 * l + 1)
                for k in range(FC):
                    b = open_job("up", l, k)
                    tile_T(b, 0, hT, None, first=k == 0, h0=16 * l + 8)
                    tile_T(b, 1, hT, filled("up", l, k)[0])
                w = None
                for k in range(4):
                    b = open_job("down", l, k)
                    for j in range(2):
                        for c in range(FC):
                            at = (2 * k + j) * FC + c
                            if at % 8 == 0:
                                w = next_unit()
                            if k == 0 and j == 0:
                                pe.wait_ge(sem("z_ready"), l * FC + c + 1)
                            mm(b[:, j * T:(j + 1) * T], w[:, at % 8], zT[:, c], c == 0, c == FC - 1,
                               filled("down", l, k)[0] if j and c == FC - 1 else None)

            def scores_of_keys(p):
                pe.wait_ge(sem("keys_in"), 16 * (p + 1))
                for k in range(4):
                    b = open_job("pq", p, k)
                    tile_T(b, 0, hT, None, first=k == 0, h0=8 * (5 + 2 * p))
                    tile_T(b, 1, hT, filled("pq", p, k)[0])
                pe.wait_ge(*freed("pq", p, 3))
                for k in range(8):
                    b = open_job("ps", p, k)
                    if k < 4:
                        pe.wait_ge(*freed("pq", p, k))
                    for j in range(2):
                        h = 2 * (k % 4) + j
                        mm(b[:, j * T:(j + 1) * T], qP[:, h, (k // 4) * P:(k // 4 + 1) * P], keysb[:, :],
                           signal=filled("ps", p, k)[0] if j else None)

            def experts(p):
                base = B_PEER[p]
                for k in range(4):
                    pe.wait_ge(*freed("ps", p, 4 + k))

                def gates_of(half, g, k, bank):
                    q = (2 * p + half) * (T // 4) + k
                    g8 = (g - (NG // 2 if half == 0 else 0)) * RING
                    pe.wait_ge(sem("hot_rows"), g8 + (q + 1))
                    pe.wait_ge(sem("hot_cols"), g8 + (q + 1))
                    pe.wait_ge(sem("gates_used"), g8 + (q + 1))
                    for t in range(4):
                        ins = nc.tensor.matmul(bank[:, t * HALF:(t + 1) * HALF], hot_r[:, k % 2, t * P:(t + 1) * P],
                                               hot_c[:, k % 2, t * HALF:(t + 1) * HALF], start=True, stop=True)
                    ins.then_inc(sem("gates_filled"), 1)

                def inputs(g0, g1, gates):
                    with pe.Fori(g0, g1) as g:
                        for k in range(RING):
                            u = base + k
                            if gates:
                                gates_of(0, g, k, lev[k % 2])
                            pe.wait_ge(sem(f"unit_in{u % RING}"), g * 16 + 16 * (u // RING + 1))
                            if k % 2 == 0:
                                pe.wait_ge(sem("act_freed"), g * 4 + (p * 4 * NG + k // 2 + 1))
                            for c in range(DC):
                                ins = nc.tensor.matmul(banks[k // 2][:, (k % 2) * T:(k % 2 + 1) * T],
                                                       ring[:, u % RING, c], hT[:, c], start=c == 0, stop=c == DC - 1)
                                if c == 0:
                                    ins.then_inc(sem("units_used"), 1)
                                if c == DC - 1 and k % 2:
                                    ins.then_inc(sem("act_filled"), 1)

                inputs(0, NG // 2, False)
                for t in range(TT):
                    pe.wait_ge(sem("chosen"), p * TT + t + 1)
                    for o in range(3):
                        mm_(lev[t][:, o * P:(o + 1) * P], chosen[:, t, o].rearrange("p h r -> p (h r)"), ident,
                            sem("chosen_filled") if o == 2 else None)
                pe.wait_ge(sem("chosen_T"), (p + 1) * TT)
                inputs(NG // 2, NG, True)
                pe.wait_ge(sem("gates_used"), (2 * p + 1) * (T // 4) + 2)
                pe.wait_ge(sem("act_freed"), (p + 1) * 4 * NG + 4)
                for b in range(4):
                    nc.tensor.matmul(lev[b // 2][:, (b % 2) * 512:(b % 2 + 1) * 512], zero[:, :], consts[:, 0:512],
                                     start=True, stop=True)
                base2 = B_PEER[p] + NK

                def outputs(g0, g1, gates):
                    with pe.Fori(g0, g1) as g:
                        for k in range(RING):
                            u = base2 + k
                            if gates:
                                gates_of(1, g, k, banks[k % 2])
                            pe.wait_ge(sem(f"unit_in{u % RING}"), g * 16 + 16 * (u // RING + 1))
                            for c in range(DC):
                                ins = nc.tensor.matmul(lev[c // 4][:, (c % 4) * T:(c % 4 + 1) * T], ring[:, u % RING, c],
                                                       acts_g[:, bass.ds(g, 1), k], start=False, stop=True,
                                                       skip_group_check=True)
                                if c == 0:
                                    ins.then_inc(sem("units_used"), 1)

                outputs(0, NG // 2, True)
                pe.wait_ge(sem("gates_used"), (2 * p + 2) * (T // 4) + 2)
                outputs(NG // 2, NG, False)
                nc.tensor.matmul(lev[1][:, 512:1024], zero[:, :], consts[:, 0:512], start=False, stop=True,
                                 skip_group_check=True).then_inc(sem("sums_y"), 1)
                state["unit"] += 2 * NK
                state["pending"] = False

            def mm_(o, lhsT, rhs, signal=None):
                ins = nc.tensor.matmul(o, lhsT, rhs, start=True, stop=True)
                if signal is not None:
                    ins.then_inc(signal, 1)

            norm_stat(4)
            for k in range(13):
                b = open_job("fin", k)
                if k in (10, 11):
                    tile_nat(b, 0, None)
                    tile_nat(b, 1, filled("fin", k)[0])
                elif k == 12:
                    tile_T(b, 0, hT, filled("fin", k)[0])
                else:
                    tile_T(b, 0, hT, None, first=k == 0, h0=32)
                    tile_T(b, 1, hT, filled("fin", k)[0])
            pe.wait_ge(sem("sqF"), 1)
            for i in range(4):
                b = open_job("statF", i)
                mm(b[:, :], blk, sq[:, 2 * i:2 * i + 2], signal=filled("statF", i)[0])
            pe.wait_ge(sem("qkF"), 1)
            pe.wait_ge(sem("vF_ready"), 1)
            attention(("attF",), fox_units(), F0)
            pe.wait_ge(*freed("attF", 6))
            pe.wait_ge(*freed("attF", 7))
            pe.wait_ge(sem("conv_out"), 1)
            for k in range(4):
                b = open_job("foxout", k)
                tile_T(b, 0, mixT, None)
                tile_T(b, 1, mixT, filled("foxout", k)[0])
            norm_stat(5)
            scores_of_keys(0)
            experts(0)
            norm_stat(6)
            pe.wait_ge(sem("rel_in"), 16)
            relt = relc[:, 2 * T:2 * T + NSA_H]
            for k in range(T):
                if k % 32 == 0:
                    b = open_job("relb", k // 32)
                s = P - k + T - 1
                mm_(b[:, (k % 32) * NSA_H:(k % 32 + 1) * NSA_H], relc[:, s:s + P], relt,
                    filled("relb", k // 32)[0] if k % 32 == 31 else None)
            b = open_job("relb", 8)
            for t in range(TT):
                for n in range(N_CMP):
                    s = P * t - CMP_STRIDE * n - (CMP_LEN - 1) + T - 1
                    i = t * N_CMP + n
                    mm_(b[:, i * NSA_H:(i + 1) * NSA_H], relc[:, s:s + P], relt,
                        filled("relb", 8)[0] if i == 2 * N_CMP - 1 else None)
            for k in range(11):
                b = open_job("nin", k)
                if k in (8, 9):
                    tile_nat(b, 0, None)
                    tile_nat(b, 1, filled("nin", k)[0])
                elif k == 10:
                    tile_nat(b, 0, filled("nin", k)[0])
                else:
                    tile_T(b, 0, hT, None, first=k == 0, h0=48)
                    tile_T(b, 1, hT, filled("nin", k)[0])
            for kv in range(2):
                bm, bp = open_job("cmp", 2 * kv), open_job("cmp", 2 * kv + 1)
                pe.wait_ge(*freed("nin", kv))
                for l in range(CMP_LEN):
                    if l % 8 == 0:
                        w = next_unit()
                    first, last = l == 0, l == CMP_LEN - 1
                    mm(bm[:, 0:2 * N_CMP], w[:, l % 8],
                       kvc[:, kv, :, l:l + CMP_STRIDE * (N_CMP - 1) + 1:CMP_STRIDE], first, last,
                       filled("cmp", 2 * kv)[0] if last else None)
                    mm(bp[:, 0:1], w[:, l % 8], col("pos", None, kv * CMP_LEN + l), first, last,
                       filled("cmp", 2 * kv + 1)[0] if last else None)
            pe.wait_ge(sem("w2_in"), 16)
            pe.wait_ge(sem("hid_ready"), 1)
            b = open_job("kc", 0)
            mm(b[:, 0:2 * N_CMP], w2bd[:, 0], hid[:, 0], signal=filled("kc", 0)[0])
            pe.wait_ge(sem("hidrep_ready"), 1)
            for c in range(2):
                b = open_job("vc", c)
                mm(b[:, 0:P], hidrep[:, c].rearrange("p h n -> p (h n)"), w2bd[:, 1], signal=filled("vc", c)[0])
            for i in range(6):
                b = open_job("statN", i)
                if i == 0:
                    pe.wait_ge(sem("sqN"), 1)
                if i == 4:
                    pe.wait_ge(sem("sqN"), 2)
                src = sq[:, 2 * i:2 * i + 2] if i < 4 else sq[:, 2 * (i - 4):2 * (i - 4) + 2]
                mm(b[:, :], blk, src, signal=filled("statN", i)[0])
            pe.wait_ge(sem("kcsq_ready"), 1)
            b = open_job("statK", 0)
            mm(b[:, 0:2 * N_CMP], blk, kcsq, signal=filled("statK", 0)[0])
            pe.wait_ge(sem("kzc_ready"), 1)
            pe.wait_ge(sem("q_ready"), 1)
            for t in range(TT):
                b = open_job("cs", t)
                for c in range(8):
                    for hh in range(2):
                        i = 2 * c + hh
                        mm(b[:, i * 16:i * 16 + N_CMP], rawQ[:, c, t * P:(t + 1) * P], kzc[:, hh, c // 4],
                           signal=filled("cs", t)[0] if i == 15 else None)
            b = open_job("ct", 0)
            for t in range(TT):
                pe.wait_ge(sem("pcs_ready"), t + 1)
                for c in range(2):
                    mm(b[:, (2 * t + c) * P:(2 * t + c + 1) * P], pcs[:, t, 8 * c:8 * c + 8].rearrange("p h n -> p (h n)"),
                       ident, signal=filled("ct", 0)[0] if t and c else None)
            pe.wait_ge(*freed("ct", 0))
            pe.wait_ge(sem("kN_ready"), 1)
            pe.wait_ge(sem("vN_ready"), 1)
            pe.wait_ge(sem("Vc_ready"), 1)
            attention(("attN",), nsa_units(), N0)
            for k in range(4):
                pe.wait_ge(*freed("attN", 12 + k))
            for k in range(4):
                b = open_job("nsaout", k)
                tile_T(b, 0, mixT, None)
                tile_T(b, 1, mixT, filled("nsaout", k)[0])
            norm_stat(7)
            scores_of_keys(1)
            experts(1)

        @ex.scalar
        def _(act):
            seq = counter(act, "act_chain")
            A = nc.scalar.activation

            def wait(*sv):
                act.wait_ge(*sv)

            def norm(o):
                if o:
                    wait(sem("x_ready"), o)
                A(sq, xT[:, :, :], ACT.Square).then_inc(sem("sq_ready"), 1)
                wait(*filled("norm", o, 0))
                A(std[:, :], bank_of("norm", o, 0)[:, 0:T], ACT.Sqrt, bias=epsc[:, :], scale=1.0 / D)\
                    .then_inc(freed("norm", o, 0)[0], 1)
                l, w = o // 2, o % 2
                for c in range(DC):
                    wait(sem("h_scaled"), 8 * o + c + 1)
                    A(hT[:, c], hT[:, c], ACT.Identity, bias=mod[:, l, 3 * w, c:c + 1]).then_inc(sem("h_ready"), 1)

            def drain(dst, *j):
                wait(*filled(*j))
                A(dst, bank_of(*j)[:, :], ACT.Copy).then_inc(freed(*j)[0], 1)

            def roots(dst, name, l, n):
                for i in range(n):
                    wait(*filled(name, l, i))
                    A(dst[:, 2 * i:2 * i + 2], bank_of(name, l, i)[:, :].rearrange("p (a t) -> p a t", a=2), ACT.Sqrt,
                      bias=epsc[:, :], scale=1.0 / HD).then_inc(freed(name, l, i)[0], 1)

            def decay(l, k):
                m = P >> k
                wait(sem("diffs"), l * 8 + k + 1)
                g = l * 9 + k
                if k >= 2:
                    wait(sem("lev_filled"), g - 1)
                d = dl[:, k % 2].rearrange("p h (n s m) -> p (h n) s m", s=2, m=m)
                for dst, j in ((eq, 0), (ek, 4)):
                    e = dst[:, k % 2].rearrange("p h (n s m) -> p (h n) s m", s=2, m=m)
                    for s in range(2):
                        c = j + 2 * s
                        A(e[:, :, s], d[:, :, s], ACT.Exp, bias=lvl[:, c + 1:c + 2], scale=lvl[:, c:c + 1])\
                            .then_inc(sem("decays"), 1)

            def attention(name, us, u0):
                n, jobs = len(us), 0
                ends = []
                mids = 0
                for un in us:
                    if un.last:
                        ends.append(filled(*name, jobs))
                        jobs += 1
                    else:
                        mids += 1
                        ends.append((sem("pv_mid"), mids))
                for step in range(n + 2):
                    if step < n:
                        u, nk = u0 + step, keys_of(us[step])
                        wait(sem("max_ready"), u + 1)
                        if u >= 3:
                            wait(sem("pt_filled"), u - 2)
                        for hh in range(2):
                            A(pr[:, u % 3, hh, 0:nk], sc[:, u % 2, hh, 0:nk], ACT.Exp, bias=nmax[:, u % 4, hh:hh + 1],
                              accum_out=sums[:, u % 4, hh:hh + 1]).then_inc(sem("exp_ready"), 1)
                    if 0 <= step - 2 < n:
                        u = u0 + step - 2
                        nc_ = keys_of(us[step - 2]) // P
                        wait(sem("pt_filled"), u + 1)
                        if step - 2 >= 2:
                            wait(*ends[step - 4])
                        A(pt[:, u % 2, :, 0:nc_], PTb(u)[:, :, 0:nc_], ACT.Copy).then_inc(sem("pt_ready"), 1)

            def experts(p):
                for k in range(4):
                    wait(*filled("pq", p, k))
                    A(qP[:, 2 * k:2 * k + 2], bank_of("pq", p, k)[:, :].rearrange("p (a t) -> p a t", a=2), ACT.Copy)\
                        .then_inc(freed("pq", p, k)[0], 1)
                for k in range(8):
                    wait(*filled("ps", p, k))
                    A(sP[:, k // 4, 2 * (k % 4):2 * (k % 4) + 2], bank_of("ps", p, k)[:, :]
                      .rearrange("p (h s k) -> p h s k", h=2, s=2), ACT.Copy).then_inc(freed("ps", p, k)[0], 1)
                if p == 0:
                    act.sem_inc(sem("act_freed"), 4)

                def gelu(g0, g1):
                    with act.Fori(g0, g1) as g:
                        for k in range(4):
                            act.wait_ge(sem("act_filled"), g * 4 + (p * 4 * NG + k + 1))
                            A(acts_g[:, bass.ds(g, 1), 2 * k:2 * k + 2], banks[k][:, :]
                              .rearrange("p (o a t) -> p o a t", o=1, a=2), ACT.Gelu_apprx_tanh).then_inc(sem("act_freed"), 1)

                gelu(0, NG // 2 - 2)
                for t in range(TT):
                    wait(sem("gate_diff"), p * TT + t + 1)
                    A(chosen[:, t, 2], chosen[:, t, 2], ACT.Exp).then_inc(sem("gate_exp"), 1)
                gelu(NG // 2 - 2, NG // 2)
                for t in range(TT):
                    wait(sem("chosen_filled"), p * TT + t + 1)
                    A(chT[:, :, t * P:(t + 1) * P], lev[t][:, 0:3 * P].rearrange("p (o q) -> p o q", o=3), ACT.Copy)\
                        .then_inc(sem("chosen_T"), 1)
                gelu(NG // 2, NG)

            wait(sem("eps_set"), 1)
            wait(sem("c_in"), 16)
            seq(A(crow[:, 0], crow[:, 0], ACT.Silu), "c_silu")
            wait(sem("params_in"), 16)
            wait(sem("lb_max"), 1)
            A(lbt[:, 2:4], lbt[:, 2:4], ACT.Exp).then_inc(sem("lb_exp"), 1)
            wait(sem("x_in"), 16)
            for l in range(DEPTH):
                norm(2 * l)
                if l == 0:
                    wait(sem("c2_in"), 16)
                    A(crow[:, 1], crow[:, 1], ACT.Silu).then_inc(sem("c_silu"), 1)
                for k in range(2):
                    wait(sem("fx_ready"), 2 * l + k + 1)
                    A(fk[:, 2 * k:2 * k + 2], fk[:, 2 * k:2 * k + 2], ACT.Exp).then_inc(sem("f_exp"), 1)
                wait(sem("f_ready"), l + 1)
                A(C2, fk, ACT.Ln).then_inc(sem("logf"), 1)
                drain(qB[:, 0:2], "in", l, 2)
                drain(qB[:, 2:4], "in", l, 3)
                for k in range(4, 11):
                    if k < 6:
                        drain(rawA[:, 2 * (k - 4):2 * (k - 4) + 2], "in", l, k)
                    elif k < 8:
                        drain(rawC[:, 2 * (k - 6):2 * (k - 6) + 2], "in", l, k)
                    elif k == 8:
                        wait(*filled("in", l, k))
                        b = bank_of("in", l, k)
                        for i, v in enumerate((vA, vC)):
                            for hh in range(2):
                                src = b[:, i * T:(i + 1) * T].rearrange("p (t c) -> p t c", t=TT)[:, :, hh * HD:(hh + 1) * HD]
                                ins = A(v[:, :, hh, hh * HD:(hh + 1) * HD], src, ACT.Copy)
                                last = i == 1 and hh == 1
                                ins.then_inc(freed("in", l, k)[0] if last else sem("act_free"), 1)
                    elif k == 9:
                        wait(*filled("in", l, k))
                        b = bank_of("in", l, k)
                        for i in range(2):
                            for hh in range(2):
                                src = b[:, i * T:(i + 1) * T].rearrange("p (t c) -> p t c", t=TT)[:, :, hh * HD:(hh + 1) * HD]
                                ins = A(vB[:, :, 2 * i + hh, hh * HD:(hh + 1) * HD], src, ACT.Copy)
                                last = i == 1 and hh == 1
                                ins.then_inc(freed("in", l, k)[0] if last else sem("vz_ready") if i == 1 and hh == 0 else sem("act_free"), 1)
                    else:
                        wait(*filled("in", l, k))
                        A(gB, bank_of("in", l, k)[:, :].rearrange("p (a t) -> p a t", a=2), ACT.Copy)\
                            .then_inc(freed("in", l, k)[0], 1)
                    decay(l, k - 4)
                decay(l, 7)
                wait(*freed("in", l, 5))
                A(sq[:, 0:4], rawA, ACT.Square).then_inc(sem("sqA"), 1)
                roots(rsq, "statA", l, 2)
                wait(*filled("statA", l, 1))
                A(sq[:, 4:8], rawC, ACT.Square).then_inc(sem("sqC0"), 1)
                wait(sem("normA"), l + 1)
                wait(sem("sqC0"), l + 1)
                A(sq[:, 0:4], sq[:, 4:8], ACT.Copy).then_inc(sem("sqC"), 1)
                roots(rsq, "statC", l, 2)
                attention(("att", l), units_of(l), l * NATT)
                wait(*filled("ob", l, 0))
                ob = bank_of("ob", l, 0)[:, :].rearrange("p (a t) -> p a t", a=2)
                seq(A(oB, ob, ACT.Copy))
                A(sq[:, 0:2], ob, ACT.Square).then_inc(sem("sqB"), 1)
                wait(sem("sqB"), l + 1)
                act.sem_inc(freed("ob", l, 0)[0], 1)
                wait(*filled("statB", l, 0))
                A(rsq[:, 0:2], bank_of("statB", l, 0)[:, :].rearrange("p (a t) -> p a t", a=2), ACT.Sqrt,
                  bias=epsc[:, :], scale=1.0 / HD).then_inc(freed("statB", l, 0)[0], 1)
                A(gB, gB, ACT.Silu).then_inc(sem("gate_silu"), 1)
                norm(2 * l + 1)
                for k in range(FC):
                    wait(*filled("up", l, k))
                    g = l * FC + k
                    if g >= 4:
                        wait(sem("z_ready"), g - 3)
                    for hh in range(2):
                        n = hh * FC + k
                        A(cv[:, g % 4, hh], bank_of("up", l, k)[:, hh * T:(hh + 1) * T], ACT.Identity,
                          bias=col("cb", l, n), scale=col("cw1", l, n)).then_inc(sem("conv_mid"), 1)
                    if k:
                        gp = g - 1
                        wait(*freed("up", l, k - 1))
                        if gp >= 2:
                            wait(sem("z_ready"), gp - 1)
                        A(sa[:, gp % 2], cv[:, gp % 4, 0], ACT.Silu).then_inc(sem("a_silu"), 1)
                gp = l * FC + FC - 1
                wait(*freed("up", l, FC - 1))
                wait(sem("z_ready"), gp - 1)
                A(sa[:, gp % 2], cv[:, gp % 4, 0], ACT.Silu).then_inc(sem("a_silu"), 1)

            def pair(b):
                return b[:, :].rearrange("p (a t) -> p a t", a=2)

            def values(v, b, i, signal):
                for hh in range(2):
                    src = b[:, i * T:(i + 1) * T].rearrange("p (t c) -> p t c", t=TT)[:, :, hh * HD:(hh + 1) * HD]
                    A(v[:, :, hh, hh * HD:(hh + 1) * HD], src, ACT.Copy).then_inc(signal if hh and signal else sem("act_free"), 1)

            norm(4)
            for k in range(12):
                wait(*filled("fin", k))
                b = bank_of("fin", k)
                if k < 2:
                    A(cbT[:, 2 * k:2 * k + 2], pair(b), ACT.Copy).then_inc(freed("fin", k)[0], 1)
                elif k < 4:
                    A(prod[:, 2 * k - 4:2 * k - 2], pair(b), ACT.Copy).then_inc(freed("fin", k)[0], 1)
                elif k < 6:
                    pass
                elif k < 10:
                    A(rawF[:, 2 * k - 12:2 * k - 10], pair(b), ACT.Copy).then_inc(freed("fin", k)[0], 1)
                else:
                    wait(sem("vF_zero"), 1)
                    values(vF[:, 2 * k - 20], b, 0, None)
                    values(vF[:, 2 * k - 19], b, 1, freed("fin", k)[0])
            wait(*freed("fin", 9))
            A(sq, rawF, ACT.Square).then_inc(sem("sqF"), 1)
            wait(sem("f_abs"), 1)
            A(lsig, lsig, ACT.Exp, scale=-1.0).then_inc(sem("f_e"), 1)
            wait(sem("f_e1"), 1)
            A(lsig, lsig, ACT.Ln).then_inc(sem("f_ln"), 1)
            for i in range(4):
                wait(*filled("statF", i))
                A(rsF[:, 2 * i:2 * i + 2], pair(bank_of("statF", i)), ACT.Sqrt, bias=epsc[:, :], scale=1.0 / HD)\
                    .then_inc(freed("statF", i)[0], 1)
            attention(("attF",), fox_units(), F0)
            norm(5)
            experts(0)
            norm(6)
            for k in range(8):
                wait(*filled("relb", k))
                A(bias[:, :, 32 * k:32 * k + 32], bank_of("relb", k)[:, :].rearrange("p (k h) -> p h k", h=NSA_H), ACT.Copy)\
                    .then_inc(freed("relb", k)[0], 1)
            wait(*filled("relb", 8))
            wait(sem("nsa_zero"), 1)
            for t in range(TT):
                A(cbias[:, t, :, 0:N_CMP], bank_of("relb", 8)[:, t * 240:(t + 1) * 240]
                  .rearrange("p (n h) -> p h n", h=NSA_H), ACT.Copy).then_inc(freed("relb", 8)[0] if t else sem("act_free"), 1)
            for k in range(10):
                wait(*filled("nin", k))
                b = bank_of("nin", k)
                if k < 2:
                    A(kvc[:, k], pair(b), ACT.Copy).then_inc(freed("nin", k)[0], 1)
                elif k < 6:
                    A(rawQ[:, 2 * k - 4:2 * k - 2], pair(b), ACT.Copy).then_inc(freed("nin", k)[0], 1)
                elif k < 8:
                    A(rawK[:, k - 6], pair(b), ACT.Copy).then_inc(freed("nin", k)[0], 1)
                else:
                    values(vN[:, k - 8, 0], b, 0, None)
                    values(vN[:, k - 8, 1], b, 1, freed("nin", k)[0])
            wait(sem("g_pre"), 1)
            A(gates, gates, ACT.Exp).then_inc(sem("g_exp"), 1)
            for kv in range(2):
                wait(*filled("cmp", 2 * kv + 1))
                seq(A(posb[:, kv:kv + 1], bank_of("cmp", 2 * kv + 1)[:, 0:1], ACT.Copy), *freed("cmp", 2 * kv + 1))
                wait(*filled("cmp", 2 * kv))
                seq(A(hid[:, kv], bank_of("cmp", 2 * kv)[:, 0:2 * N_CMP].rearrange("p (c n) -> p c n", c=2),
                      ACT.Gelu_apprx_tanh, bias=posb[:, kv:kv + 1]), *freed("cmp", 2 * kv))
                if kv == 0:
                    act.sem_inc(sem("hid_ready"), 1)
            for c in range(2):
                A(hidrep[:, c, :, 0:N_CMP], hid[:, 1, c].unsqueeze(1).broadcast_to([P, 8, N_CMP]), ACT.Copy)\
                    .then_inc(sem("hidrep_ready") if c else sem("act_free"), 1)
            wait(*filled("kc", 0))
            kb = bank_of("kc", 0)[:, 0:2 * N_CMP].rearrange("p (c n) -> p c n", c=2)
            A(kcn, kb, ACT.Copy).then_inc(sem("kcn_ready"), 1)
            seq(A(kcsq, kb, ACT.Square), *freed("kc", 0))
            act.sem_inc(sem("kcsq_ready"), 1)
            for c in range(2):
                wait(*filled("vc", c))
                A(vrep[:, c], bank_of("vc", c)[:, 0:P], ACT.Copy).then_inc(freed("vc", c)[0], 1)
            A(sq, rawQ, ACT.Square).then_inc(sem("sqN"), 1)
            for i in range(6):
                if i < 4:
                    wait(*filled("statN", i))
                    A(rsQ[:, 2 * i:2 * i + 2], pair(bank_of("statN", i)), ACT.Sqrt, bias=epsc[:, :], scale=1.0 / HD)\
                        .then_inc(freed("statN", i)[0], 1)
                    if i == 3:
                        A(sq[:, 0:4], rawK.rearrange("p a c t -> p (a c) t"), ACT.Square).then_inc(sem("sqN"), 1)
                        wait(sem("q_ready"), 1)
                else:
                    wait(*filled("statN", i))
                    A(rsQ[:, 2 * (i - 4):2 * (i - 4) + 2], pair(bank_of("statN", i)), ACT.Sqrt, bias=epsc[:, :], scale=1.0 / HD)\
                        .then_inc(freed("statN", i)[0], 1)
            wait(*filled("statK", 0))
            A(kcrs, bank_of("statK", 0)[:, 0:2 * N_CMP].rearrange("p (c n) -> p c n", c=2), ACT.Sqrt, bias=epsc[:, :],
              scale=1.0 / HD).then_inc(freed("statK", 0)[0], 1)
            for t in range(TT):
                wait(sem("cs_diff"), t + 1)
                A(pcs[:, t, :, 0:N_CMP], pcs[:, t, :, 0:N_CMP], ACT.Exp).then_inc(sem("cs_exp"), 1)
            wait(*filled("ct", 0))
            A(pcT, bank_of("ct", 0)[:, :].rearrange("p (t c q) -> p t c q", t=TT, c=2), ACT.Copy).then_inc(freed("ct", 0)[0], 1)
            attention(("attN",), nsa_units(), N0)
            norm(7)
            experts(1)

        @ex.gpsimd
        def _(pool):
            G = nc.gpsimd
            seq = counter(pool, "pool_chain")

            def attention(name, us, u0):
                for k in range(len(us)):
                    u = u0 + k
                    pool.wait_ge(sem("rinv_ready"), u + 1)
                    if u >= 3:
                        pool.wait_ge(sem("pt_filled"), u - 2)
                    for hh in range(2):
                        ins = G.tensor_scalar(dg[:, u % 3, hh], ident, rinv[:, u % 4, hh:hh + 1], None, ALU.mult)
                        ins.then_inc(sem("diag_ready") if hh else sem("diag_half"), 1)

            pool.wait_ge(sem("consts_in"), 16)
            for l in range(DEPTH):
                for k in range(8):
                    pool.wait_ge(sem("decays"), (l * 8 + k + 1) * 4)
                    pool.wait_ge(sem("keys_ready"), l + 1)
                    G.tensor_tensor(ek[:, k % 2], ek[:, k % 2], fk, ALU.mult).then_inc(sem("keys_decayed"), 1)
                attention(("att", l), units_of(l), l * NATT)
                for k in range(FC):
                    g = l * FC + k
                    pool.wait_ge(sem("a_silu"), g + 1)
                    G.tensor_tensor(zT[:, k], sa[:, g % 2], cv[:, g % 4, 1], ALU.mult).then_inc(sem("z_ready"), 1)
            attention(("attF",), fox_units(), F0)

            def hot_columns(p):
                pool.wait_ge(sem("chosen_T"), (p + 1) * TT)
                cols = chT[:, 1].rearrange("p (g k t) -> p g k t", k=2, t=4)
                for half in range(2):
                    q = (2 * p + half) * (T // 4)
                    with pool.Fori(0, T // 8) as g:
                        for k in range(2):
                            pool.wait_ge(sem("gates_used"), g * 2 + (q + k + 1))
                            pool.sem_inc(sem("pool_step"), 1)
                            G.tensor_copy(turn[:, k:k + 1], cols[:, bass.ds(g, 1), k]).then_inc(sem("turn"), 1)
                            pool.wait_ge(sem("turn"), g * 2 + (q + k + 1))
                            pool.sem_inc(sem("pool_step"), 1)
                            for t in range(4):
                                ins = G.tensor_scalar(hot_c[:, k, t * HALF:(t + 1) * HALF], iota[:, half * HALF:(half + 1) * HALF],
                                                      turn[:, k, t:t + 1], None, ALU.is_equal)
                            ins.then_inc(sem("hot_cols"), 1)

            hot_columns(0)
            attention(("attN",), nsa_units(), N0)
            hot_columns(1)

        @ex.vector
        def _(dve):
            V = nc.vector
            seq = counter(dve, "dve_chain")

            def wait(*sv):
                dve.wait_ge(*sv)

            ada_n = [0]

            def do_ada(k):
                for _ in range(min(k, 4 * ADA - ada_n[0])):
                    n = ada_n[0]
                    if n < 16:
                        wait(sem(f"ada_first{n // 2}"), 32)
                    else:
                        wait(sem(f"ada_in{n % ADA_RING}"), 16 * ((n - 16) // ADA_RING + 1))
                    if n == DEPTH * ADA:
                        wait(sem("c_silu"), 2)
                    l, ch = n // ADA, n % ADA
                    seq(V.tensor_tensor_reduce(out=junk, in0=ada_slot(n), in1=crow[:, l // DEPTH], scale=1.0,
                                               scalar=0.0, op0=ALU.mult, op1=ALU.add,
                                               accum_out=mod[:, l, ch // DC, ch % DC:ch % DC + 1]), "ada_used")
                    ada_n[0] += 1

            def mods(l, a, b):
                m = mod[:, l, a:b]
                seq(V.tensor_tensor(m, m, col("bada", l, a * DC, (b - a) * DC).rearrange("p (a c) -> p a c", c=DC), ALU.add))
                for w in range(2):
                    if a <= 3 * w + 1 < b:
                        g = col(f"ng{w + 1}", l, 0, DC) if l < DEPTH else col("png", None, ((l - DEPTH) * 2 + w) * DC, DC)
                        seq(V.tensor_scalar(gscale[:, l, w], mod[:, l, 3 * w + 1], 1.0, None, ALU.add))
                        seq(V.tensor_tensor(gscale[:, l, w], gscale[:, l, w], g, ALU.mult))

            def norm(o):
                l, w = o // 2, o % 2
                wait(*freed("norm", o, 0))
                seq(V.reciprocal(rstd[:, :], std[:, :]))
                for c in range(DC):
                    V.scalar_tensor_tensor(out=hT[:, c], in0=xT[:, c], scalar=gscale[:, l, w, c:c + 1], in1=rstd[:, :],
                                           op0=ALU.mult, op1=ALU.mult).then_inc(sem("h_scaled"), 1)

            def residual(name, l, which, beside=(0, 0, 0, 0)):
                for k in range(4):
                    do_ada(beside[k])
                    wait(*filled(*name, k))
                    b = bank_of(*name, k)
                    for j in range(2):
                        n = 2 * k + j
                        ins = V.scalar_tensor_tensor(out=xT[:, n], in0=b[:, j * T:(j + 1) * T],
                                                     scalar=mod[:, l, which, n:n + 1], in1=xT[:, n],
                                                     op0=ALU.mult, op1=ALU.add)
                        if j == 1:
                            ins.then_inc(freed(*name, k)[0], 1)
                        else:
                            ins.then_inc(sem("x_half"), 1)
                wait(*freed(*name, 3))
                dve.sem_inc(sem("x_ready"), 1)

            def attention(name, us, u0, beside=0):
                n, jobs = len(us), 0
                for step in range(n + 4):
                    if step < n:
                        u = u0 + step
                        b, nk = us[step].bias, keys_of(us[step])
                        do_ada(beside)
                        wait(sem("scores_filled"), u + 1)
                        if u >= 2:
                            wait(sem("exp_ready"), 2 * (u - 1))
                        if b is None:
                            seq(V.tensor_scalar(sc[:, u % 2], S(u), SCALE, None, ALU.mult), "scores_read")
                        else:
                            seq(V.scalar_tensor_tensor(out=sc[:, u % 2, :, 0:nk], in0=S(u)[:, :, 0:nk], scalar=SCALE, in1=b,
                                                       op0=ALU.mult, op1=ALU.add), "scores_read")
                        seq(V.tensor_reduce(nmax[:, u % 4], sc[:, u % 2, :, 0:nk], AX.X, ALU.max))
                        seq(V.tensor_scalar(nmax[:, u % 4], nmax[:, u % 4], -1.0, None, ALU.mult), "max_ready")
                    if 0 <= step - 1 < n:
                        u = u0 + step - 1
                        wait(sem("exp_ready"), 2 * (u + 1))
                        if u >= 4:
                            wait(sem("diag_ready"), u - 3)
                        gate = us[step - 1].gate
                        if gate is None:
                            seq(V.reciprocal(rinv[:, u % 4], sums[:, u % 4]), "rinv_ready")
                        else:
                            seq(V.reciprocal(rinv[:, u % 4], sums[:, u % 4]))
                            seq(V.tensor_tensor(rinv[:, u % 4], rinv[:, u % 4], gate, ALU.mult), "rinv_ready")
                    if 0 <= step - 4 < n and us[step - 4].last:
                        j = (*name, jobs)
                        jobs += 1
                        wait(*filled(*j))
                        seq(V.tensor_copy(us[step - 4].out, bank_of(*j)[:, 0:P]), *freed(*j))

            V.memset(epsc[:, :], EPS).then_inc(sem("eps_set"), 1)
            wait(sem("params_in"), 16)
            lb0, lb1 = col("lb", 0, 0, 4), col("lb", 1, 0, 4)
            seq(V.tensor_tensor(lbt[:, 0], lb0, lb1, ALU.max))
            seq(V.tensor_tensor(lbt[:, 2], lb0, lbt[:, 0], ALU.subtract))
            seq(V.tensor_tensor(lbt[:, 3], lb1, lbt[:, 0], ALU.subtract), "lb_max")
            wait(sem("lb_exp"), 1)
            seq(V.tensor_tensor(lbt[:, 0], lbt[:, 2], lbt[:, 3], ALU.add))
            seq(V.reciprocal(lbt[:, 0], lbt[:, 0]))
            for k in (2, 3):
                seq(V.tensor_tensor(lbt[:, k], lbt[:, k], lbt[:, 0], ALU.mult))
            seq(V.tensor_tensor(lbt[:, 1], lbt[:, 2], lbt[:, 3], ALU.add))
            seq(V.tensor_tensor(lbt[:, 4], lbt[:, 2], lbt[:, 2], ALU.subtract))
            seq(V.tensor_tensor(lbt[:, 5], lbt[:, 1], lbt[:, 2], ALU.subtract))
            seq(V.tensor_scalar(lbt[:, 6:8], lbt[:, 4:6], -1.0, 1.0, ALU.mult, ALU.add))
            wait(sem("c_silu"), 1)
            do_ada(16)
            mods(0, 0, 2)
            for l in range(DEPTH):
                norm(2 * l)
                for z in (vA, vC, vB, Cx[:, :, 0:1]):
                    seq(V.memset(z, 0.0))
                if l == 0:
                    wait(sem("consts_in"), 16)
                for k in range(2):
                    wait(*filled("in", l, k))
                    b = bank_of("in", l, k)[:, :].rearrange("p (a t) -> p a t", a=2)
                    seq(V.tensor_scalar(fk[:, 2 * k:2 * k + 2], b, -80.0, -1.0, ALU.max, ALU.mult), freed("in", l, k)[0],
                        freed("in", l, k)[1])
                    dve.sem_inc(sem("fx_ready"), 1)
                wait(sem("f_exp"), 2 * (l + 1))
                seq(V.tensor_scalar(fk, fk, 1.0, None, ALU.add))
                seq(V.reciprocal(fk, fk))
                for h in range(4):
                    seq(V.tensor_scalar(fk[:, h], fk[:, h], lbt[:, 6 + l, h:h + 1], lbt[:, 4 + l, h:h + 1], ALU.mult, ALU.add))
                seq(V.tensor_scalar(fk, fk, F_MIN, None, ALU.max), "f_ready")
                wait(sem("logf"), l + 1)
                seq(V.tensor_scalar(fk, fk, -1.0, 1.0, ALU.mult, ALU.add), "keys_ready")
                seq(V.memset(rsq[:, 0], 0.0))
                for h in range(4):
                    seq(V.tensor_tensor_scan(Cx[:, h, 1:T + 1], C2[:, h], rsq[:, 0], 0.0, ALU.add, ALU.add))
                seq(V.tensor_copy(C2[0:HD], Cx[0:HD, :, 1:T + 1]))
                seq(V.tensor_copy(C2[HD:P], Cx[HD:P, :, 0:T]))
                wait(sem("mixc_in"), 16)
                for step in range(11):
                    if step < 8:
                        k, m = step, P >> step
                        d = dl[:, k % 2].rearrange("p h (n m) -> p h n m", m=2 * m)
                        c2 = C2.rearrange("p h (n m) -> p h n m", m=2 * m)
                        ref = Cx[:, :, m:T + 1:2 * m].unsqueeze(3).broadcast_to([P, 4, T // (2 * m), 2 * m])
                        seq(V.tensor_tensor(d, c2, ref, ALU.subtract), "diffs")
                    if 0 <= step - 1 < 8:
                        k = step - 1
                        if k == 0:
                            wait(*freed("in", l, 3))
                        wait(sem("decays"), (l * 8 + k + 1) * 4)
                        seq(V.tensor_tensor(eq[:, k % 2], eq[:, k % 2], qB, ALU.mult), "queries_decayed")
                    if step >= 2:
                        k = step - 2
                        g = l * 9 + k
                        wait(sem("lev_filled"), g + 1)
                        src = lev[g % 2][:, :].rearrange("p (h t q) -> p h t q", h=4, t=TT)
                        if k < 2:
                            seq(V.tensor_copy((ATo, ATd)[k], src), "lev_freed")
                        else:
                            mk = lmask[:, k - 2].unsqueeze(1).broadcast_to([P, 8, P])
                            seq(V.tensor_tensor(junk.rearrange("p (a q) -> p a q", a=8),
                                                src.rearrange("p h t q -> p (h t) q"), mk, ALU.mult), "lev_freed")
                            seq(V.tensor_tensor(ATd.rearrange("p h t q -> p (h t q)"), ATd.rearrange("p h t q -> p (h t q)"), junk, ALU.add))
                wait(*freed("statA", l, 1))
                seq(V.reciprocal(rsq, rsq))
                seq(V.scalar_tensor_tensor(out=rawA[:, 0:3], in0=rawA[:, 0:3], scalar=col("aq", l), in1=rsq[:, 0:3],
                                           op0=ALU.mult, op1=ALU.mult))
                seq(V.scalar_tensor_tensor(out=rawA[:, 3], in0=rawA[:, 3], scalar=col("ak", l), in1=rsq[:, 3],
                                           op0=ALU.mult, op1=ALU.mult), "normA")
                bc = lambda v: v.unsqueeze(1).broadcast_to([P, 2, T])
                for i in range(2):
                    wait(*filled("rot", l, i))
                    x2, r2 = rawA[:, 2 * i:2 * i + 2], ropec[:, 2 * i:2 * i + 2]
                    seq(V.tensor_tensor(r2, bank_of("rot", l, i)[:, :].rearrange("p (a t) -> p a t", a=2), bc(sin), ALU.mult),
                        freed("rot", l, i)[0], freed("rot", l, i)[1])
                    seq(V.tensor_tensor(x2, x2, bc(cos), ALU.mult))
                    seq(V.tensor_tensor(x2, x2, r2, ALU.add))
                seq(V.tensor_scalar(kzA[:, 0], rawA[:, 3], half[:, 0:1], None, ALU.mult))
                seq(V.tensor_scalar(kzA[:, 1], rawA[:, 3], half[:, 1:2], None, ALU.mult), "qkA")
                wait(*freed("statC", l, 1))
                seq(V.reciprocal(rsq, rsq))
                seq(V.scalar_tensor_tensor(out=rawC[:, 0:3], in0=rawC[:, 0:3], scalar=col("cq", l), in1=rsq[:, 0:3],
                                           op0=ALU.mult, op1=ALU.mult))
                seq(V.scalar_tensor_tensor(out=kzC[:, 0], in0=rawC[:, 3], scalar=col("ck_lo", l), in1=rsq[:, 3],
                                           op0=ALU.mult, op1=ALU.mult))
                seq(V.scalar_tensor_tensor(out=kzC[:, 1], in0=rawC[:, 3], scalar=col("ck_hi", l), in1=rsq[:, 3],
                                           op0=ALU.mult, op1=ALU.mult), "qkC")
                attention(("att", l), units_of(l), l * NATT, ADA_TURNS[l][0] // NATT)
                wait(*freed("statB", l, 0))
                seq(V.reciprocal(rsq[:, 0:2], rsq[:, 0:2]))
                seq(V.scalar_tensor_tensor(out=oB, in0=oB, scalar=col("bo", l), in1=rsq[:, 0:2], op0=ALU.mult, op1=ALU.mult))
                wait(sem("gate_silu"), l + 1)
                seq(V.tensor_tensor(mixT[:, 3:5], oB, gB, ALU.mult), "mixB")
                if l == 0:
                    mods(0, 2, 5)
                residual(("out", l), l, 2)
                norm(2 * l + 1)
                for k in range(FC):
                    g = l * FC + k
                    wait(sem("conv_mid"), 2 * (g + 1))
                    b = bank_of("up", l, k)
                    for hh in range(2):
                        n = hh * FC + k
                        u = b[:, hh * T:(hh + 1) * T]
                        c = cv[:, g % 4, hh]
                        seq(V.scalar_tensor_tensor(out=c[:, 1:T], in0=u[:, 0:T - 1], scalar=col("cw0", l, n), in1=c[:, 1:T],
                                                   op0=ALU.mult, op1=ALU.add))
                        fin = V.scalar_tensor_tensor(out=c[:, 0:T - 1], in0=u[:, 1:T], scalar=col("cw2", l, n),
                                                     in1=c[:, 0:T - 1], op0=ALU.mult, op1=ALU.add)
                        if hh:
                            seq(fin, freed("up", l, k)[0], freed("up", l, k)[1])
                        else:
                            seq(fin)
                    do_ada(ADA_TURNS[l][1 + k])
                if l == 0:
                    mods(0, 5, 6)
                residual(("down", l), l, 5, ADA_TURNS[l][1 + FC:])
                if l == 0:
                    mods(1, 0, 6)
            mods(2, 0, 6)
            mods(3, 0, 6)

            def k_norms(dst, raw, rs, lo, hi):
                for hh, g in enumerate((lo, hi)):
                    last = V.scalar_tensor_tensor(out=dst[:, :, hh], in0=raw, scalar=g, in1=rs, op0=ALU.mult, op1=ALU.mult)
                    if hh == 0:
                        seq(last)
                return last

            def choose(p):
                for t in range(TT):
                    wait(*freed("ps", p, 4 * t + 3))
                    for h in range(PH):
                        for s in range(2):
                            x, v, i = sP[:, t, h, s], sv[:, t, h, s], siu[:, t, h, s]
                            seq(V.max(v[:, 0:8], x))
                            seq(V.max_index(i[:, 0:8], v[:, 0:8], x))
                            seq(V.match_replace(wk[:, 0:NK], v[:, 0:8], x, -3e38))
                            seq(V.max(v[:, 8:16], wk[:, 0:NK]))
                            seq(V.max_index(i[:, 8:16], v[:, 8:16], wk[:, 0:NK]))
                    flat = lambda a: a.rearrange("p h s r -> p (h s r)")
                    seq(V.tensor_copy(flat(sif[:, t]), flat(siu[:, t])))
                    seq(V.tensor_tensor(cand, sv[:, t, :, 0].unsqueeze(3).broadcast_to([P, PH, TOPK, TOPK]),
                                        sv[:, t, :, 1].unsqueeze(2).broadcast_to([P, PH, TOPK, TOPK]), ALU.add))
                    for h in range(PH):
                        x, v, i = cand[:, h].rearrange("p a b -> p (a b)"), cvv[:, t, h], ciu[:, t, h]
                        seq(V.max(v[:, 0:8], x))
                        seq(V.max_index(i[:, 0:8], v[:, 0:8], x))
                        seq(V.match_replace(wk, v[:, 0:8], x, -3e38))
                        seq(V.max(v[:, 8:16], wk))
                        seq(V.max_index(i[:, 8:16], v[:, 8:16], wk))
                    g = chosen[:, t, 2]
                    seq(V.tensor_tensor(g, cvv[:, t], cvv[:, t, :, 0:1].broadcast_to([P, PH, TOPK]), ALU.subtract), "gate_diff")
                    seq(V.tensor_scalar(cau[:, t, 0], ciu[:, t], 4, None, ALU.logical_shift_right))
                    seq(V.tensor_scalar(cau[:, t, 1], ciu[:, t], 15, None, ALU.bitwise_and))
                    seq(V.tensor_copy(caf[:, t], cau[:, t]))
                    for s in range(2):
                        at = caf[:, t, s].rearrange("p h r -> p (h r)").unsqueeze(2).broadcast_to([P, PH * TOPK, TOPK])
                        io16 = iota[:, 0:TOPK].unsqueeze(1).broadcast_to([P, PH * TOPK, TOPK])
                        seq(V.tensor_tensor(hit, io16, at, ALU.is_equal))
                        h4 = hit.rearrange("p (h r) a -> p h r a", h=PH)
                        seq(V.tensor_tensor(h4, h4, sif[:, t, :, s].unsqueeze(2).broadcast_to([P, PH, TOPK, TOPK]), ALU.mult))
                        seq(V.tensor_reduce(chosen[:, t, s].rearrange("p h r -> p (h r)"), hit, AX.X, ALU.add))
                for t in range(TT):
                    g = chosen[:, t, 2]
                    wait(sem("gate_exp"), p * TT + t + 1)
                    seq(V.tensor_reduce(gsum[:, t], g, AX.X, ALU.add))
                    seq(V.reciprocal(gsum[:, t], gsum[:, t]))
                    seq(V.tensor_tensor(g, g, gsum[:, t].unsqueeze(2).broadcast_to([P, PH, TOPK]), ALU.mult), "chosen")

            def experts(p):
                choose(p)
                wait(sem("chosen_T"), (p + 1) * TT)
                if p == 0:
                    dve.sem_inc(sem("gates_used"), 2)

                def rows(k, of):
                    for t in range(4):
                        ins = V.tensor_scalar(hot_r[:, k, t * P:(t + 1) * P], iota, of(0, t), of(2, t), ALU.is_equal, ALU.mult)
                    ins.then_inc(sem("hot_rows"), 1)

                odd = chT[:, :, 0:T - 8].rearrange("p o (g k t) -> p o g k t", k=2, t=4)
                even = chT[:, :, 8:T].rearrange("p o (g k t) -> p o g k t", k=2, t=4)
                for half in range(2):
                    q = (2 * p + half) * (T // 4)
                    bank = (lev, banks)[half]
                    by_token = arena[:, half * HALF * T:(half + 1) * HALF * T]\
                        .rearrange("p (j g k t) -> p g k t j", j=HALF, k=2, t=4)

                    def weigh(k, dst):
                        V.tensor_tensor(dst, bank[k][:, 0:4 * HALF].rearrange("p (o t j) -> p o t j", o=1, t=4), dst, ALU.mult)\
                            .then_inc(sem("gates_used"), 1)

                    wait(sem("act_freed"), 4 + p * 4 * NG + (half + 1) * 2 * NG)
                    rows(0, lambda o, t: chT[:, o, t:t + 1])
                    with dve.Fori(0, T // 8 - 1) as g:
                        dve.wait_ge(sem("gates_used"), g * 2 + (q + 2))
                        rows(1, lambda o, t: odd[:, o, bass.ds(g, 1), 1, t])
                        dve.wait_ge(sem("gates_filled"), g * 2 + (q + 1))
                        weigh(0, by_token[:, bass.ds(g, 1), 0])
                        dve.wait_ge(sem("gates_used"), g * 2 + (q + 3))
                        rows(0, lambda o, t: even[:, o, bass.ds(g, 1), 0, t])
                        dve.wait_ge(sem("gates_filled"), g * 2 + (q + 2))
                        weigh(1, by_token[:, bass.ds(g, 1), 1])
                    rows(1, lambda o, t: chT[:, o, T - 4 + t:T - 3 + t])
                    dve.wait_ge(sem("gates_filled"), q + T // 4 - 1)
                    weigh(0, by_token[:, T // 8 - 1:T // 8, 0])
                    dve.wait_ge(sem("gates_filled"), q + T // 4)
                    weigh(1, by_token[:, T // 8 - 1:T // 8, 1])
                wait(sem("sums_y"), p + 1)
                for c in range(DC):
                    seq(V.scalar_tensor_tensor(out=xT[:, c], in0=lev[c // 4][:, (c % 4) * T:(c % 4 + 1) * T],
                                               scalar=mod[:, 2 + p, 5, c:c + 1], in1=xT[:, c], op0=ALU.mult, op1=ALU.add))
                dve.sem_inc(sem("x_ready"), 1)

            norm(4)
            seq(V.memset(fzero, 0.0))
            seq(V.memset(cum, 0.0))
            seq(V.memset(zero[:, :], 0.0))
            seq(V.memset(vF, 0.0), "vF_zero")
            pair = lambda b: b[:, :].rearrange("p (a t) -> p a t", a=2)
            for i in range(2):
                wait(*freed("fin", 2 + i))
                wait(*filled("fin", 4 + i))
                x = prod[:, 2 * i:2 * i + 2]
                seq(V.tensor_tensor(x, x, pair(bank_of("fin", 4 + i)), ALU.mult), *freed("fin", 4 + i))
            fcw = lambda j, c: col("fcw", None, 4 * j + c)
            for c in range(4):
                x, y = prod[:, c], cmid[:, c]
                seq(V.tensor_scalar(y, x, fcw(2, c), None, ALU.mult))
                seq(V.scalar_tensor_tensor(out=y[:, 1:T], in0=x[:, 0:T - 1], scalar=fcw(1, c), in1=y[:, 1:T], op0=ALU.mult, op1=ALU.add))
                seq(V.scalar_tensor_tensor(out=y[:, 2:T], in0=x[:, 0:T - 2], scalar=fcw(0, c), in1=y[:, 2:T], op0=ALU.mult, op1=ALU.add))
            wait(*freed("fin", 1))
            seq(V.tensor_tensor(mixT[:, 0:4], cmid, cbT, ALU.mult), "conv_out")
            wait(*filled("fin", 12))
            R8 = slice(0, 8)
            seq(V.tensor_scalar(cum[R8], bank_of("fin", 12)[R8, 0:T], col("bf")[R8], None, ALU.add), *freed("fin", 12))
            seq(V.scalar_tensor_tensor(out=lsig, in0=cum, scalar=-1.0, in1=cum, op0=ALU.mult, op1=ALU.max), "f_abs")
            wait(sem("f_e"), 1)
            seq(V.tensor_scalar(lsig, lsig, 1.0, None, ALU.add), "f_e1")
            wait(sem("f_ln"), 1)
            seq(V.tensor_scalar(cum[R8], cum[R8], 0.0, None, ALU.min))
            seq(V.tensor_tensor(lsig[R8], cum[R8], lsig[R8], ALU.subtract))
            seq(V.tensor_tensor_scan(cum[R8], lsig[R8], fzero[R8], 0.0, ALU.add, ALU.add))
            wait(*freed("statF", 3))
            seq(V.reciprocal(rsF, rsF))
            seq(V.scalar_tensor_tensor(out=rawF[:, 0:4], in0=rawF[:, 0:4], scalar=col("fq"), in1=rsF[:, 0:4], op0=ALU.mult, op1=ALU.mult))
            seq(k_norms(kzF, rawF[:, 4:8], rsF[:, 4:8], col("fk_lo"), col("fk_hi")), "qkF")
            wait(*freed("fin", 11))
            dve.sem_inc(sem("vF_ready"), 1)
            attention(("attF",), fox_units(), F0)
            residual(("foxout",), 2, 2)
            norm(5)
            experts(0)
            seq(V.memset(vN, 0.0))
            seq(V.memset(pcs, 0.0))
            seq(V.memset(hidrep, 0.0), "nsa_zero")
            norm(6)
            wait(*filled("nin", 10))
            for t in range(TT):
                seq(V.tensor_tensor(gates[:, t], bank_of("nin", 10)[:, t * P:t * P + 48], col("bgate", None, 0, 48), ALU.add),
                    *(freed("nin", 10) if t else ()))
            seq(V.tensor_scalar(gates, gates, -80.0, -1.0, ALU.max, ALU.mult), "g_pre")
            wait(sem("g_exp"), 1)
            seq(V.tensor_scalar(gates, gates, 1.0, None, ALU.add))
            seq(V.reciprocal(gates, gates))
            wait(*freed("nin", 9))
            dve.sem_inc(sem("vN_ready"), 1)
            for c in range(2):
                wait(*freed("vc", c))
                for i in range(8):
                    hh = i % 2
                    seq(V.tensor_scalar(Vc[:, c, i // 2, hh * HD:(hh + 1) * HD], vrep[:, c, hh * HD:(hh + 1) * HD],
                                        const("vmask")[:, i:i + 1], None, ALU.mult))
            dve.sem_inc(sem("Vc_ready"), 1)
            wait(*freed("statN", 3))
            seq(V.reciprocal(rsQ, rsQ))
            seq(V.scalar_tensor_tensor(out=rawQ, in0=rawQ, scalar=col("nq"), in1=rsQ, op0=ALU.mult, op1=ALU.mult), "q_ready")
            wait(*freed("statN", 5))
            seq(V.reciprocal(rsQ[:, 0:4], rsQ[:, 0:4]))
            seq(k_norms(kzN[:, 0], rawK[:, 0], rsQ[:, 0:2], col("nks_lo"), col("nks_hi")))
            seq(k_norms(kzN[:, 1], rawK[:, 1], rsQ[:, 2:4], col("nkw_lo"), col("nkw_hi")), "kN_ready")
            wait(*freed("statK", 0))
            seq(V.reciprocal(kcrs, kcrs))
            for hh, g in enumerate(("nkc_lo", "nkc_hi")):
                seq(V.scalar_tensor_tensor(out=kzc[:, hh], in0=kcn, scalar=col(g), in1=kcrs, op0=ALU.mult, op1=ALU.mult))
            dve.sem_inc(sem("kzc_ready"), 1)
            wait(*freed("relb", 8))
            pc = lambda t: pcs[:, t, :, 0:N_CMP]
            hb = lambda a, t: a[:, t].unsqueeze(2).broadcast_to([P, NSA_H, N_CMP])
            for t in range(TT):
                wait(*filled("cs", t))
                sco = bank_of("cs", t)[:, 0:T].rearrange("p (h n) -> p h n", h=NSA_H)[:, :, 0:N_CMP]
                seq(V.scalar_tensor_tensor(out=pc(t), in0=sco, scalar=SCALE, in1=cbias[:, t, :, 0:N_CMP],
                                           op0=ALU.mult, op1=ALU.add), *freed("cs", t))
                seq(V.tensor_reduce(cmx[:, t], pc(t), AX.X, ALU.max))
                seq(V.tensor_tensor(pc(t), pc(t), hb(cmx, t), ALU.subtract), "cs_diff")
            for t in range(TT):
                wait(sem("cs_exp"), t + 1)
                seq(V.tensor_reduce(csm[:, t], pc(t), AX.X, ALU.add))
                seq(V.reciprocal(csm[:, t], csm[:, t]))
                gt = gates[:, t].rearrange("p (g h j b) -> p g j h b", g=2, h=2, b=3)[:, :, :, :, 0]
                s4 = csm[:, t].rearrange("p (g j h) -> p g j h", g=2, h=2)
                seq(V.tensor_tensor(s4, s4, gt, ALU.mult))
                seq(V.tensor_tensor(pc(t), pc(t), hb(csm, t), ALU.mult))
                seq(V.tensor_tensor(pc(t), pc(t), cmask[:, t].unsqueeze(1).broadcast_to([P, NSA_H, N_CMP]), ALU.mult), "pcs_ready")
            attention(("attN",), nsa_units(), N0)
            residual(("nsaout",), 3, 2)
            norm(7)
            experts(1)



INPUTS = ("xT_in", "params", "consts", "mixer_consts", "rel", "c_rows", "ada", "small",
          "stream_first", "stream_fox", "stream_nsa", "peer_u", "peer_v")


def kernel(**inputs):
    from concourse import bacc
    from concourse.bass_utils import run_bass_kernel_spmd

    arrays = lay_out(inputs)
    nc = bacc.Bacc("TRN2", target_bir_lowering=False, num_devices=1)
    io = {n: nc.dram_tensor("in_" + n, arrays[n].shape, F32, kind="ExternalInput").ap() for n in INPUTS}
    out = nc.dram_tensor("out", (P, DC, T), F32, kind="ExternalOutput").ap()
    build(nc, io, out)
    r = run_bass_kernel_spmd(nc, [{"in_" + n: np.ascontiguousarray(arrays[n]) for n in INPUTS}], core_ids=[0])
    return np.ascontiguousarray(r.results[0]["out"].transpose(2, 1, 0)).reshape(1, T, D)
```

```python
import math
from contextlib import ExitStack

import numpy as np

import concourse.bass as bass
from concourse import mybir

F32 = mybir.dt.float32
BF16 = mybir.dt.bfloat16
U32 = mybir.dt.uint32
ALU = mybir.AluOpType
ACT = mybir.ActivationFunctionType
AX = mybir.AxisListType

P = 128
D = 1024
T = 256
HD = 64
DC = D // P
TT = T // P
DEPTH = 2
EPS = 1e-6
F_MIN = 1e-6
NEG = -1e30
FF = 2816
FC = FF // P
GRID_W = 64
SCALE = HD ** -0.5
UNIT = 1024
RING = 8
ADA_RING = 4
ADA = 6 * DC
N_CMP, CMP_LEN, CMP_STRIDE = 15, 32, 16
NSA_H, REL_BUCKETS, REL_MAX = 16, 32, 128
REL_SHIFTS = P // (REL_BUCKETS + 1)
REL_W = REL_SHIFTS * NSA_H
REL_COLS = 10 * REL_SHIFTS
REL_JOBS = -(-256 // REL_COLS)
PH, NK, TOPK = 8, 128, 16

U_IN, U_OUT, U_UP, U_DOWN = 22, DC, 2 * FC, FC
U_LAYER = U_IN + U_OUT + U_UP + U_DOWN
U_FOX = 25 + DC
U_NSA = 21 + 8 + DC
U_PQ = DC
B_FOX = DEPTH * U_LAYER
B_PEER = (B_FOX + U_FOX + U_PQ, B_FOX + U_FOX + U_PQ + 2 * NK + U_NSA + U_PQ)
B_NSA = B_PEER[0] + 2 * NK
FOX_ORDER = (6, 7, 8, 9, 12, 0, 1, 2, 3, 4, 5, 10, 11)
NSA_ORDER = (0, 1, 2, "w1", 3, 4, 5, 6, 7, 8, 10, 9)
NG = NK // RING


def columns():
    at, n = {}, 0
    for l in range(DEPTH):
        for name, k in (("ng1", DC), ("ng2", DC), ("cw0", 2 * FC), ("cw1", 2 * FC), ("cw2", 2 * FC), ("cb", 2 * FC),
                        ("aq", 1), ("ak", 1), ("cq", 1), ("ck_lo", 1), ("ck_hi", 1), ("bo", 1), ("lb", 4)):
            at[name, l] = n
            n += k
    for l in range(2 * DEPTH):
        at["bada", l] = n
        n += ADA
    for name, k in (("png", 4 * DC), ("fcw", 12), ("fq", 1), ("fk_lo", 1), ("fk_hi", 1), ("bf", 1),
                    ("nq", 1), ("nkc_lo", 1), ("nkc_hi", 1), ("nks_lo", 1), ("nks_hi", 1), ("nkw_lo", 1), ("nkw_hi", 1),
                    ("bgate", 48), ("pos", 2 * CMP_LEN)):
        at[name] = n
        n += k
    return at, n


COL, N_COL = columns()

CONST = {}
_n = 0
for _name, _k in (("ident", P), ("ones", P), ("blk", P), ("rot", P), ("cos", T), ("sin", T), ("iota", P),
                  ("half", 2), ("lvl", 8), ("sel8", 8 * P), ("cmask", 2 * N_CMP), ("vmask", 8)):
    CONST[_name] = (_n, _n + _k)
    _n += _k
N_CONST = _n
N_ALIBI, N_LM, N_CAUSAL = 6 * 384, 7 * P, 384


def constants():
    out = np.zeros((P, N_CONST), np.float32)
    put = lambda name, v: out[:, CONST[name][0]:CONST[name][1]].__setitem__(slice(None), v)
    p = np.arange(P)
    put("ident", np.eye(P))
    put("ones", 1.0)
    put("blk", (p[:, None] // HD == p[None] // HD))
    rot = np.zeros((P, P))
    for m in range(P):
        if m % 32 < 16:
            rot[m + 16, m] = -1.0
        else:
            rot[m - 16, m] = 1.0
    put("rot", rot)
    inv = np.float32(10000.0) ** (-np.arange(0, 32, 2, dtype=np.float32) / np.float32(32))
    t = np.arange(T)
    row, col = (t // GRID_W).astype(np.float32), (t % GRID_W).astype(np.float32)
    ang = np.where((p % HD < 32)[:, None], row[None], col[None]).astype(np.float32) * inv[p % 16][:, None]
    put("cos", np.cos(ang.astype(np.float32)))
    put("sin", np.sin(ang.astype(np.float32)))
    put("iota", p[None, :])
    put("half", np.stack([p < HD, p >= HD], 1))
    fwd = p < HD
    lv = np.zeros((P, 8))
    lv[:, 0], lv[:, 1] = np.where(fwd, 0, -1), np.where(fwd, NEG, 0)
    lv[:, 2], lv[:, 3] = np.where(fwd, 1, 0), np.where(fwd, 0, NEG)
    lv[:, 4], lv[:, 5] = np.where(fwd, -1, 0), np.where(fwd, 0, NEG)
    lv[:, 6], lv[:, 7] = np.where(fwd, 0, 1), np.where(fwd, NEG, 0)
    put("lvl", lv)
    sel = np.zeros((P, 8, P))
    for h in range(8):
        sel[h, h, :] = -1.0 / SCALE
    put("sel8", sel.reshape(P, -1))
    tq = p[:, None, None] + P * np.arange(TT)[None, :, None]
    ends = (np.arange(N_CMP) * CMP_STRIDE + CMP_LEN - 1)[None, None, :]
    put("cmask", (ends <= tq).reshape(P, -1))
    put("vmask", (p[:, None] // 16 == np.arange(8)[None]) & (p[:, None] % 16 < N_CMP))
    return out


def mixer_constants():
    p = np.arange(P)
    x = np.arange(384)
    d = x[None] - P - p[:, None]
    m = (np.abs(d) <= 64).astype(np.float32) + (d % 4 == 0) + (d % 16 == 0)
    slopes = (2.0 ** (-8.0 * np.arange(1, 7) / 6)).astype(np.float32)
    logm = np.log(np.maximum(m, 1))
    al = -slopes[None, :, None] * np.abs(d)[:, None, :] + logm[:, None, :]
    al = np.where(m[:, None, :] > 0, al, NEG).astype(np.float32)
    causal = np.where(d <= 0, 0.0, NEG).astype(np.float32)
    lm = [(p[:, None] // b == p[None] // b) for b in (64, 32, 16, 8, 4, 2)] + [np.eye(P)]
    return np.concatenate([al.reshape(P, -1)] + [a.astype(np.float32) for a in lm] + [causal], 1).astype(np.float32)


def bucket_strip():
    n = np.arange(2 * T) - (T - 1)
    nf = np.maximum(n, 1).astype(np.float32)
    large = 16 + (np.log(nf / 16) / math.log(REL_MAX / 16) * 16).astype(np.int32)
    b = np.where(n < 16, np.maximum(n, 0), np.minimum(large, REL_BUCKETS - 1))
    one = np.zeros((REL_BUCKETS + 1, 2 * T), np.float32)
    for k in range(REL_BUCKETS):
        one[k] = (b == k) & (n >= 0)
    one[REL_BUCKETS] = n < 0
    out = np.zeros((P, 2 * T), np.float32)
    for r in range(REL_SHIFTS):
        out[r * (REL_BUCKETS + 1):(r + 1) * (REL_BUCKETS + 1), r:] = one[:, :2 * T - r]
    return out


def tile_unit(w):
    return w.reshape(DC, P, P).transpose(1, 0, 2).reshape(P, UNIT)


def pad_cols(w):
    return np.concatenate([w, np.zeros((w.shape[0], P - w.shape[1]), w.dtype)], 1)


def heads(w, hs):
    return np.concatenate([w[:, h * HD:(h + 1) * HD] for h in hs], 1)


def lay_out(x):
    A = np.asarray
    g = {k: A(v) for k, v in x.items()}
    out = {}
    f32 = np.float32
    xT = g["x"][0].T.reshape(DC, P, T).transpose(1, 0, 2)
    out["xT_in"] = np.ascontiguousarray(xT)
    par = np.zeros((P, N_COL), f32)
    dup = lambda v: np.concatenate([v, v])
    lo = lambda v: np.concatenate([v, np.zeros_like(v)])
    hi = lambda v: np.concatenate([np.zeros_like(v), v])
    ch = lambda v: v.reshape(-1, P).T
    for l in range(DEPTH):
        def put(name, v):
            v = v if v.ndim == 2 else v[:, None]
            par[:v.shape[0], COL[name, l]:COL[name, l] + v.shape[1]] = v
        put("ng1", ch(g["norm_g"][l, 0])); put("ng2", ch(g["norm_g"][l, 1]))
        for j in range(3):
            put(f"cw{j}", ch(g["conv_w"][l, j]))
        put("cb", ch(g["conv_b"][l]))
        put("aq", dup(g["a_q_norm"][l])); put("ak", dup(g["a_k_norm"][l]))
        put("cq", dup(g["c_q_norm"][l])); put("ck_lo", lo(g["c_k_norm"][l])); put("ck_hi", hi(g["c_k_norm"][l]))
        put("bo", dup(g["b_out_norm"][l]))
        put("lb", np.concatenate([g["b_lb"][0, l].reshape(4, HD).T, g["b_lb"][1, l].reshape(4, HD).T], 0))
        put("bada", ch(g["b_ada"][l]))
    for l in range(DEPTH):
        par[:, COL["bada", DEPTH + l]:COL["bada", DEPTH + l] + ADA] = ch(g["ada_b_2"][l])
    def put(name, v):
        v = v if v.ndim == 2 else v[:, None]
        par[:v.shape[0], COL[name]:COL[name] + v.shape[1]] = v
    put("png", ch(g["norm_g_2"].reshape(-1)))
    put("fcw", np.concatenate([ch(g["even_conv_w_2"][0, j]) for j in range(3)], 1))
    put("fq", dup(g["even_q_g_2"][0])); put("fk_lo", lo(g["even_k_g_2"][0])); put("fk_hi", hi(g["even_k_g_2"][0]))
    put("bf", g["even_b_f_2"][0])
    put("nq", dup(g["odd_q_g_2"][0]))
    for i, n in enumerate(("nkc", "nks", "nkw")):
        put(n + "_lo", lo(g["odd_k_g_2"][0, i])); put(n + "_hi", hi(g["odd_k_g_2"][0, i]))
    put("bgate", np.broadcast_to(g["odd_b_gate_2"][0], (P, 48)))
    pos = g["odd_cmp_pos_2"][0]
    put("pos", np.concatenate([dup(pos[0].T), dup(pos[1].T)], 1))
    out["params"] = par
    out["consts"] = constants()
    out["mixer_consts"] = mixer_constants()
    order = [(2 * gg + hh) * 4 + j for gg in range(2) for j in range(4) for hh in range(2)]
    rel = np.zeros((P, REL_W), f32)
    for r in range(REL_SHIFTS):
        at, cols = r * (REL_BUCKETS + 1), slice(r * NSA_H, (r + 1) * NSA_H)
        rel[at:at + REL_BUCKETS, cols] = g["rel_table_2"][:, order]
        rel[at + REL_BUCKETS, cols] = NEG
    out["rel"] = np.concatenate([bucket_strip(), rel], 1)
    out["c_rows"] = np.ascontiguousarray(np.stack([np.broadcast_to(g["c"][0], (P, D)), np.broadcast_to(g["c_2"][0], (P, D))], 1))
    out["ada"] = np.stack([w.T.reshape(ADA, P, D) for w in (*g["w_ada"], *g["ada_w_2"])])

    units = []
    for l in range(DEPTH):
        w = g["w_in"][l]
        cut = np.split(w, np.cumsum([384, 128, 128, 256, 256, 256, 256, 256, 384, 128]), 1)
        aq, ak, av, bq, bff, bfb, bi, bg, cq, ck, cv = cut
        tiles = [np.concatenate([bff[:, h * HD:(h + 1) * HD], bfb[:, h * HD:(h + 1) * HD]], 1) for h in range(4)]
        tiles += [heads(bq, (h, h)) for h in range(4)]
        tiles += [heads(aq, (p, p + 3)) for p in range(3)] + [ak]
        tiles += [heads(cq, (p, p + 3)) for p in range(3)] + [ck]
        tiles += [av, cv, bi[:, :P], bi[:, P:], bg[:, :P], bg[:, P:]]
        assert len(tiles) == U_IN
        units += [tile_unit(t) for t in tiles]
        rows = g["w_out"][l].reshape(16, HD, D)
        order = [h for p in range(3) for h in (p, p + 3)] + [6, 7, 8, 9] + [10 + h for p in range(3) for h in (p, p + 3)]
        wo = rows[order].reshape(D, D)
        units += [tile_unit(wo[:, n * P:(n + 1) * P]) for n in range(DC)]
        wu = g["w_up"][l]
        for i in range(FC):
            for s in (i, FC + i):
                units.append(tile_unit(wu[:, s * P:(s + 1) * P]))
        blocks = g["w_down"][l].reshape(FC, P, DC, P).transpose(2, 0, 1, 3).reshape(FC, 8, P, P)
        units += list(blocks.transpose(0, 2, 1, 3).reshape(FC, P, UNIT))
    out["stream_first"] = np.stack(units)

    units = []
    w = g["even_w_in_2"][0]
    for k in FOX_ORDER:
        units += [tile_unit(w[:, n * P:(n + 1) * P]) for n in (2 * k, 2 * k + 1)] if k < 12 else [tile_unit(pad_cols(w[:, 3072:3080]))]
    units += [tile_unit(g["even_w_out_2"][0][:, n * P:(n + 1) * P]) for n in range(DC)]
    units += [tile_unit(g["peer_w_q_2"][0][:, n * P:(n + 1) * P]) for n in range(DC)]
    out["stream_fox"] = np.stack(units)

    units = []
    w = g["odd_w_in_2"][0]
    pairs = [((2 * gg) * 4 + j, (2 * gg + 1) * 4 + j) for gg in range(2) for j in range(4)]
    kv = w[:, 1024:1024 + 6 * 256]
    tile = lambda i, c: kv[:, i * 256 + c * P:i * 256 + (c + 1) * P]
    jobs = {k: [tile_unit(tile(k, 0)), tile_unit(tile(k, 1))] for k in (0, 1)}
    jobs |= {k: [tile_unit(heads(w[:, :1024], pr)) for pr in pairs[2 * k - 4:2 * k - 2]] for k in range(2, 6)}
    jobs |= {k: [tile_unit(tile(i, 0)), tile_unit(tile(i, 1))] for k, i in zip(range(6, 10), (2, 4, 3, 5))}
    jobs[10] = [tile_unit(pad_cols(w[:, 2560:2608]))]
    w1 = g["odd_cmp_w1_2"][0].reshape(2, CMP_LEN, HD, HD)
    bd = np.zeros((2, CMP_LEN, P, P), f32)
    bd[:, :, :HD, :HD] = w1
    bd[:, :, HD:, HD:] = w1
    jobs["w1"] = list(bd.reshape(2, 4, 8, P, P).transpose(0, 1, 3, 2, 4).reshape(8, P, UNIT))
    for k in NSA_ORDER:
        units += jobs[k]
    rows = g["odd_w_out_2"][0].reshape(16, HD, D)
    wo = rows[[h for pr in pairs for h in pr]].reshape(D, D)
    units += [tile_unit(wo[:, n * P:(n + 1) * P]) for n in range(DC)]
    units += [tile_unit(g["peer_w_q_2"][1][:, n * P:(n + 1) * P]) for n in range(DC)]
    out["stream_nsa"] = np.stack(units)

    w2 = g["odd_cmp_w2_2"][0]
    bd = np.zeros((2, P, P), f32)
    bd[:, :HD, :HD] = w2
    bd[:, HD:, HD:] = w2
    keys = np.zeros((DEPTH, P, 2, NK), f32)
    for p_ in range(2):
        keys[:, p_ * HD:(p_ + 1) * HD, p_, :] = g["peer_keys_2"][:, p_].transpose(0, 2, 1)
    out["small"] = np.ascontiguousarray(np.concatenate([bd[0], bd[1], keys[0].reshape(P, -1), keys[1].reshape(P, -1)], 1))
    u = g["peer_u_2"].reshape(DEPTH, NK, NK, DC, P)
    out["peer_u"] = np.ascontiguousarray(u.transpose(0, 2, 4, 3, 1)).reshape(DEPTH, NK, P, UNIT)
    v = g["peer_v_2"].reshape(DEPTH, NK, NK, D)
    out["peer_v"] = np.ascontiguousarray(v.transpose(0, 2, 1, 3))
    return out


def build(nc, io, out):
    ctx = ExitStack()
    with ctx:
        sb = lambda name, shape, dt=F32: ctx.enter_context(nc.sbuf_tensor(name, shape, dt))
        sems = {}

        def sem(name):
            if name not in sems:
                sems[name] = ctx.enter_context(nc.semaphore(name))
            return sems[name]

        ring = sb("ring", [P, RING, DC, P])
        xT = sb("xT", [P, DC, T])
        hT = sb("hT", [P, DC, T])
        consts = sb("consts", [P, N_CONST])
        params = sb("params", [P, N_COL])
        mod = sb("mod", [P, 2 * DEPTH, 6, DC])
        gscale = sb("gscale", [P, 2 * DEPTH, 2, DC])
        std = sb("std", [P, T])
        rstd = sb("rstd", [P, T])
        epsc = sb("epsc", [P, 1])
        tiny = sb("tiny", [P, 1])
        sums = sb("sums", [P, 4, 2])
        nmax = sb("nmax", [P, 4, 2])
        rinv = sb("rinv", [P, 4, 2])
        lbt = sb("lbt", [P, 8, 4])
        extra = sb("extra", [P, 2 * UNIT])
        arena = sb("arena", [P, 128 * T])

        top = [0]

        def place(*shape):
            n = int(np.prod(shape))
            v = arena[:, top[0]:top[0] + n]
            top[0] += n
            assert top[0] <= 128 * T, top[0]
            if len(shape) == 1:
                return v
            names = "abcde"[:len(shape)]
            return v.rearrange(f"p ({' '.join(names)}) -> p {' '.join(names)}", **dict(zip(names[1:], shape[1:])))

        const = lambda name: consts[:, CONST[name][0]:CONST[name][1]]
        ident, ones, blk, rot = const("ident"), const("ones"), const("blk"), const("rot")
        cos, sin, iota, half, lvl = const("cos"), const("sin"), const("iota"), const("half"), const("lvl")
        sel8 = const("sel8").rearrange("p (h m) -> p h m", h=8)
        cmask = const("cmask").rearrange("p (t n) -> p t n", t=TT)

        def col(name, l=None, k=0, n=1):
            at = COL[name if l is None else (name, l)] + k
            return params[:, at:at + n]

        crow = place(2, D)
        ada = place(2, D)
        junk = place(D)
        mixc = place(N_ALIBI + N_LM + N_CAUSAL)
        alibi = mixc[:, 0:N_ALIBI].rearrange("p (h x) -> p h x", h=6)
        lmask = mixc[:, N_ALIBI:N_ALIBI + N_LM].rearrange("p (l t) -> p l t", l=7)
        causal = mixc[:, N_ALIBI + N_LM:]
        common = top[0]
        mixT = place(DC, T)
        sq = place(DC, T)
        levels = top[0]
        dl = place(2, 4, T)
        eq, ek = place(2, 4, T), place(2, 4, T)
        after_levels, top[0] = top[0], levels
        sc = place(2, 2, T)
        pr = place(4, 2, T)
        dg = place(4, 2, P)
        pt = place(2, 2, 2, P)
        oB = place(2, T)
        assert top[0] <= after_levels
        top[0] = after_levels
        mixers = top[0]
        rawA, rawC = place(4, T), place(4, T)
        vA, vC = place(TT, 2, P), place(TT, 2, P)
        kzA, kzC = place(2, T), place(2, T)
        rsq = place(4, T)
        vB = place(TT, 4, P)
        fk = place(4, T)
        qB = place(4, T)
        gB = place(2, T)
        Cx = place(4, T + 1)
        C2 = place(4, T)
        ATd, ATo = place(4, TT, P), place(4, TT, P)
        ropec = sq[:, 4:8]
        first_end = top[0]
        top[0] = mixers
        zT = place(FC, T)
        cv = place(4, 2, T)
        sa = place(2, T)

        top[0] = levels
        ada_first = [place(D) for _ in range(6)]
        top[0] = mixers
        ada_first += [place(D) for _ in range(10)]
        assert len(ada_first) == 16
        late_row = hT[:, 0:4].rearrange("p c t -> p (c t)")
        late_junk = hT[:, 4:8].rearrange("p c t -> p (c t)")
        ada_slot = lambda n: ada_first[n] if n < 16 else (ada[:, n % 4] if n % 4 < 2 else extra[:, (n % 2) * D:(n % 2 + 1) * D])
        top[0] = mixers
        cbT, prod, cmid = place(4, T), place(4, T), place(4, T)
        rawF = place(8, T)
        rsF = place(8, T)
        kzF = place(4, 2, T)
        vF = place(4, TT, 2, P)
        cum, lsig, fzero = place(T), place(T), place(T)
        top[0] = mixers
        rawQ, rsQ = place(8, T), place(8, T)
        kvc = place(2, 3, T)
        rawK = place(2, 2, T)
        kzN = place(2, 2, 2, T)
        vN = place(2, 2, TT, 2, P)
        Vc = place(2, 4, P)
        top[0] = 0
        relc = place(2 * T + REL_W)
        bias = place(NSA_H, T)
        cbias = place(TT, NSA_H, 16)
        pcs = place(TT, NSA_H, 16)
        pcT = place(TT, 2, P)
        hid = place(2, 2, N_CMP)
        hidrep = place(2, 8, 16)
        posb = place(2)
        kcn, kcsq, kcrs = place(2, N_CMP), place(2, N_CMP), place(2, N_CMP)
        kzc = place(2, 2, N_CMP)
        gates = place(TT, 48)
        cmx, csm = place(TT, NSA_H), place(TT, NSA_H)
        vrep = place(2, P)
        assert top[0] <= common
        acts = arena[:, :].rearrange("p (j t) -> p j t", t=T)
        acts_g = arena[:, :].rearrange("p (g k t) -> p g k t", k=RING, t=T)
        top[0] = NK // 2 * T
        qP = place(PH, T)
        sP = place(TT, PH, 2, NK)
        wk = place(T)
        sv = place(TT, PH, 2, TOPK)
        siu = place(TT, PH, 2, TOPK).bitcast(U32)
        sif = place(TT, PH, 2, TOPK)
        cand = place(PH, TOPK, TOPK)
        cvv = place(TT, PH, TOPK)
        ciu = place(TT, PH, TOPK).bitcast(U32)
        cau = place(TT, 2, PH, TOPK).bitcast(U32)
        caf = place(TT, 2, PH, TOPK)
        hit = place(PH * TOPK, TOPK)
        chosen = place(TT, 3, PH, TOPK)
        gsum = place(TT, PH)
        chT = sb("chT", [P, 5, T])
        keysb = sb("keysb", [P, 2 * NK])
        w2bd = sb("w2bd", [P, 2, P])
        turn = sb("turn", [P, 2, 4])
        zero = sb("zero", [P, P])
        HALF = NK // 2
        PARTS = 3
        extra_b = extra[:, :].bitcast(BF16)
        hot_r = extra_b[:, 0:8 * P].rearrange("p (b t x) -> p b t x", b=2, t=4)
        hot_c = extra_b[:, 8 * P:8 * P + 8 * PARTS * HALF].rearrange("p (b t s x) -> p b t s x", b=2, t=4, s=PARTS)
        part_b = extra_b[:, 3072:3072 + T]
        gate_of = extra[:, 1664:1664 + 4 * HALF].rearrange("p (t j) -> p t j", t=4)

        lev = [ctx.enter_context(nc.psum_tensor(f"lev{i}", [P, 1024], F32)) for i in range(2)]
        four = ctx.enter_context(nc.psum_tensor("banks", [P, 2048], F32))
        banks = [four[:, 512 * i:512 * (i + 1)] for i in range(4)]
        gate_banks = [[lev[k][:, :] for k in range(2)], [four[:, 1024 * k:1024 * (k + 1)] for k in range(2)]]
        S = lambda u: lev[0][:, 512 * (u % 2):512 * (u % 2) + 512].rearrange("p (h k) -> p h k", h=2)
        PTb = lambda u: lev[1][:, 512 * (u % 2):512 * (u % 2) + 512].rearrange("p (h c q) -> p h c q", h=2, c=2)

        job = {}
        NATT = 12

        def plan(name, n, first=0):
            for i in range(first, first + n):
                job[name + (i,)] = len(job)

        for l in range(DEPTH):
            plan(("norm", 2 * l), 1)
            plan(("in", l), 7)
            plan(("statA", l), 2)
            plan(("in", l), 2, 7)
            plan(("statC", l), 2)
            plan(("rot", l), 2)
            plan(("in", l), 2, 9)
            plan(("ob", l), 1)
            plan(("statB", l), 1)
            plan(("att", l), NATT)
            plan(("out", l), 4)
            plan(("norm", 2 * l + 1), 1)
            plan(("up", l), FC)
            plan(("down", l), 4)
        plan(("norm", 4), 1)
        for k in FOX_ORDER:
            plan(("fin",), 1, k)
            if k == 0:
                plan(("statF",), 4)
        plan(("attF",), 8)
        plan(("foxout",), 4)
        plan(("norm", 5), 1)
        plan(("pq", 0), 4)
        plan(("ps", 0), 8)
        plan(("norm", 6), 1)
        plan(("relb",), REL_JOBS)
        beside = {3: [("kc", 1, 0), ("vc", 2, 0)], 4: [("statK", 1, 0)], 6: [("statN", 4, 0)], 8: [("statN", 2, 4)],
                  10: [("cs", 2, 0)], 9: [("ct", 1, 0)]}
        for k in NSA_ORDER:
            plan(("cmp",) if k == "w1" else ("nin",), 2 if k == "w1" else 1, 0 if k == "w1" else k)
            for name, n, first in beside.get(k, ()):
                plan((name,), n, first)
        plan(("attN",), 16)
        plan(("nsaout",), 4)
        plan(("norm", 7), 1)
        plan(("pq", 1), 4)
        plan(("ps", 1), 8)
        bank_of = lambda *j: banks[job[j] % 4]
        filled = lambda *j: (sem(f"filled{job[j] % 4}"), job[j] // 4 + 1)
        freed = lambda *j: (sem(f"freed{job[j] % 4}"), job[j] // 4 + 1)

        class Unit:
            def __init__(self, q, kz, v, bias, out, gate=None, forget=None, pre=None, first=True, last=True):
                self.q, self.kz, self.v, self.bias, self.out = q, kz, v, bias, out
                self.gate, self.forget, self.pre, self.first, self.last = gate, forget, pre, first, last

        window = lambda t: slice(P - P * t, P - P * t + T)

        def units_of(l):
            us = []
            for q, kz, v, al, o in ((rawA, kzA, vA, None, 0), (rawC, kzC, vC, alibi, 5)):
                for p in range(3):
                    for t in range(TT):
                        b = None if al is None else al[:, p::3, window(t)]
                        us.append(Unit(q[:, p, t * P:(t + 1) * P], kz, v, b, mixT[:, o + p, t * P:(t + 1) * P]))
            return us

        def fox_units():
            return [Unit(rawF[:, c, t * P:(t + 1) * P], kzF[:, c], vF[:, c],
                         causal[:, P - P * t:2 * P].unsqueeze(1).broadcast_to([P, 2, P * (t + 1)]),
                         mixT[:, 4 + c, t * P:(t + 1) * P], forget=(2 * c, 2 * c + 1))
                    for c in range(4) for t in range(TT)]

        def nsa_units():
            us = []
            for c in range(8):
                g2, j = c // 4, c % 4
                for t in range(TT):
                    for br in range(2):
                        at = (8 * g2 + j) * 3 + 1 + br
                        us.append(Unit(rawQ[:, c, t * P:(t + 1) * P], kzN[:, br, g2], vN[:, br, g2],
                                       bias[:, 2 * c:2 * c + 2, :] if t else bias[:, 2 * c:2 * c + 2, P:T],
                                       mixT[:, c, t * P:(t + 1) * P], gate=gates[:, t, at:at + 13:12],
                                       pre=(Vc[:, g2, j], pcT[:, t, g2]) if br == 0 else None,
                                       first=br == 0, last=br == 1))
            return us

        keys_of = lambda un: un.bias.shape[-1] if un.bias is not None else T
        A0, F0, N0 = 0, DEPTH * NATT, DEPTH * NATT + 8
        N_ATT = N0 + 32

        ADA_TURNS = [[24] + [2] * FC + [6] * 4, [0] + [2] * (FC - 4) + [0] * 8]
        EARLY = 3 * ADA
        FIRST = CONST["ones"][1]
        LATE = NG - ADA // RING

        ex = ctx.enter_context(nc.Block())

        def counter(eng, chain):
            n = {}

            def seq(ins, signal=chain, value=None):
                if value is None:
                    n[signal] = n.get(signal, 0) + 1
                    ins.then_inc(sem(signal), 1)
                    eng.wait_ge(sem(signal), n[signal])
                else:
                    ins.then_inc(signal, 1)
                    eng.wait_ge(signal, value)
            return seq

        @ex.sync
        def _(sp):
            sp.dma_start(crow[:, 0], io["c_rows"][:, 0]).then_inc(sem("c_in"), 16)
            sp.dma_start(params[:, :], io["params"]).then_inc(sem("params_in"), 16)
            ada_n = [0]

            def load_ada(k):
                for _ in range(min(k, EARLY - ada_n[0])):
                    n = ada_n[0]
                    if n >= 16 + ADA_RING:
                        sp.wait_ge(sem("ada_used"), n - ADA_RING + 1)
                    elif n >= 16:
                        sp.wait_ge(sem("ada_used"), 16)
                    arrived = sem(f"ada_first{n // 2}") if n < 16 else sem(f"ada_in{n % ADA_RING}")
                    sp.dma_start(ada_slot(n), io["ada"][n // ADA, n % ADA]).then_inc(arrived, 16)
                    ada_n[0] += 1

            def load_unit(src, u):
                if u >= RING:
                    sp.wait_ge(sem("units_used"), u - RING + 1)
                sp.dma_start(ring[:, u % RING].rearrange("p c n -> p (c n)"), src)\
                    .then_inc(sem(f"unit_in{u % RING}"), 16)

            load_ada(4)
            sp.dma_start(xT[:, :, :], io["xT_in"]).then_inc(sem("x_in"), 16)
            sp.dma_start(consts[:, 0:FIRST], io["consts"][:, 0:FIRST]).then_inc(sem("ones_in"), 16)
            load_ada(12)
            for l in range(DEPTH):
                turns = iter(ADA_TURNS[l][1:])
                for k in range(U_LAYER):
                    load_unit(io["stream_first"][l * U_LAYER + k], l * U_LAYER + k)
                    if l == 0 and k == 1:
                        sp.dma_start(consts[:, FIRST:], io["consts"][:, FIRST:]).then_inc(sem("consts_in"), 16)
                    if l == 0 and k == RING - 1:
                        sp.dma_start(mixc, io["mixer_consts"]).then_inc(sem("mixc_in"), 16)
                    if l == 0 and k == RING:
                        sp.dma_start(crow[:, 1], io["c_rows"][:, 1]).then_inc(sem("c2_in"), 16)
                    if k == U_IN + 5:
                        load_ada(ADA_TURNS[l][0])
                    at = k - (U_IN + U_OUT)
                    if at >= 6 and at % 2 == 0 and at < U_UP + 6:
                        load_ada(next(turns))
                    elif at >= U_UP + 10 and (at - U_UP) % 5 == 1:
                        load_ada(next(turns))
                for n in turns:
                    load_ada(n)

            def load_experts(p):
                late = io["ada"][3].rearrange("(g k) p n -> g k p n", k=RING)

                def groups_of(side, g0, g1, beside=False):
                    base = B_PEER[p] + side * NK
                    groups = io[("peer_u", "peer_v")[side]][p].rearrange("(g k) p n -> g k p n", k=RING)[g0:g1]
                    with sp.Fori(0, g1 - g0) as g:
                        for k in range(RING):
                            sp.wait_ge(sem("units_used"), g * RING + (base + g0 * RING + k - RING + 1))
                            sp.dma_start(ring[:, (base + k) % RING].rearrange("p (o c) n -> p o (c n)", o=1),
                                         groups[bass.ds(g, 1), k].rearrange("o p n -> p o n"))\
                                .then_inc(sem(f"unit_in{(base + k) % RING}"), 16)
                            if beside:
                                sp.wait_ge(sem("late_used"), g * RING + (k + 1))
                                sp.dma_start(extra[:, (k % 2) * D:(k % 2 + 1) * D].rearrange("p (o n) -> p o n", o=1),
                                             late[bass.ds(g, 1), k].rearrange("o p n -> p o n"))\
                                    .then_inc(sem(f"late_in{k % 2}"), 16)

                groups_of(0, 0, NG)
                if p:
                    groups_of(1, 0, NG)
                else:
                    groups_of(1, 0, LATE)
                    sp.wait_ge(sem("gates_used"), 2 * (T // 4) + 2)
                    sp.dma_start(late_row, io["c_rows"][:, 1]).then_inc(sem("late_row_in"), 16)
                    groups_of(1, LATE, NG, True)

            sp.dma_start(keysb[:, :], io["small"][:, 2 * P:4 * P]).then_inc(sem("keys_in"), 16)
            sp.dma_start(w2bd[:, :, :].rearrange("p a m -> p (a m)"), io["small"][:, 0:2 * P]).then_inc(sem("w2_in"), 16)
            for k in range(U_FOX + U_PQ):
                load_unit(io["stream_fox"][k], B_FOX + k)
            load_experts(0)
            for k in range(U_NSA + U_PQ):
                load_unit(io["stream_nsa"][k], B_NSA + k)
                if k == 6:
                    sp.wait_ge(sem("sums_y"), 1)
                    sp.dma_start(relc, io["rel"]).then_inc(sem("rel_in"), 16)
                    sp.dma_start(keysb[:, :], io["small"][:, 4 * P:6 * P]).then_inc(sem("keys_in"), 16)
            load_experts(1)
            for k in range(4):
                sp.wait_ge(sem("x_ready"), 4 * 7 + k + 1)
                sp.dma_start(out[:, 2 * k:2 * k + 2], xT[:, 2 * k:2 * k + 2]).then_inc(sem("out_written"), 16)
            sp.wait_ge(sem("out_written"), 4 * 16)

        @ex.tensor
        def _(pe):
            state = {"unit": -1, "pending": False}

            def mm(o, lhsT, rhs, start=True, stop=True, signal=None, **kw):
                ins = nc.tensor.matmul(o, lhsT, rhs, start=start, stop=stop, **kw)
                if signal is not None:
                    ins.then_inc(signal, 1)
                elif state["pending"]:
                    ins.then_inc(sem("units_used"), 1)
                    state["pending"] = False

            def next_unit():
                if state["unit"] >= 0:
                    state["pending"] = True
                state["unit"] += 1
                u = state["unit"]
                pe.wait_ge(sem(f"unit_in{u % RING}"), 16 * (u // RING + 1))
                return ring[:, u % RING]

            def open_job(*j):
                if job[j] >= 4:
                    pe.wait_ge(freed(*j)[0], freed(*j)[1] - 1)
                return bank_of(*j)

            def norm_stat(o):
                b = open_job("norm", o, 0)
                for c in range(DC):
                    if c % 2 == 0:
                        pe.wait_ge(sem("sq_ready"), 4 * o + c // 2 + 1)
                    mm(b[:, 0:T], ones, sq[:, c], c == 0, c == DC - 1, filled("norm", o, 0)[0] if c == DC - 1 else None)

            def tile_T(b, k, src, signal, first=False, h0=0, before={}):
                w = next_unit()
                for c in range(DC):
                    for sv in before.get(c, ()):
                        pe.wait_ge(*sv)
                    if first:
                        pe.wait_ge(sem("h_ready"), h0 + c + 1)
                    mm(b[:, k * T:(k + 1) * T], w[:, c], src[:, c], c == 0, c == DC - 1,
                       signal if c == DC - 1 else None)

            def tile_nat(b, k, signal):
                w = next_unit()
                for t in range(TT):
                    for c in range(DC):
                        last = t == TT - 1 and c == DC - 1
                        mm(b[:, k * T + t * P:k * T + (t + 1) * P], hT[:, c, t * P:(t + 1) * P], w[:, c],
                           c == 0, c == DC - 1, signal if last else None)

            def stat(name, l, n, ready, value, src=sq):
                pe.wait_ge(sem(ready), value)
                for i in range(n):
                    b = open_job(name, l, i)
                    mm(b[:, :], blk, src[:, 2 * i:2 * i + 2], signal=filled(name, l, i)[0])

            def level(l, k):
                g = l * 9 + k
                if g >= 2:
                    pe.wait_ge(sem("lev_freed"), g - 1)
                if l > 0 and k < 2:
                    pe.wait_ge(sem("pt_ready"), l * NATT)
                if k < 8:
                    pe.wait_ge(sem("keys_decayed"), l * 8 + k + 1)
                    pe.wait_ge(sem("queries_decayed"), l * 8 + k + 1)
                kk = ek[:, k % 2] if k < 8 else fk
                qq = eq[:, k % 2] if k < 8 else qB
                out_ = lev[g % 2][:, :].rearrange("p (h t q) -> p h t q", h=4, t=TT)
                for h in range(4):
                    for t in range(TT):
                        s = 1 - t if k == 0 else t
                        mm(out_[:, h, t], kk[:, h, s * P:(s + 1) * P], qq[:, h, t * P:(t + 1) * P],
                           signal=sem("lev_filled") if h == 3 and t == 1 else None)

            def attention(name, us, u0, beside={}):
                n, jobs = len(us), 0
                for step in range(n + 4):
                    if step in beside:
                        beside[step]()
                    if step < n:
                        u, un = u0 + step, us[step]
                        nk = keys_of(un)
                        if u >= 2:
                            pe.wait_ge(sem("scores_read"), u - 1)
                        for hh in range(2):
                            f = un.forget is not None
                            mm(S(u)[:, hh, 0:nk], un.q, un.kz[:, hh, 0:nk], stop=not f,
                               signal=sem("scores_filled") if hh and not f else None)
                            if f:
                                mm(S(u)[:, hh, 0:nk], sel8[:, un.forget[hh]], cum[:, 0:nk], start=False,
                                   signal=sem("scores_filled") if hh else None)
                    if 0 <= step - 3 < n:
                        u, un = u0 + step - 3, us[step - 3]
                        nc_ = keys_of(un) // P
                        pe.wait_ge(sem("diag_ready"), u + 1)
                        if u >= 2:
                            pe.wait_ge(sem("pt_ready"), u - 1)
                        for hh in range(2):
                            for c in range(nc_):
                                mm(PTb(u)[:, hh, c], pr[:, u % 4, hh, c * P:(c + 1) * P], dg[:, u % 4, hh],
                                   signal=sem("pt_filled") if hh and c == nc_ - 1 else None)
                    if 0 <= step - 4 < n:
                        u, un = u0 + step - 4, us[step - 4]
                        nc_ = keys_of(un) // P
                        pe.wait_ge(sem("pt_ready"), u + 1)
                        if un.first:
                            j = (*name, jobs)
                            jobs += 1
                            ob = open_job(*j)
                        if un.pre is not None:
                            mm(ob[:, 0:P], un.pre[0], un.pre[1], True, False)
                        for hh in range(2):
                            for c in range(nc_):
                                end = hh and c == nc_ - 1
                                mm(ob[:, 0:P], un.v[:, c, hh], pt[:, u % 2, hh, c],
                                   un.first and un.pre is None and hh + c == 0, bool(end) and un.last,
                                   None if not end else filled(*j)[0] if un.last else sem("pv_mid"))

            pe.wait_ge(sem("ones_in"), 16)
            for l in range(DEPTH):
                norm_stat(2 * l)
                if l == 0:
                    pe.wait_ge(sem("consts_in"), 16)
                for k in range(4):
                    b = open_job("in", l, k)
                    tile_T(b, 0, hT, None, first=k == 0, h0=16 * l)
                    tile_T(b, 1, hT, filled("in", l, k)[0])
                for k in range(4, 11):
                    b = open_job("in", l, k)
                    if k in (8, 9):
                        tile_nat(b, 0, None)
                        tile_nat(b, 1, filled("in", l, k)[0])
                    else:
                        tile_T(b, 0, hT, None)
                        tile_T(b, 1, hT, filled("in", l, k)[0])
                    if k >= 5:
                        level(l, k - 5)
                    if k == 6:
                        stat("statA", l, 2, "sqA", l + 1)
                    if k == 8:
                        stat("statC", l, 2, "sqC", l + 1)
                        pe.wait_ge(sem("normA"), l + 1)
                        for i in range(2):
                            b = open_job("rot", l, i)
                            mm(b[:, :], rot, rawA[:, 2 * i:2 * i + 2], signal=filled("rot", l, i)[0])
                for k in (6, 7, 8):
                    level(l, k)
                pe.wait_ge(sem("lev_freed"), 9 * (l + 1))
                pe.wait_ge(sem("qkA"), l + 1)
                pe.wait_ge(sem("qkC"), l + 1)
                pe.wait_ge(sem("vz_ready"), l + 1)
                def outputs_B():
                    pe.wait_ge(sem("levels_summed"), l + 1)
                    b = open_job("ob", l, 0)
                    for cc in range(2):
                        for t in range(TT):
                            for i, (h, s, at) in enumerate([(2 * cc + k, t if dd else 1 - t, ATd if dd else ATo)
                                                            for k in range(2) for dd in range(2)]):
                                mm(b[:, cc * T + t * P:cc * T + (t + 1) * P], vB[:, s, h], at[:, h, t], i == 0, i == 3,
                                   filled("ob", l, 0)[0] if cc and t and i == 3 else None)

                attention(("att", l), units_of(l), l * NATT, 
                          {2: outputs_B, 3: lambda: stat("statB", l, 1, "sqB", l + 1)})
                mixed = {c: [freed("att", l, 2 * (c if c < 3 else c - 2) + t) for t in range(TT)] for c in (0, 1, 2, 5, 6, 7)}
                mixed[3] = [(sem("mixB"), l + 1)]
                for k in range(4):
                    b = open_job("out", l, k)
                    tile_T(b, 0, mixT, None, before={} if k else mixed)
                    tile_T(b, 1, mixT, filled("out", l, k)[0])
                norm_stat(2 * l + 1)
                for k in range(FC):
                    b = open_job("up", l, k)
                    tile_T(b, 0, hT, None, first=k == 0, h0=16 * l + 8)
                    tile_T(b, 1, hT, filled("up", l, k)[0])
                w = None
                for k in range(4):
                    b = open_job("down", l, k)
                    for j in range(2):
                        for c in range(FC):
                            at = (2 * k + j) * FC + c
                            if at % 8 == 0:
                                w = next_unit()
                            if k == 0 and j == 0:
                                pe.wait_ge(sem("z_ready"), l * FC + c + 1)
                            mm(b[:, j * T:(j + 1) * T], w[:, at % 8], zT[:, c], c == 0, c == FC - 1,
                               filled("down", l, k)[0] if j and c == FC - 1 else None)

            def scores_of_keys(p):
                pe.wait_ge(sem("keys_in"), 16 * (p + 1))
                for k in range(4):
                    b = open_job("pq", p, k)
                    tile_T(b, 0, hT, None, first=k == 0, h0=8 * (5 + 2 * p))
                    tile_T(b, 1, hT, filled("pq", p, k)[0])
                pe.wait_ge(*freed("pq", p, 3))
                for k in range(8):
                    b = open_job("ps", p, k)
                    if k < 4:
                        pe.wait_ge(*freed("pq", p, k))
                    for j in range(2):
                        h = 2 * (k % 4) + j
                        mm(b[:, j * T:(j + 1) * T], qP[:, h, (k // 4) * P:(k // 4 + 1) * P], keysb[:, :],
                           signal=filled("ps", p, k)[0] if j else None)

            def experts(p):
                base = B_PEER[p]
                for k in range(4):
                    pe.wait_ge(*freed("ps", p, 4 + k))

                def gates_of(half, g, k):
                    q = (2 * p + half) * (T // 4) + k
                    g8 = (g - (NG // 2 if half == 0 else 0)) * RING
                    pe.wait_ge(sem("hot_rows"), g8 + (q + 1))
                    pe.wait_ge(sem("hot_cols"), g8 + (q + 1))
                    pe.wait_ge(sem("gates_used"), g8 + (q + 1))
                    for t in range(4):
                        ins = nc.tensor.matmul(gate_banks[half][k % 2][:, t * 256:t * 256 + PARTS * HALF],
                                               hot_r[:, k % 2, t], hot_c[:, k % 2, t].rearrange("p s x -> p (s x)"),
                                               start=True, stop=True)
                    ins.then_inc(sem("gates_filled"), 1)

                def inputs(g0, g1, gates):
                    with pe.Fori(g0, g1) as g:
                        for k in range(RING):
                            u = base + k
                            if gates:
                                gates_of(0, g, k)
                            pe.wait_ge(sem(f"unit_in{u % RING}"), g * 16 + 16 * (u // RING + 1))
                            if k % 2 == 0:
                                pe.wait_ge(sem("act_freed"), g * 4 + (p * 4 * NG + k // 2 + 1))
                            for c in range(DC):
                                ins = nc.tensor.matmul(banks[k // 2][:, (k % 2) * T:(k % 2 + 1) * T],
                                                       ring[:, u % RING, c], hT[:, c], start=c == 0, stop=c == DC - 1)
                                if c == 0:
                                    ins.then_inc(sem("units_used"), 1)
                                if c == DC - 1 and k % 2:
                                    ins.then_inc(sem("act_filled"), 1)

                inputs(0, NG // 2, False)
                for t in range(TT):
                    pe.wait_ge(sem("chosen"), p * TT + t + 1)
                    for o in range(3):
                        mm_(lev[t][:, o * P:(o + 1) * P], chosen[:, t, o].rearrange("p h r -> p (h r)"), ident,
                            sem("chosen_filled") if o == 2 else None)
                pe.wait_ge(sem("chosen_T"), (p + 1) * TT)
                inputs(NG // 2, NG, True)
                pe.wait_ge(sem("gates_used"), (2 * p + 1) * (T // 4) + 2)
                pe.wait_ge(sem("act_freed"), (p + 1) * 4 * NG + 4)
                for b in range(4):
                    nc.tensor.matmul(lev[b // 2][:, (b % 2) * 512:(b % 2 + 1) * 512], zero[:, :], consts[:, 0:512],
                                     start=True, stop=True)
                base2 = B_PEER[p] + NK

                def outputs(g0, g1, gates):
                    with pe.Fori(g0, g1) as g:
                        for k in range(RING):
                            u = base2 + k
                            if gates:
                                gates_of(1, g, k)
                            pe.wait_ge(sem(f"unit_in{u % RING}"), g * 16 + 16 * (u // RING + 1))
                            for c in range(DC):
                                ins = nc.tensor.matmul(lev[c // 4][:, (c % 4) * T:(c % 4 + 1) * T], ring[:, u % RING, c],
                                                       acts_g[:, bass.ds(g, 1), k], start=False, stop=True,
                                                       skip_group_check=True)
                                if c == 0:
                                    ins.then_inc(sem("units_used"), 1)

                outputs(0, NG // 2, True)
                pe.wait_ge(sem("gates_used"), (2 * p + 2) * (T // 4) + 2)
                outputs(NG // 2, NG, False)
                nc.tensor.matmul(lev[1][:, 512:1024], zero[:, :], consts[:, 0:512], start=False, stop=True,
                                 skip_group_check=True).then_inc(sem("sums_y"), 1)
                state["unit"] += 2 * NK
                state["pending"] = False

            def mm_(o, lhsT, rhs, signal=None):
                ins = nc.tensor.matmul(o, lhsT, rhs, start=True, stop=True)
                if signal is not None:
                    ins.then_inc(signal, 1)

            norm_stat(4)
            for k in FOX_ORDER:
                b = open_job("fin", k)
                if k in (10, 11):
                    tile_nat(b, 0, None)
                    tile_nat(b, 1, filled("fin", k)[0])
                elif k == 12:
                    tile_T(b, 0, hT, filled("fin", k)[0])
                else:
                    tile_T(b, 0, hT, None, first=k == FOX_ORDER[0], h0=32)
                    tile_T(b, 1, hT, filled("fin", k)[0])
                if k == 0:
                    pe.wait_ge(sem("sqF"), 1)
                    for i in range(4):
                        b = open_job("statF", i)
                        mm(b[:, :], blk, sq[:, 2 * i:2 * i + 2], signal=filled("statF", i)[0])
            pe.wait_ge(sem("qkF"), 1)
            pe.wait_ge(sem("vF_ready"), 1)
            attention(("attF",), fox_units(), F0)
            mixed = {4 + c: [freed("attF", 2 * c + t) for t in range(TT)] for c in range(4)}
            mixed[0] = [(sem("conv_out"), 1)]
            for k in range(4):
                b = open_job("foxout", k)
                tile_T(b, 0, mixT, None, before={} if k else mixed)
                tile_T(b, 1, mixT, filled("foxout", k)[0])
            norm_stat(5)
            scores_of_keys(0)
            experts(0)
            norm_stat(6)
            pe.wait_ge(sem("rel_in"), 16)
            relt = relc[:, 2 * T:2 * T + REL_W]
            for k in range(0, T, REL_SHIFTS):
                i = k % REL_COLS
                if i == 0:
                    b = open_job("relb", k // REL_COLS)
                s = P - k + T - 1
                end = i == REL_COLS - REL_SHIFTS or k + REL_SHIFTS >= T
                mm_(b[:, i * NSA_H:i * NSA_H + REL_W], relc[:, s:s + P], relt,
                    filled("relb", k // REL_COLS)[0] if end else None)
            def compress():
                pe.wait_ge(sem("pos_ready"), 1)
                for kv in range(2):
                    bm = open_job("cmp", kv)
                    pe.wait_ge(*freed("nin", kv))
                    for l in range(CMP_LEN):
                        if l % 8 == 0:
                            w = next_unit()
                        last = l == CMP_LEN - 1
                        mm(bm[:, 0:3 * N_CMP], w[:, l % 8],
                           kvc[:, kv, :, l:l + CMP_STRIDE * (N_CMP - 1) + 1:CMP_STRIDE], l == 0, last,
                           filled("cmp", kv)[0] if last else None)

            def compressed():
                pe.wait_ge(sem("w2_in"), 16)
                pe.wait_ge(sem("hid_ready"), 1)
                b = open_job("kc", 0)
                mm(b[:, 0:2 * N_CMP], w2bd[:, 0], hid[:, 0], signal=filled("kc", 0)[0])
                pe.wait_ge(sem("hidrep_ready"), 1)
                for c in range(2):
                    b = open_job("vc", c)
                    mm(b[:, 0:P], hidrep[:, c].rearrange("p h n -> p (h n)"), w2bd[:, 1], signal=filled("vc", c)[0])

            def stat_of_compressed():
                pe.wait_ge(sem("kcsq_ready"), 1)
                b = open_job("statK", 0)
                mm(b[:, 0:2 * N_CMP], blk, kcsq, signal=filled("statK", 0)[0])

            def stats(i0, i1, ready):
                pe.wait_ge(sem("sqN"), ready)
                for i in range(i0, i1):
                    b = open_job("statN", i)
                    mm(b[:, :], blk, sq[:, 2 * (i - i0):2 * (i - i0) + 2], signal=filled("statN", i)[0])

            def compressed_scores():
                pe.wait_ge(sem("kzc_ready"), 1)
                pe.wait_ge(sem("q_ready"), 1)
                for t in range(TT):
                    b = open_job("cs", t)
                    for c in range(8):
                        for hh in range(2):
                            i = 2 * c + hh
                            mm(b[:, i * 16:i * 16 + N_CMP], rawQ[:, c, t * P:(t + 1) * P], kzc[:, hh, c // 4],
                               signal=filled("cs", t)[0] if i == 15 else None)

            def compressed_probabilities():
                b = open_job("ct", 0)
                for t in range(TT):
                    pe.wait_ge(sem("pcs_ready"), t + 1)
                    for c in range(2):
                        mm(b[:, (2 * t + c) * P:(2 * t + c + 1) * P], pcs[:, t, 8 * c:8 * c + 8].rearrange("p h n -> p (h n)"),
                           ident, signal=filled("ct", 0)[0] if t and c else None)

            for k in NSA_ORDER:
                if k == "w1":
                    compress()
                    continue
                b = open_job("nin", k)
                if k in (8, 9):
                    tile_nat(b, 0, None)
                    tile_nat(b, 1, filled("nin", k)[0])
                elif k == 10:
                    tile_nat(b, 0, filled("nin", k)[0])
                else:
                    tile_T(b, 0, hT, None, first=k == 0, h0=48)
                    tile_T(b, 1, hT, filled("nin", k)[0])
                if k == 3:
                    compressed()
                elif k == 4:
                    stat_of_compressed()
                elif k == 6:
                    stats(0, 4, 1)
                elif k == 8:
                    stats(4, 6, 2)
                elif k == 10:
                    compressed_scores()
            compressed_probabilities()
            pe.wait_ge(*freed("ct", 0))
            pe.wait_ge(sem("kN_ready"), 1)
            pe.wait_ge(sem("vN_ready"), 1)
            pe.wait_ge(sem("Vc_ready"), 1)
            attention(("attN",), nsa_units(), N0)
            mixed = {c: [freed("attN", 2 * c + t) for t in range(TT)] for c in range(8)}
            for k in range(4):
                b = open_job("nsaout", k)
                tile_T(b, 0, mixT, None, before={} if k else mixed)
                tile_T(b, 1, mixT, filled("nsaout", k)[0])
            norm_stat(7)
            scores_of_keys(1)
            experts(1)

        @ex.scalar
        def _(act):
            seq = counter(act, "act_chain")
            A = nc.scalar.activation

            def wait(*sv):
                act.wait_ge(*sv)

            def norm(o):
                A(tiny[:, :], epsc[:, :], ACT.Sqrt).then_inc(sem("act_free"), 1)
                for k in range(4):
                    if o:
                        wait(sem("x_ready"), 4 * (o - 1) + k + 1)
                    A(sq[:, 2 * k:2 * k + 2], xT[:, 2 * k:2 * k + 2], ACT.Square).then_inc(sem("sq_ready"), 1)
                wait(*filled("norm", o, 0))
                A(std[:, :], bank_of("norm", o, 0)[:, 0:T], ACT.Sqrt, bias=epsc[:, :], scale=1.0 / D)\
                    .then_inc(freed("norm", o, 0)[0], 1)
                l, w = o // 2, o % 2
                for c in range(DC):
                    wait(sem("h_scaled"), 8 * o + c + 1)
                    A(hT[:, c], hT[:, c], ACT.Identity, bias=mod[:, l, 3 * w, c:c + 1]).then_inc(sem("h_ready"), 1)

            def drain(dst, *j):
                wait(*filled(*j))
                A(dst, bank_of(*j)[:, :], ACT.Copy).then_inc(freed(*j)[0], 1)

            def roots(dst, name, l, n):
                for i in range(n):
                    wait(*filled(name, l, i))
                    A(dst[:, 2 * i:2 * i + 2], bank_of(name, l, i)[:, :].rearrange("p (a t) -> p a t", a=2), ACT.Sqrt,
                      bias=epsc[:, :], scale=1.0 / HD).then_inc(freed(name, l, i)[0], 1)

            def decay(l, k):
                m = P >> k
                wait(sem("diffs"), l * 8 + k + 1)
                g = l * 9 + k
                if k >= 2:
                    wait(sem("lev_filled"), g - 1)
                d = dl[:, k % 2].rearrange("p h (n s m) -> p (h n) s m", s=2, m=m)
                for dst, j in ((eq, 0), (ek, 4)):
                    e = dst[:, k % 2].rearrange("p h (n s m) -> p (h n) s m", s=2, m=m)
                    for s in range(2):
                        c = j + 2 * s
                        A(e[:, :, s], d[:, :, s], ACT.Exp, bias=lvl[:, c + 1:c + 2], scale=lvl[:, c:c + 1])\
                            .then_inc(sem("decays"), 1)

            def attention(name, us, u0, beside={}):
                n, jobs = len(us), 0
                ends = []
                mids = 0
                for un in us:
                    if un.last:
                        ends.append(filled(*name, jobs))
                        jobs += 1
                    else:
                        mids += 1
                        ends.append((sem("pv_mid"), mids))
                for step in range(n + 3):
                    if step in beside:
                        beside[step]()
                    if step < n:
                        u, nk = u0 + step, keys_of(us[step])
                        wait(sem("max_ready"), u + 1)
                        if u >= 4:
                            wait(sem("pt_filled"), u - 3)
                        for hh in range(2):
                            A(pr[:, u % 4, hh, 0:nk], sc[:, u % 2, hh, 0:nk], ACT.Exp, bias=nmax[:, u % 4, hh:hh + 1],
                              accum_out=sums[:, u % 4, hh:hh + 1]).then_inc(sem("exp_ready"), 1)
                    if 0 <= step - 3 < n:
                        u = u0 + step - 3
                        nc_ = keys_of(us[step - 3]) // P
                        wait(sem("pt_filled"), u + 1)
                        if step - 3 >= 2:
                            wait(*ends[step - 5])
                        A(pt[:, u % 2, :, 0:nc_], PTb(u)[:, :, 0:nc_], ACT.Copy).then_inc(sem("pt_ready"), 1)

            def experts(p):
                for k in range(4):
                    wait(*filled("pq", p, k))
                    A(qP[:, 2 * k:2 * k + 2], bank_of("pq", p, k)[:, :].rearrange("p (a t) -> p a t", a=2), ACT.Copy)\
                        .then_inc(freed("pq", p, k)[0], 1)
                for k in range(8):
                    wait(*filled("ps", p, k))
                    A(sP[:, k // 4, 2 * (k % 4):2 * (k % 4) + 2], bank_of("ps", p, k)[:, :]
                      .rearrange("p (h s k) -> p h s k", h=2, s=2), ACT.Copy).then_inc(freed("ps", p, k)[0], 1)
                if p == 0:
                    act.sem_inc(sem("act_freed"), 4)

                def gelu(g0, g1):
                    with act.Fori(g0, g1) as g:
                        for k in range(4):
                            act.wait_ge(sem("act_filled"), g * 4 + (p * 4 * NG + k + 1))
                            A(acts_g[:, bass.ds(g, 1), 2 * k:2 * k + 2], banks[k][:, :]
                              .rearrange("p (o a t) -> p o a t", o=1, a=2), ACT.Gelu_apprx_tanh).then_inc(sem("act_freed"), 1)

                gelu(0, NG // 2 - 2)
                for t in range(TT):
                    wait(sem("gate_diff"), p * TT + t + 1)
                    A(chosen[:, t, 2], chosen[:, t, 2], ACT.Exp).then_inc(sem("gate_exp"), 1)
                gelu(NG // 2 - 2, NG // 2)
                for t in range(TT):
                    wait(sem("chosen_filled"), p * TT + t + 1)
                    A(chT[:, 0:3, t * P:(t + 1) * P], lev[t][:, 0:3 * P].rearrange("p (o q) -> p o q", o=3), ACT.Copy)\
                        .then_inc(sem("chosen_T"), 1)
                gelu(NG // 2, NG)
                if p == 0:
                    wait(sem("late_row_in"), 16)
                    A(late_row, late_row, ACT.Silu).then_inc(sem("c_silu"), 1)

            wait(sem("eps_set"), 1)
            wait(sem("c_in"), 16)
            seq(A(crow[:, 0], crow[:, 0], ACT.Silu), "c_silu")
            wait(sem("params_in"), 16)
            wait(sem("lb_max"), 1)
            A(lbt[:, 2:4], lbt[:, 2:4], ACT.Exp).then_inc(sem("lb_exp"), 1)
            wait(sem("x_in"), 16)
            for l in range(DEPTH):
                norm(2 * l)
                if l == 0:
                    wait(sem("c2_in"), 16)
                    A(crow[:, 1], crow[:, 1], ACT.Silu).then_inc(sem("c_silu"), 1)
                for k in range(2):
                    wait(sem("fx_ready"), 2 * l + k + 1)
                    A(fk[:, 2 * k:2 * k + 2], fk[:, 2 * k:2 * k + 2], ACT.Exp).then_inc(sem("f_exp"), 1)
                wait(sem("f_ready"), l + 1)
                A(C2, fk, ACT.Ln).then_inc(sem("logf"), 1)
                drain(qB[:, 0:2], "in", l, 2)
                drain(qB[:, 2:4], "in", l, 3)
                for k in range(4, 11):
                    if k < 6:
                        drain(rawA[:, 2 * (k - 4):2 * (k - 4) + 2], "in", l, k)
                    elif k < 8:
                        drain(rawC[:, 2 * (k - 6):2 * (k - 6) + 2], "in", l, k)
                    elif k == 8:
                        wait(*filled("in", l, k))
                        b = bank_of("in", l, k)
                        for i, v in enumerate((vA, vC)):
                            for hh in range(2):
                                src = b[:, i * T:(i + 1) * T].rearrange("p (t c) -> p t c", t=TT)[:, :, hh * HD:(hh + 1) * HD]
                                ins = A(v[:, :, hh, hh * HD:(hh + 1) * HD], src, ACT.Copy)
                                last = i == 1 and hh == 1
                                ins.then_inc(freed("in", l, k)[0] if last else sem("act_free"), 1)
                    elif k == 9:
                        wait(*filled("in", l, k))
                        b = bank_of("in", l, k)
                        for i in range(2):
                            for hh in range(2):
                                src = b[:, i * T:(i + 1) * T].rearrange("p (t c) -> p t c", t=TT)[:, :, hh * HD:(hh + 1) * HD]
                                ins = A(vB[:, :, 2 * i + hh, hh * HD:(hh + 1) * HD], src, ACT.Copy)
                                last = i == 1 and hh == 1
                                ins.then_inc(freed("in", l, k)[0] if last else sem("vz_ready") if i == 1 and hh == 0 else sem("act_free"), 1)
                    else:
                        wait(*filled("in", l, k))
                        A(gB, bank_of("in", l, k)[:, :].rearrange("p (a t) -> p a t", a=2), ACT.Copy)\
                            .then_inc(freed("in", l, k)[0], 1)
                    decay(l, k - 4)
                    if k == 5:
                        wait(*freed("in", l, 5))
                        A(sq[:, 0:4], rawA, ACT.Square).then_inc(sem("sqA"), 1)
                    if k == 6:
                        roots(rsq, "statA", l, 2)
                    if k == 7:
                        wait(*freed("in", l, 7))
                        A(sq[:, 0:4], rawC, ACT.Square).then_inc(sem("sqC"), 1)
                    if k == 8:
                        wait(sem("normA"), l + 1)
                        roots(rsq, "statC", l, 2)
                decay(l, 7)
                def outputs_B():
                    wait(*filled("ob", l, 0))
                    ob = bank_of("ob", l, 0)[:, :].rearrange("p (a t) -> p a t", a=2)
                    seq(A(oB, ob, ACT.Copy))
                    A(sq[:, 0:2], ob, ACT.Square).then_inc(sem("sqB"), 1)
                    wait(sem("sqB"), l + 1)
                    act.sem_inc(freed("ob", l, 0)[0], 1)

                def finish_B():
                    wait(*filled("statB", l, 0))
                    A(rsq[:, 0:2], bank_of("statB", l, 0)[:, :].rearrange("p (a t) -> p a t", a=2), ACT.Sqrt,
                      bias=epsc[:, :], scale=1.0 / HD).then_inc(freed("statB", l, 0)[0], 1)
                    A(gB, gB, ACT.Silu).then_inc(sem("gate_silu"), 1)

                attention(("att", l), units_of(l), l * NATT, {2: outputs_B, 4: finish_B})
                norm(2 * l + 1)
                for k in range(FC):
                    wait(*filled("up", l, k))
                    g = l * FC + k
                    if g >= 4:
                        wait(sem("z_ready"), g - 3)
                    for hh in range(2):
                        n = hh * FC + k
                        A(cv[:, g % 4, hh], bank_of("up", l, k)[:, hh * T:(hh + 1) * T], ACT.Identity,
                          bias=col("cb", l, n), scale=col("cw1", l, n)).then_inc(sem("conv_mid"), 1)
                    if k:
                        gp = g - 1
                        wait(*freed("up", l, k - 1))
                        if gp >= 2:
                            wait(sem("z_ready"), gp - 1)
                        A(sa[:, gp % 2], cv[:, gp % 4, 0], ACT.Silu).then_inc(sem("a_silu"), 1)
                gp = l * FC + FC - 1
                wait(*freed("up", l, FC - 1))
                wait(sem("z_ready"), gp - 1)
                A(sa[:, gp % 2], cv[:, gp % 4, 0], ACT.Silu).then_inc(sem("a_silu"), 1)

            def pair(b):
                return b[:, :].rearrange("p (a t) -> p a t", a=2)

            def values(v, b, i, signal):
                for hh in range(2):
                    src = b[:, i * T:(i + 1) * T].rearrange("p (t c) -> p t c", t=TT)[:, :, hh * HD:(hh + 1) * HD]
                    A(v[:, :, hh, hh * HD:(hh + 1) * HD], src, ACT.Copy).then_inc(signal if hh and signal else sem("act_free"), 1)

            norm(4)
            for k in FOX_ORDER:
                b = bank_of("fin", k)
                if k not in (4, 5, 12):
                    wait(*filled("fin", k))
                if k < 2:
                    A(cbT[:, 2 * k:2 * k + 2], pair(b), ACT.Copy).then_inc(freed("fin", k)[0], 1)
                elif k < 4:
                    A(prod[:, 2 * k - 4:2 * k - 2], pair(b), ACT.Copy).then_inc(freed("fin", k)[0], 1)
                elif 6 <= k < 10:
                    A(rawF[:, 2 * k - 12:2 * k - 10], pair(b), ACT.Copy).then_inc(freed("fin", k)[0], 1)
                    if k == 9:
                        wait(*freed("fin", 9))
                        A(sq, rawF, ACT.Square).then_inc(sem("sqF"), 1)
                elif k == 12:
                    wait(sem("f_abs"), 1)
                    A(lsig, lsig, ACT.Exp, scale=-1.0).then_inc(sem("f_e"), 1)
                    wait(sem("f_e1"), 1)
                    A(lsig, lsig, ACT.Ln).then_inc(sem("f_ln"), 1)
                elif k >= 10:
                    wait(sem("vF_zero"), 1)
                    values(vF[:, 2 * k - 20], b, 0, None)
                    values(vF[:, 2 * k - 19], b, 1, freed("fin", k)[0])
                if k == 0:
                    for i in range(4):
                        wait(*filled("statF", i))
                        A(rsF[:, 2 * i:2 * i + 2], pair(bank_of("statF", i)), ACT.Sqrt, bias=epsc[:, :], scale=1.0 / HD)\
                            .then_inc(freed("statF", i)[0], 1)
            attention(("attF",), fox_units(), F0)
            norm(5)
            experts(0)
            norm(6)
            for k in range(REL_JOBS):
                n = min(REL_COLS, T - k * REL_COLS)
                wait(*filled("relb", k))
                A(bias[:, :, REL_COLS * k:REL_COLS * k + n], bank_of("relb", k)[:, 0:n * NSA_H]
                  .rearrange("p (k h) -> p h k", h=NSA_H), ACT.Copy).then_inc(freed("relb", k)[0], 1)
            wait(*freed("relb", REL_JOBS - 1))
            wait(sem("nsa_zero"), 1)
            for t in range(TT):
                last = bias[:, :, P * (TT - 1 - t) + CMP_LEN - 1:T:CMP_STRIDE]
                A(cbias[:, t, :, 0:last.shape[-1]], last, ACT.Copy).then_inc(sem("cbias_ready"), 1)
            for k in NSA_ORDER:
                if k == "w1":
                    for kv in range(2):
                        wait(*filled("cmp", kv))
                        b = bank_of("cmp", kv)
                        seq(A(posb[:, kv:kv + 1], b[:, 2 * N_CMP:2 * N_CMP + 1], ACT.Copy))
                        seq(A(hid[:, kv], b[:, 0:2 * N_CMP].rearrange("p (c n) -> p c n", c=2),
                              ACT.Gelu_apprx_tanh, bias=posb[:, kv:kv + 1]), *freed("cmp", kv))
                        if kv == 0:
                            act.sem_inc(sem("hid_ready"), 1)
                    for c in range(2):
                        A(hidrep[:, c, :, 0:N_CMP], hid[:, 1, c].unsqueeze(1).broadcast_to([P, 8, N_CMP]), ACT.Copy)\
                            .then_inc(sem("hidrep_ready") if c else sem("act_free"), 1)
                    continue
                b = bank_of("nin", k)
                if k == 10:
                    wait(sem("g_pre"), 1)
                    A(gates, gates, ACT.Exp).then_inc(sem("g_exp"), 1)
                    for t in range(TT):
                        wait(sem("cs_diff"), t + 1)
                        A(pcs[:, t, :, 0:N_CMP], pcs[:, t, :, 0:N_CMP], ACT.Exp).then_inc(sem("cs_exp"), 1)
                    continue
                wait(*filled("nin", k))
                if k < 2:
                    A(kvc[:, k, 0:2], pair(b), ACT.Copy).then_inc(freed("nin", k)[0], 1)
                elif k < 6:
                    A(rawQ[:, 2 * k - 4:2 * k - 2], pair(b), ACT.Copy).then_inc(freed("nin", k)[0], 1)
                elif k < 8:
                    A(rawK[:, k - 6], pair(b), ACT.Copy).then_inc(freed("nin", k)[0], 1)
                else:
                    values(vN[:, k - 8, 0], b, 0, None)
                    values(vN[:, k - 8, 1], b, 1, freed("nin", k)[0])
                if k == 3:
                    wait(*filled("kc", 0))
                    kb = bank_of("kc", 0)[:, 0:2 * N_CMP].rearrange("p (c n) -> p c n", c=2)
                    A(kcn, kb, ACT.Copy).then_inc(sem("kcn_ready"), 1)
                    seq(A(kcsq, kb, ACT.Square), *freed("kc", 0))
                    act.sem_inc(sem("kcsq_ready"), 1)
                    for c in range(2):
                        wait(*filled("vc", c))
                        A(vrep[:, c], bank_of("vc", c)[:, 0:P], ACT.Copy).then_inc(freed("vc", c)[0], 1)
                elif k == 4:
                    wait(*filled("statK", 0))
                    A(kcrs, bank_of("statK", 0)[:, 0:2 * N_CMP].rearrange("p (c n) -> p c n", c=2), ACT.Sqrt, bias=epsc[:, :],
                      scale=1.0 / HD).then_inc(freed("statK", 0)[0], 1)
                elif k == 5:
                    wait(*freed("nin", 5))
                    A(sq, rawQ, ACT.Square).then_inc(sem("sqN"), 1)
                elif k == 6:
                    for i in range(4):
                        wait(*filled("statN", i))
                        A(rsQ[:, 2 * i:2 * i + 2], pair(bank_of("statN", i)), ACT.Sqrt, bias=epsc[:, :], scale=1.0 / HD)\
                            .then_inc(freed("statN", i)[0], 1)
                elif k == 7:
                    wait(*freed("nin", 7))
                    A(sq[:, 0:4], rawK.rearrange("p a c t -> p (a c) t"), ACT.Square).then_inc(sem("sqN"), 1)
                elif k == 8:
                    wait(sem("q_ready"), 1)
                    for i in (4, 5):
                        wait(*filled("statN", i))
                        A(rsQ[:, 2 * (i - 4):2 * (i - 4) + 2], pair(bank_of("statN", i)), ACT.Sqrt, bias=epsc[:, :],
                          scale=1.0 / HD).then_inc(freed("statN", i)[0], 1)
            wait(*filled("ct", 0))
            A(pcT, bank_of("ct", 0)[:, :].rearrange("p (t c q) -> p t c q", t=TT, c=2), ACT.Copy).then_inc(freed("ct", 0)[0], 1)
            attention(("attN",), nsa_units(), N0)
            norm(7)
            experts(1)

        @ex.gpsimd
        def _(pool):
            G = nc.gpsimd
            seq = counter(pool, "pool_chain")

            def attention(name, us, u0):
                for k in range(len(us)):
                    u = u0 + k
                    pool.wait_ge(sem("rinv_ready"), u + 1)
                    if u >= 4:
                        pool.wait_ge(sem("pt_filled"), u - 3)
                    for hh in range(2):
                        ins = G.tensor_scalar(dg[:, u % 4, hh], ident, rinv[:, u % 4, hh:hh + 1], None, ALU.mult)
                        ins.then_inc(sem("diag_ready") if hh else sem("diag_half"), 1)

            pool.wait_ge(sem("consts_in"), 16)
            for l in range(DEPTH):
                for k in range(8):
                    pool.wait_ge(sem("decays"), (l * 8 + k + 1) * 4)
                    pool.wait_ge(sem("keys_ready"), l + 1)
                    G.tensor_tensor(ek[:, k % 2], ek[:, k % 2], fk, ALU.mult).then_inc(sem("keys_decayed"), 1)
                attention(("att", l), units_of(l), l * NATT)
                for k in range(FC):
                    g = l * FC + k
                    pool.wait_ge(sem("a_silu"), g + 1)
                    G.tensor_tensor(zT[:, k], sa[:, g % 2], cv[:, g % 4, 1], ALU.mult).then_inc(sem("z_ready"), 1)
            attention(("attF",), fox_units(), F0)

            def hot_rows(p):
                pool.wait_ge(sem("chosen_T"), (p + 1) * TT)
                rows = chT[:, 0].rearrange("p (g k t) -> p g k t", k=2, t=4)
                for half in range(2):
                    q = (2 * p + half) * (T // 4)
                    with pool.Fori(0, T // 8) as g:
                        for k in range(2):
                            pool.wait_ge(sem("gates_used"), g * 2 + (q + k + 1))
                            pool.sem_inc(sem("pool_step"), 1)
                            G.tensor_copy(turn[:, k:k + 1], rows[:, bass.ds(g, 1), k]).then_inc(sem("turn"), 1)
                            pool.wait_ge(sem("turn"), g * 2 + (q + k + 1))
                            pool.sem_inc(sem("pool_step"), 1)
                            for t in range(4):
                                ins = G.tensor_scalar(hot_r[:, k, t], iota, turn[:, k, t:t + 1], None, ALU.is_equal)
                            ins.then_inc(sem("hot_rows"), 1)

            hot_rows(0)
            attention(("attN",), nsa_units(), N0)
            hot_rows(1)

        @ex.vector
        def _(dve):
            V = nc.vector
            seq = counter(dve, "dve_chain")

            def wait(*sv):
                dve.wait_ge(*sv)

            ada_n = [0]

            def do_ada(k):
                for _ in range(min(k, EARLY - ada_n[0])):
                    n = ada_n[0]
                    if n < 16:
                        wait(sem(f"ada_first{n // 2}"), 32)
                    else:
                        wait(sem(f"ada_in{n % ADA_RING}"), 16 * ((n - 16) // ADA_RING + 1))
                    if n == DEPTH * ADA:
                        wait(sem("c_silu"), 2)
                    l, ch = n // ADA, n % ADA
                    seq(V.tensor_tensor_reduce(out=junk, in0=ada_slot(n), in1=crow[:, l // DEPTH], scale=1.0,
                                               scalar=0.0, op0=ALU.mult, op1=ALU.add,
                                               accum_out=mod[:, l, ch // DC, ch % DC:ch % DC + 1]), "ada_used")
                    ada_n[0] += 1

            def late_ada():
                dve.sem_inc(sem("late_used"), 2)
                wait(sem("c_silu"), 3)
                for n in range(ADA):
                    wait(sem(f"late_in{n % 2}"), 16 * (n // 2 + 1))
                    seq(V.tensor_tensor_reduce(out=late_junk, in0=extra[:, (n % 2) * D:(n % 2 + 1) * D], in1=late_row,
                                               scale=1.0, scalar=0.0, op0=ALU.mult, op1=ALU.add,
                                               accum_out=mod[:, 3, n // DC, n % DC:n % DC + 1]), sem("late_used"), n + 3)
                mods(3, 0, 6)

            def mods(l, a, b):
                m = mod[:, l, a:b]
                seq(V.tensor_tensor(m, m, col("bada", l, a * DC, (b - a) * DC).rearrange("p (a c) -> p a c", c=DC), ALU.add))
                for w in range(2):
                    if a <= 3 * w + 1 < b:
                        g = col(f"ng{w + 1}", l, 0, DC) if l < DEPTH else col("png", None, ((l - DEPTH) * 2 + w) * DC, DC)
                        seq(V.tensor_scalar(gscale[:, l, w], mod[:, l, 3 * w + 1], 1.0, None, ALU.add))
                        seq(V.tensor_tensor(gscale[:, l, w], gscale[:, l, w], g, ALU.mult))

            def invert_std(o):
                wait(*freed("norm", o, 0))
                seq(V.reciprocal(rstd[:, :], std[:, :]))

            def norm(o):
                l, w = o // 2, o % 2
                if o:
                    invert_std(o)
                for c in range(DC):
                    V.scalar_tensor_tensor(out=hT[:, c], in0=xT[:, c], scalar=gscale[:, l, w, c:c + 1], in1=rstd[:, :],
                                           op0=ALU.mult, op1=ALU.mult).then_inc(sem("h_scaled"), 1)

            def residual(name, l, which, beside=(0, 0, 0, 0)):
                for k in range(4):
                    do_ada(beside[k])
                    wait(*filled(*name, k))
                    b = bank_of(*name, k)
                    for j in range(2):
                        n = 2 * k + j
                        ins = V.scalar_tensor_tensor(out=xT[:, n], in0=b[:, j * T:(j + 1) * T],
                                                     scalar=mod[:, l, which, n:n + 1], in1=xT[:, n],
                                                     op0=ALU.mult, op1=ALU.add)
                        if j == 1:
                            ins.then_inc(freed(*name, k)[0], 1)
                        else:
                            ins.then_inc(sem("x_half"), 1)
                    wait(*freed(*name, k))
                    dve.sem_inc(sem("x_ready"), 1)

            def attention(name, us, u0, projections=0, beside={}):
                n, jobs = len(us), 0
                for step in range(n + 5):
                    if step in beside:
                        beside[step]()
                    if step < n:
                        u = u0 + step
                        b, nk = us[step].bias, keys_of(us[step])
                        do_ada(projections)
                        wait(sem("scores_filled"), u + 1)
                        if u >= 2:
                            wait(sem("exp_ready"), 2 * (u - 1))
                        if b is None:
                            seq(V.tensor_scalar(sc[:, u % 2], S(u), SCALE, None, ALU.mult), "scores_read")
                        else:
                            seq(V.scalar_tensor_tensor(out=sc[:, u % 2, :, 0:nk], in0=S(u)[:, :, 0:nk], scalar=SCALE, in1=b,
                                                       op0=ALU.mult, op1=ALU.add), "scores_read")
                        seq(V.tensor_reduce(nmax[:, u % 4], sc[:, u % 2, :, 0:nk], AX.X, ALU.max))
                        seq(V.tensor_scalar(nmax[:, u % 4], nmax[:, u % 4], -1.0, None, ALU.mult), "max_ready")
                    if 0 <= step - 1 < n:
                        u = u0 + step - 1
                        wait(sem("exp_ready"), 2 * (u + 1))
                        if u >= 4:
                            wait(sem("diag_ready"), u - 3)
                        gate = us[step - 1].gate
                        if gate is None:
                            seq(V.reciprocal(rinv[:, u % 4], sums[:, u % 4]), "rinv_ready")
                        else:
                            seq(V.reciprocal(rinv[:, u % 4], sums[:, u % 4]))
                            seq(V.tensor_tensor(rinv[:, u % 4], rinv[:, u % 4], gate, ALU.mult), "rinv_ready")
                    if 0 <= step - 5 < n and us[step - 5].last:
                        j = (*name, jobs)
                        jobs += 1
                        wait(*filled(*j))
                        seq(V.tensor_copy(us[step - 5].out, bank_of(*j)[:, 0:P]), *freed(*j))

            V.memset(epsc[:, :], EPS).then_inc(sem("eps_set"), 1)
            wait(sem("params_in"), 16)
            lb0, lb1 = col("lb", 0, 0, 4), col("lb", 1, 0, 4)
            seq(V.tensor_tensor(lbt[:, 0], lb0, lb1, ALU.max))
            seq(V.tensor_tensor(lbt[:, 2], lb0, lbt[:, 0], ALU.subtract))
            seq(V.tensor_tensor(lbt[:, 3], lb1, lbt[:, 0], ALU.subtract), "lb_max")
            wait(sem("lb_exp"), 1)
            seq(V.tensor_tensor(lbt[:, 0], lbt[:, 2], lbt[:, 3], ALU.add))
            seq(V.reciprocal(lbt[:, 0], lbt[:, 0]))
            for k in (2, 3):
                seq(V.tensor_tensor(lbt[:, k], lbt[:, k], lbt[:, 0], ALU.mult))
            seq(V.tensor_tensor(lbt[:, 1], lbt[:, 2], lbt[:, 3], ALU.add))
            seq(V.tensor_tensor(lbt[:, 4], lbt[:, 2], lbt[:, 2], ALU.subtract))
            seq(V.tensor_tensor(lbt[:, 5], lbt[:, 1], lbt[:, 2], ALU.subtract))
            seq(V.tensor_scalar(lbt[:, 6:8], lbt[:, 4:6], -1.0, 1.0, ALU.mult, ALU.add))
            wait(sem("c_silu"), 1)
            do_ada(14)
            invert_std(0)
            do_ada(2)
            mods(0, 0, 2)
            for l in range(DEPTH):
                norm(2 * l)
                for z in (vA, vC, vB, Cx[:, :, 0:1]):
                    seq(V.memset(z, 0.0))
                if l == 0:
                    wait(sem("consts_in"), 16)
                for k in range(2):
                    wait(*filled("in", l, k))
                    b = bank_of("in", l, k)[:, :].rearrange("p (a t) -> p a t", a=2)
                    seq(V.tensor_scalar(fk[:, 2 * k:2 * k + 2], b, -80.0, -1.0, ALU.max, ALU.mult), freed("in", l, k)[0],
                        freed("in", l, k)[1])
                    dve.sem_inc(sem("fx_ready"), 1)
                wait(sem("f_exp"), 2 * (l + 1))
                seq(V.tensor_scalar(fk, fk, 1.0, None, ALU.add))
                seq(V.reciprocal(fk, fk))
                for h in range(4):
                    seq(V.tensor_scalar(fk[:, h], fk[:, h], lbt[:, 6 + l, h:h + 1], lbt[:, 4 + l, h:h + 1], ALU.mult, ALU.add))
                seq(V.tensor_scalar(fk, fk, F_MIN, None, ALU.max), "f_ready")
                wait(sem("logf"), l + 1)
                seq(V.tensor_scalar(fk, fk, -1.0, 1.0, ALU.mult, ALU.add), "keys_ready")
                seq(V.memset(rsq[:, 0], 0.0))
                for h in range(4):
                    seq(V.tensor_tensor_scan(Cx[:, h, 1:T + 1], C2[:, h], rsq[:, 0], 0.0, ALU.add, ALU.add))
                seq(V.tensor_copy(C2[0:HD], Cx[0:HD, :, 1:T + 1]))
                seq(V.tensor_copy(C2[HD:P], Cx[HD:P, :, 0:T]))
                wait(sem("mixc_in"), 16)

                def norm_A():
                    wait(*freed("statA", l, 1))
                    seq(V.reciprocal(rsq, rsq))
                    seq(V.scalar_tensor_tensor(out=rawA[:, 0:3], in0=rawA[:, 0:3], scalar=col("aq", l), in1=rsq[:, 0:3],
                                               op0=ALU.mult, op1=ALU.mult))
                    seq(V.scalar_tensor_tensor(out=rawA[:, 3], in0=rawA[:, 3], scalar=col("ak", l), in1=rsq[:, 3],
                                               op0=ALU.mult, op1=ALU.mult), "normA")

                def norm_C():
                    wait(*freed("statC", l, 1))
                    seq(V.reciprocal(rsq, rsq))
                    seq(V.scalar_tensor_tensor(out=rawC[:, 0:3], in0=rawC[:, 0:3], scalar=col("cq", l), in1=rsq[:, 0:3],
                                               op0=ALU.mult, op1=ALU.mult))
                    seq(V.scalar_tensor_tensor(out=kzC[:, 0], in0=rawC[:, 3], scalar=col("ck_lo", l), in1=rsq[:, 3],
                                               op0=ALU.mult, op1=ALU.mult))
                    seq(V.scalar_tensor_tensor(out=kzC[:, 1], in0=rawC[:, 3], scalar=col("ck_hi", l), in1=rsq[:, 3],
                                               op0=ALU.mult, op1=ALU.mult), "qkC")

                def rotary_A():
                    bc = lambda v: v.unsqueeze(1).broadcast_to([P, 2, T])
                    for i in range(2):
                        wait(*filled("rot", l, i))
                        x2, r2 = rawA[:, 2 * i:2 * i + 2], ropec[:, 2 * i:2 * i + 2]
                        seq(V.tensor_tensor(r2, bank_of("rot", l, i)[:, :].rearrange("p (a t) -> p a t", a=2), bc(sin), ALU.mult),
                            freed("rot", l, i)[0], freed("rot", l, i)[1])
                        seq(V.tensor_tensor(x2, x2, bc(cos), ALU.mult))
                        seq(V.tensor_tensor(x2, x2, r2, ALU.add))
                    seq(V.tensor_scalar(kzA[:, 0], rawA[:, 3], half[:, 0:1], None, ALU.mult))
                    seq(V.tensor_scalar(kzA[:, 1], rawA[:, 3], half[:, 1:2], None, ALU.mult), "qkA")

                beside = {3: norm_A, 5: norm_C, 6: rotary_A}
                for step in range(11):
                    if step < 8:
                        k, m = step, P >> step
                        d = dl[:, k % 2].rearrange("p h (n m) -> p h n m", m=2 * m)
                        c2 = C2.rearrange("p h (n m) -> p h n m", m=2 * m)
                        ref = Cx[:, :, m:T + 1:2 * m].unsqueeze(3).broadcast_to([P, 4, T // (2 * m), 2 * m])
                        seq(V.tensor_tensor(d, c2, ref, ALU.subtract), "diffs")
                    if 0 <= step - 1 < 8:
                        k = step - 1
                        if k == 0:
                            wait(*freed("in", l, 3))
                        wait(sem("decays"), (l * 8 + k + 1) * 4)
                        seq(V.tensor_tensor(eq[:, k % 2], eq[:, k % 2], qB, ALU.mult), "queries_decayed")
                    if step >= 2:
                        k = step - 2
                        g = l * 9 + k
                        wait(sem("lev_filled"), g + 1)
                        src = lev[g % 2][:, :].rearrange("p (h t q) -> p h t q", h=4, t=TT)
                        if k < 2:
                            seq(V.tensor_copy((ATo, ATd)[k], src), "lev_freed")
                        else:
                            mk = lmask[:, k - 2].unsqueeze(1).broadcast_to([P, 8, P])
                            seq(V.tensor_tensor(junk.rearrange("p (a q) -> p a q", a=8),
                                                src.rearrange("p h t q -> p (h t) q"), mk, ALU.mult), "lev_freed")
                            seq(V.tensor_tensor(ATd.rearrange("p h t q -> p (h t q)"), ATd.rearrange("p h t q -> p (h t q)"), junk, ALU.add),
                                "levels_summed" if k == 8 else "dve_chain")
                    if step in beside:
                        beside[step]()
                def norm_B():
                    wait(*freed("statB", l, 0))
                    seq(V.reciprocal(rsq[:, 0:2], rsq[:, 0:2]))
                    seq(V.scalar_tensor_tensor(out=oB, in0=oB, scalar=col("bo", l), in1=rsq[:, 0:2], op0=ALU.mult, op1=ALU.mult))
                    wait(sem("gate_silu"), l + 1)
                    seq(V.tensor_tensor(mixT[:, 3:5], oB, gB, ALU.mult), "mixB")

                attention(("att", l), units_of(l), l * NATT, ADA_TURNS[l][0] // 2 // NATT, {7: norm_B})
                if l == 0:
                    mods(0, 2, 3)
                residual(("out", l), l, 2, [ADA_TURNS[l][0] // 8] * 4)
                if l == 0:
                    mods(0, 3, 5)
                norm(2 * l + 1)
                for k in range(FC):
                    g = l * FC + k
                    wait(sem("conv_mid"), 2 * (g + 1))
                    b = bank_of("up", l, k)
                    for hh in range(2):
                        n = hh * FC + k
                        u = b[:, hh * T:(hh + 1) * T]
                        c = cv[:, g % 4, hh]
                        seq(V.scalar_tensor_tensor(out=c[:, 1:T], in0=u[:, 0:T - 1], scalar=col("cw0", l, n), in1=c[:, 1:T],
                                                   op0=ALU.mult, op1=ALU.add))
                        fin = V.scalar_tensor_tensor(out=c[:, 0:T - 1], in0=u[:, 1:T], scalar=col("cw2", l, n),
                                                     in1=c[:, 0:T - 1], op0=ALU.mult, op1=ALU.add)
                        if hh:
                            seq(fin, freed("up", l, k)[0], freed("up", l, k)[1])
                        else:
                            seq(fin)
                    do_ada(ADA_TURNS[l][1 + k])
                if l == 0:
                    mods(0, 5, 6)
                residual(("down", l), l, 5, ADA_TURNS[l][1 + FC:])
                if l == 0:
                    mods(1, 0, 6)
            mods(2, 0, 6)

            def k_norms(dst, raw, rs, lo, hi):
                for hh, g in enumerate((lo, hi)):
                    last = V.scalar_tensor_tensor(out=dst[:, :, hh], in0=raw, scalar=g, in1=rs, op0=ALU.mult, op1=ALU.mult)
                    if hh == 0:
                        seq(last)
                return last

            def choose(p):
                for t in range(TT):
                    wait(*freed("ps", p, 4 * t + 3))
                    for h in range(PH):
                        for s in range(2):
                            x, v, i = sP[:, t, h, s], sv[:, t, h, s], siu[:, t, h, s]
                            seq(V.max(v[:, 0:8], x))
                            seq(V.max_index(i[:, 0:8], v[:, 0:8], x))
                            seq(V.match_replace(wk[:, 0:NK], v[:, 0:8], x, -3e38))
                            seq(V.max(v[:, 8:16], wk[:, 0:NK]))
                            seq(V.max_index(i[:, 8:16], v[:, 8:16], wk[:, 0:NK]))
                    flat = lambda a: a.rearrange("p h s r -> p (h s r)")
                    seq(V.tensor_copy(flat(sif[:, t]), flat(siu[:, t])))
                    seq(V.tensor_tensor(cand, sv[:, t, :, 0].unsqueeze(3).broadcast_to([P, PH, TOPK, TOPK]),
                                        sv[:, t, :, 1].unsqueeze(2).broadcast_to([P, PH, TOPK, TOPK]), ALU.add))
                    for h in range(PH):
                        x, v, i = cand[:, h].rearrange("p a b -> p (a b)"), cvv[:, t, h], ciu[:, t, h]
                        seq(V.max(v[:, 0:8], x))
                        seq(V.max_index(i[:, 0:8], v[:, 0:8], x))
                        seq(V.match_replace(wk, v[:, 0:8], x, -3e38))
                        seq(V.max(v[:, 8:16], wk))
                        seq(V.max_index(i[:, 8:16], v[:, 8:16], wk))
                    g = chosen[:, t, 2]
                    seq(V.tensor_tensor(g, cvv[:, t], cvv[:, t, :, 0:1].broadcast_to([P, PH, TOPK]), ALU.subtract), "gate_diff")
                    seq(V.tensor_scalar(cau[:, t, 0], ciu[:, t], 4, None, ALU.logical_shift_right))
                    seq(V.tensor_scalar(cau[:, t, 1], ciu[:, t], 15, None, ALU.bitwise_and))
                    seq(V.tensor_copy(caf[:, t], cau[:, t]))
                    for s in range(2):
                        at = caf[:, t, s].rearrange("p h r -> p (h r)").unsqueeze(2).broadcast_to([P, PH * TOPK, TOPK])
                        io16 = iota[:, 0:TOPK].unsqueeze(1).broadcast_to([P, PH * TOPK, TOPK])
                        seq(V.tensor_tensor(hit, io16, at, ALU.is_equal))
                        h4 = hit.rearrange("p (h r) a -> p h r a", h=PH)
                        seq(V.tensor_tensor(h4, h4, sif[:, t, :, s].unsqueeze(2).broadcast_to([P, PH, TOPK, TOPK]), ALU.mult))
                        seq(V.tensor_reduce(chosen[:, t, s].rearrange("p h r -> p (h r)"), hit, AX.X, ALU.add))
                for t in range(TT):
                    g = chosen[:, t, 2]
                    wait(sem("gate_exp"), p * TT + t + 1)
                    seq(V.tensor_reduce(gsum[:, t], g, AX.X, ALU.add))
                    seq(V.reciprocal(gsum[:, t], gsum[:, t]))
                    seq(V.tensor_tensor(g, g, gsum[:, t].unsqueeze(2).broadcast_to([P, PH, TOPK]), ALU.mult), "chosen")

            def experts(p):
                choose(p)
                wait(sem("chosen_T"), (p + 1) * TT)
                seq(V.tensor_copy(part_b, chT[:, 2]))
                seq(V.tensor_copy(chT[:, 4], part_b))
                seq(V.tensor_tensor(chT[:, 3], chT[:, 2], chT[:, 4], ALU.subtract))
                seq(V.tensor_copy(chT[:, 2], part_b))
                seq(V.tensor_copy(part_b, chT[:, 3]))
                seq(V.tensor_copy(chT[:, 4], part_b))
                seq(V.tensor_tensor(chT[:, 3], chT[:, 3], chT[:, 4], ALU.subtract))
                if p == 0:
                    dve.sem_inc(sem("gates_used"), 2)

                odd = chT[:, :, 0:T - 8].rearrange("p o (g k t) -> p o g k t", k=2, t=4)
                even = chT[:, :, 8:T].rearrange("p o (g k t) -> p o g k t", k=2, t=4)
                for half in range(2):
                    q = (2 * p + half) * (T // 4)
                    by_token = arena[:, half * HALF * T:(half + 1) * HALF * T]\
                        .rearrange("p (j g k t) -> p g k t j", j=HALF, k=2, t=4)

                    def columns_of(k, of):
                        for t in range(4):
                            ins = V.scalar_tensor_tensor(
                                out=hot_c[:, k, t], in0=iota[:, half * HALF:(half + 1) * HALF].unsqueeze(1).broadcast_to([P, PARTS, HALF]),
                                scalar=of(1, 2, t), in1=of(2, 5, t).broadcast_to([P, PARTS, HALF]),
                                op0=ALU.is_equal, op1=ALU.mult)
                        ins.then_inc(sem("hot_cols"), 1)

                    def weigh(k, dst, turn_no):
                        dve.wait_ge(sem("gates_used"), turn_no + 1)
                        dve.wait_ge(sem("gates_filled"), turn_no)
                        V.tensor_reduce(gate_of, gate_banks[half][k].rearrange("p (t x) -> p t x", t=4)[:, :, 0:PARTS * HALF]
                                        .rearrange("p t (s j) -> p t j s", s=PARTS), AX.X, ALU.add).then_inc(sem("gates_summed"), 1)
                        dve.wait_ge(sem("gates_summed"), turn_no)
                        V.tensor_tensor(dst, gate_of.unsqueeze(1), dst, ALU.mult).then_inc(sem("gates_used"), 1)

                    wait(sem("act_freed"), 4 + p * 4 * NG + (half + 1) * 2 * NG)
                    columns_of(0, lambda a, b, t: chT[:, a:b, t:t + 1] if b - a > 1 else chT[:, a, t:t + 1])
                    with dve.Fori(0, T // 8 - 1) as g:
                        dve.wait_ge(sem("gates_used"), g * 2 + (q + 2))
                        columns_of(1, lambda a, b, t: odd[:, a:b, bass.ds(g, 1), 1, t] if b - a > 1 else odd[:, a, bass.ds(g, 1), 1, t])
                        weigh(0, by_token[:, bass.ds(g, 1), 0], g * 2 + (q + 1))
                        dve.wait_ge(sem("gates_used"), g * 2 + (q + 3))
                        columns_of(0, lambda a, b, t: even[:, a:b, bass.ds(g, 1), 0, t] if b - a > 1 else even[:, a, bass.ds(g, 1), 0, t])
                        weigh(1, by_token[:, bass.ds(g, 1), 1], g * 2 + (q + 2))
                    columns_of(1, lambda a, b, t: chT[:, a:b, T - 4 + t:T - 3 + t] if b - a > 1 else chT[:, a, T - 4 + t:T - 3 + t])
                    weigh(0, by_token[:, T // 8 - 1:T // 8, 0], q + T // 4 - 1)
                    weigh(1, by_token[:, T // 8 - 1:T // 8, 1], q + T // 4)
                if p == 0:
                    late_ada()
                wait(sem("sums_y"), p + 1)
                for c in range(DC):
                    V.scalar_tensor_tensor(out=xT[:, c], in0=lev[c // 4][:, (c % 4) * T:(c % 4 + 1) * T],
                                           scalar=mod[:, 2 + p, 5, c:c + 1], in1=xT[:, c], op0=ALU.mult, op1=ALU.add)\
                        .then_inc(sem("x_ready" if c % 2 else "x_half"), 1)
                dve.wait_ge(sem("x_ready"), 4 * (6 + 2 * p))

            norm(4)
            seq(V.memset(fzero, 0.0))
            seq(V.memset(cum, 0.0))
            seq(V.memset(zero[:, :], 0.0))
            seq(V.memset(vF, 0.0), "vF_zero")
            pair = lambda b: b[:, :].rearrange("p (a t) -> p a t", a=2)
            wait(*filled("fin", 12))
            R8 = slice(0, 8)
            seq(V.tensor_scalar(cum[R8], bank_of("fin", 12)[R8, 0:T], col("bf")[R8], None, ALU.add), *freed("fin", 12))
            seq(V.scalar_tensor_tensor(out=lsig, in0=cum, scalar=-1.0, in1=cum, op0=ALU.mult, op1=ALU.max), "f_abs")
            wait(sem("f_e"), 1)
            seq(V.tensor_scalar(lsig, lsig, 1.0, None, ALU.add), "f_e1")
            wait(sem("f_ln"), 1)
            seq(V.tensor_scalar(cum[R8], cum[R8], 0.0, None, ALU.min))
            seq(V.tensor_tensor(lsig[R8], cum[R8], lsig[R8], ALU.subtract))
            seq(V.tensor_tensor_scan(cum[R8], lsig[R8], fzero[R8], 0.0, ALU.add, ALU.add))
            wait(*freed("statF", 3))
            seq(V.reciprocal(rsF, rsF))
            seq(V.scalar_tensor_tensor(out=rawF[:, 0:4], in0=rawF[:, 0:4], scalar=col("fq"), in1=rsF[:, 0:4], op0=ALU.mult, op1=ALU.mult))
            seq(k_norms(kzF, rawF[:, 4:8], rsF[:, 4:8], col("fk_lo"), col("fk_hi")), "qkF")
            for i in range(2):
                wait(*freed("fin", 2 + i))
                wait(*filled("fin", 4 + i))
                x = prod[:, 2 * i:2 * i + 2]
                seq(V.tensor_tensor(x, x, pair(bank_of("fin", 4 + i)), ALU.mult), *freed("fin", 4 + i))
            fcw = lambda j, c: col("fcw", None, 4 * j + c)
            for c in range(4):
                x, y = prod[:, c], cmid[:, c]
                seq(V.tensor_scalar(y, x, fcw(2, c), None, ALU.mult))
                seq(V.scalar_tensor_tensor(out=y[:, 1:T], in0=x[:, 0:T - 1], scalar=fcw(1, c), in1=y[:, 1:T], op0=ALU.mult, op1=ALU.add))
                seq(V.scalar_tensor_tensor(out=y[:, 2:T], in0=x[:, 0:T - 2], scalar=fcw(0, c), in1=y[:, 2:T], op0=ALU.mult, op1=ALU.add))
            wait(*freed("fin", 1))
            seq(V.tensor_tensor(mixT[:, 0:4], cmid, cbT, ALU.mult), "conv_out")
            wait(*freed("fin", 11))
            dve.sem_inc(sem("vF_ready"), 1)
            attention(("attF",), fox_units(), F0)
            residual(("foxout",), 2, 2)
            norm(5)
            experts(0)
            seq(V.memset(vN, 0.0))
            seq(V.memset(kvc[:, :, 2], 0.0))
            seq(V.memset(cbias, NEG))
            seq(V.memset(pcs, 0.0))
            seq(V.memset(hidrep, 0.0), "nsa_zero")
            norm(6)
            for kv in range(2):
                seq(V.tensor_copy(kvc[:, kv, 2, 0:CMP_LEN], col("pos", None, kv * CMP_LEN, CMP_LEN)))
            dve.sem_inc(sem("pos_ready"), 1)
            for c in range(2):
                wait(*freed("vc", c))
                for i in range(8):
                    hh = i % 2
                    seq(V.tensor_scalar(Vc[:, c, i // 2, hh * HD:(hh + 1) * HD], vrep[:, c, hh * HD:(hh + 1) * HD],
                                        const("vmask")[:, i:i + 1], None, ALU.mult))
            dve.sem_inc(sem("Vc_ready"), 1)
            wait(*freed("statK", 0))
            seq(V.reciprocal(kcrs, kcrs))
            for hh, g in enumerate(("nkc_lo", "nkc_hi")):
                seq(V.scalar_tensor_tensor(out=kzc[:, hh], in0=kcn, scalar=col(g), in1=kcrs, op0=ALU.mult, op1=ALU.mult))
            dve.sem_inc(sem("kzc_ready"), 1)
            wait(*freed("statN", 3))
            seq(V.reciprocal(rsQ, rsQ))
            seq(V.scalar_tensor_tensor(out=rawQ, in0=rawQ, scalar=col("nq"), in1=rsQ, op0=ALU.mult, op1=ALU.mult), "q_ready")
            wait(*freed("statN", 5))
            seq(V.reciprocal(rsQ[:, 0:4], rsQ[:, 0:4]))
            seq(k_norms(kzN[:, 0], rawK[:, 0], rsQ[:, 0:2], col("nks_lo"), col("nks_hi")))
            seq(k_norms(kzN[:, 1], rawK[:, 1], rsQ[:, 2:4], col("nkw_lo"), col("nkw_hi")), "kN_ready")
            wait(*filled("nin", 10))
            for t in range(TT):
                seq(V.tensor_tensor(gates[:, t], bank_of("nin", 10)[:, t * P:t * P + 48], col("bgate", None, 0, 48), ALU.add),
                    *(freed("nin", 10) if t else ()))
            seq(V.tensor_scalar(gates, gates, -80.0, -1.0, ALU.max, ALU.mult), "g_pre")
            wait(sem("g_exp"), 1)
            seq(V.tensor_scalar(gates, gates, 1.0, None, ALU.add))
            seq(V.reciprocal(gates, gates))
            wait(sem("cbias_ready"), TT)
            pc = lambda t: pcs[:, t, :, 0:N_CMP]
            hb = lambda a, t: a[:, t].unsqueeze(2).broadcast_to([P, NSA_H, N_CMP])
            for t in range(TT):
                wait(*filled("cs", t))
                sco = bank_of("cs", t)[:, 0:T].rearrange("p (h n) -> p h n", h=NSA_H)[:, :, 0:N_CMP]
                seq(V.scalar_tensor_tensor(out=pc(t), in0=sco, scalar=SCALE, in1=cbias[:, t, :, 0:N_CMP],
                                           op0=ALU.mult, op1=ALU.add), *freed("cs", t))
                seq(V.tensor_reduce(cmx[:, t], pc(t), AX.X, ALU.max))
                seq(V.tensor_tensor(pc(t), pc(t), hb(cmx, t), ALU.subtract), "cs_diff")
            for t in range(TT):
                wait(sem("cs_exp"), t + 1)
                seq(V.tensor_reduce(csm[:, t], pc(t), AX.X, ALU.add))
                seq(V.reciprocal(csm[:, t], csm[:, t]))
                gt = gates[:, t].rearrange("p (g h j b) -> p g j h b", g=2, h=2, b=3)[:, :, :, :, 0]
                s4 = csm[:, t].rearrange("p (g j h) -> p g j h", g=2, h=2)
                seq(V.tensor_tensor(s4, s4, gt, ALU.mult))
                seq(V.tensor_tensor(pc(t), pc(t), hb(csm, t), ALU.mult))
                seq(V.tensor_tensor(pc(t), pc(t), cmask[:, t].unsqueeze(1).broadcast_to([P, NSA_H, N_CMP]), ALU.mult), "pcs_ready")
            wait(*freed("nin", 9))
            dve.sem_inc(sem("vN_ready"), 1)
            attention(("attN",), nsa_units(), N0)
            residual(("nsaout",), 3, 2)
            norm(7)
            experts(1)



INPUTS = ("xT_in", "params", "consts", "mixer_consts", "rel", "c_rows", "ada", "small",
          "stream_first", "stream_fox", "stream_nsa", "peer_u", "peer_v")


def kernel(**inputs):
    from concourse import bacc
    from concourse.bass_utils import run_bass_kernel_spmd

    arrays = lay_out(inputs)
    nc = bacc.Bacc("TRN2", target_bir_lowering=False, num_devices=1)
    io = {n: nc.dram_tensor("in_" + n, arrays[n].shape, F32, kind="ExternalInput").ap() for n in INPUTS}
    out = nc.dram_tensor("out", (P, DC, T), F32, kind="ExternalOutput").ap()
    build(nc, io, out)
    r = run_bass_kernel_spmd(nc, [{"in_" + n: np.ascontiguousarray(arrays[n]) for n in INPUTS}], core_ids=[0])
    return np.ascontiguousarray(r.results[0]["out"].transpose(2, 1, 0)).reshape(1, T, D)
```
